# Optimizing a Trainium2 kernel written in Bass

```python
import math
import functools
import jax
import jax.numpy as jnp
from jax import lax
import numpy as np

D_MODEL = 2048
BATCH = 1
SEQ = 256
DEPTH = 1
DEC_BATCH = 8
DEC_SEQ = 1
PAST_LEN = 2048
PAGE_SIZE = 128

HEAD_DIM = 128
N_HEADS = D_MODEL // HEAD_DIM
N_KV_HEADS = 4
GROUP = N_HEADS // N_KV_HEADS
ROPE_DIM = HEAD_DIM // 4
IDX_HEADS = 16
IDX_DIM = 64
IDX_ROPE_DIM = IDX_DIM // 4
TOPK_MAX = 256
ROPE_THETA = 500000.0
Q_BLOCK = 128
GDN_DK = 128
GDN_DV = 128
GDN_HEADS = D_MODEL // GDN_DV
CONV_W = 4
CONV_DIM = 2 * GDN_HEADS * GDN_DK + GDN_HEADS * GDN_DV
CHUNK = 64
D_FF = 5632
LN_EPS = 1e-5
NORM_EPS = 1e-6
DN_ALPHA = (2 * DEPTH) ** 0.25
DN_BETA = (8 * DEPTH) ** -0.25

IN_SPLITS = (
    ('q_a', N_HEADS * HEAD_DIM), ('k_a', N_KV_HEADS * HEAD_DIM), ('v_a', N_KV_HEADS * HEAD_DIM),
    ('q_idx', IDX_HEADS * IDX_DIM), ('k_idx', IDX_DIM), ('w_idx', IDX_HEADS),
    ('qkv_b', CONV_DIM), ('a_b', GDN_HEADS), ('beta_b', GDN_HEADS), ('z_b', GDN_HEADS * GDN_DV),
    ('gate_a', D_MODEL), ('gate_b', D_MODEL),
)
IN_COLS = sum(n for _, n in IN_SPLITS)

kernel_name = 'hybrid_dsa_gdn_macaron_step'

def _layer_norm(x, g, b):
    xf = x.astype(jnp.float32)
    mu = jnp.mean(xf, axis=-1, keepdims=True)
    var = jnp.mean(jnp.square(xf - mu), axis=-1, keepdims=True)
    return ((xf - mu) * lax.rsqrt(var + LN_EPS) * g.astype(jnp.float32) + b.astype(jnp.float32)).astype(x.dtype)

def _rms_norm(x, g):
    xf = x.astype(jnp.float32)
    return xf * lax.rsqrt(jnp.mean(jnp.square(xf), axis=-1, keepdims=True) + NORM_EPS) * g.astype(jnp.float32)

def _l2norm(x):
    xf = x.astype(jnp.float32)
    return xf * lax.rsqrt(jnp.sum(jnp.square(xf), axis=-1, keepdims=True) + NORM_EPS)

def _swiglu(x, wg, wu, wd):
    return (jax.nn.silu(x @ wg) * (x @ wu)) @ wd

def _split_columns(u):
    offs = np.cumsum([n for _, n in IN_SPLITS])[:-1].tolist()
    return dict(zip([nm for nm, _ in IN_SPLITS], jnp.split(u, offs, axis=-1)))

def _rope(x, pos, rot_dim):
    half = rot_dim // 2
    inv = ROPE_THETA ** (-jnp.arange(half, dtype=jnp.float32) / half)
    ang = pos.astype(jnp.float32)[:, None] * inv[None, :]
    cos = jnp.cos(ang)[:, None, :]
    sin = jnp.sin(ang)[:, None, :]
    xf = x.astype(jnp.float32)
    x1, x2, rest = xf[..., :half], xf[..., half:rot_dim], xf[..., rot_dim:]
    out = jnp.concatenate([x1 * cos - x2 * sin, x2 * cos + x1 * sin, rest], axis=-1)
    return out.astype(x.dtype)

def _causal_conv(x, buf, w):
    T = x.shape[1]
    xp = jnp.concatenate([buf.astype(x.dtype), x], axis=1)
    y = w[0] * xp[:, 0:T]
    for j in range(1, CONV_W):
        y = y + w[j] * xp[:, j:j + T]
    return jax.nn.silu(y), xp[:, xp.shape[1] - (CONV_W - 1):]

def _gated_delta(q, k, v, g, beta, s0):
    B, T, H, dk = q.shape
    dv = v.shape[-1]
    pad = (-T) % CHUNK
    def padt(a):
        return jnp.pad(a, [(0, 0), (0, pad)] + [(0, 0)] * (a.ndim - 2))
    nc = (T + pad) // CHUNK
    def chunks(a):
        a = padt(a.astype(jnp.float32))
        return jnp.moveaxis(a.reshape((B, nc, CHUNK, H) + a.shape[3:]), 3, 1)
    q, k, v, g, beta = chunks(q), chunks(k), chunks(v), chunks(g), chunks(beta)
    G = jnp.cumsum(g, axis=-1)
    tri_incl = jnp.tril(jnp.ones((CHUNK, CHUNK), dtype=bool))
    tri_strict = jnp.tril(jnp.ones((CHUNK, CHUNK), dtype=bool), -1)
    diff = G[..., :, None] - G[..., None, :]
    decay_incl = jnp.where(tri_incl, jnp.exp(jnp.where(tri_incl, diff, 0.0)), 0.0)
    decay_strict = jnp.where(tri_strict, decay_incl, 0.0)
    kb = k * beta[..., None]
    a_mat = jnp.einsum('bhnid,bhnjd->bhnij', kb, k) * decay_strict + jnp.eye(CHUNK, dtype=jnp.float32)
    u = lax.linalg.triangular_solve(a_mat, v * beta[..., None], left_side=True, lower=True, unit_diagonal=True)
    w = lax.linalg.triangular_solve(a_mat, kb * jnp.exp(G)[..., None], left_side=True, lower=True, unit_diagonal=True)
    qk = jnp.einsum('bhnid,bhnjd->bhnij', q, k) * decay_incl
    xs = tuple(jnp.moveaxis(a, 2, 0) for a in (q, k, u, w, G, qk))

    def step(S, c):
        qc, kc, uc, wc, Gc, qkc = c
        v_new = uc - jnp.einsum('bhcd,bhde->bhce', wc, S)
        o = jnp.einsum('bhcd,bhde->bhce', qc * jnp.exp(Gc)[..., None], S) + jnp.einsum('bhij,bhje->bhie', qkc, v_new)
        g_last = Gc[..., -1:]
        S = S * jnp.exp(g_last)[..., None] + jnp.einsum('bhcd,bhce->bhde', kc * jnp.exp(g_last - Gc)[..., None], v_new)
        return S, o

    S, o = lax.scan(step, s0.astype(jnp.float32), xs)
    o = jnp.moveaxis(jnp.moveaxis(o, 0, 2), 1, 3).reshape(B, nc * CHUNK, H, dv)[:, :T]
    return o, S

def _indexer_select(qi, wi, ki, qpos, ktop):
    L = ki.shape[1]
    s = jax.nn.relu(jnp.einsum('bthd,bld->bthl', qi, ki))
    score = jnp.einsum('bth,bthl->btl', wi, s).astype(jnp.float32)
    allowed = jnp.arange(L, dtype=jnp.int32)[None, :] <= qpos[:, None]
    score = jnp.where(allowed[None], score, -jnp.inf)
    _, sel = lax.top_k(score, ktop)
    valid = sel <= qpos[None, :, None]
    return sel, valid

def _gather_rows(a, sel):
    return a[jnp.arange(a.shape[0])[:, None, None], sel]

def _sparse_attend(q, ks, vs, valid):
    s = jnp.einsum('btngd,btknd->btngk', q, ks).astype(jnp.float32) * (HEAD_DIM ** -0.5)
    s = jnp.where(valid[:, :, None, None, :], s, -jnp.inf)
    p = jax.nn.softmax(s, axis=-1)
    return jnp.einsum('btngk,btknd->btngd', p.astype(vs.dtype), vs)

def _dsa_prompt(q, k, v, qi, ki, wi):
    B, S = q.shape[:2]
    ktop = min(TOPK_MAX, S // 4)
    nb = S // Q_BLOCK
    def blocks(a):
        return jnp.moveaxis(a.reshape((B, nb, Q_BLOCK) + a.shape[2:]), 1, 0)
    qpos = jnp.arange(S, dtype=jnp.int32).reshape(nb, Q_BLOCK)

    def one_block(args):
        qb, qib, wib, pb = args
        sel, valid = _indexer_select(qib, wib, ki, pb, ktop)
        return _sparse_attend(qb, _gather_rows(k, sel), _gather_rows(v, sel), valid)

    o = lax.map(one_block, (blocks(q), blocks(qi), blocks(wi), qpos))
    return jnp.moveaxis(o, 0, 1).reshape(q.shape)

def _gather_paged(pool, page_table, new_rows, sel):
    DB, T = new_rows.shape[:2]
    bidx = jnp.arange(DB)[:, None, None]
    ps = jnp.minimum(sel, PAST_LEN - 1)
    phys = page_table[bidx, ps // PAGE_SIZE]
    past = pool[phys, ps % PAGE_SIZE].astype(new_rows.dtype)
    new = new_rows[bidx, jnp.clip(sel - PAST_LEN, 0, T - 1)]
    return jnp.where((sel < PAST_LEN)[..., None, None], past, new)

def _dsa_sample(q, k, v, qi, ki, wi, cache_k, cache_v, cache_ki, page_table):
    DB, T = q.shape[:2]
    ktop = min(TOPK_MAX, (PAST_LEN + T) // 4)
    qpos = PAST_LEN + jnp.arange(T, dtype=jnp.int32)
    ki_past = cache_ki[page_table].reshape(DB, PAST_LEN, IDX_DIM)
    ki_all = jnp.concatenate([ki_past.astype(ki.dtype), ki], axis=1)
    sel, valid = _indexer_select(qi, wi, ki_all, qpos, ktop)
    ks = _gather_paged(cache_k, page_table, k, sel)
    vs = _gather_paged(cache_v, page_table, v, sel)
    return _sparse_attend(q, ks, vs, valid)

def _layer(x, pos, w, dsa_fn, conv_buf, ssm0):
    (ffn1_g, ffn1_u, ffn1_d, ln1_g, ln1_b, w_in, conv_w, a_log, dt_bias, gdn_norm_g,
     w_o, ln2_g, ln2_b, ffn2_g, ffn2_u, ffn2_d, ln3_g, ln3_b) = w
    B, T, _ = x.shape
    x = _layer_norm(DN_ALPHA * x + 0.5 * _swiglu(x, ffn1_g, ffn1_u, ffn1_d), ln1_g, ln1_b)
    parts = _split_columns(x @ w_in)
    q = _rope(parts['q_a'].reshape(B, T, N_HEADS, HEAD_DIM), pos, ROPE_DIM).reshape(B, T, N_KV_HEADS, GROUP, HEAD_DIM)
    k = _rope(parts['k_a'].reshape(B, T, N_KV_HEADS, HEAD_DIM), pos, ROPE_DIM)
    v = parts['v_a'].reshape(B, T, N_KV_HEADS, HEAD_DIM)
    qi = _rope(parts['q_idx'].reshape(B, T, IDX_HEADS, IDX_DIM), pos, IDX_ROPE_DIM)
    ki = _rope(parts['k_idx'].reshape(B, T, 1, IDX_DIM), pos, IDX_ROPE_DIM)[:, :, 0]
    wi = parts['w_idx'] * (IDX_HEADS ** -0.5 * IDX_DIM ** -0.5)
    o_a = dsa_fn(q, k, v, qi, ki, wi).reshape(B, T, D_MODEL)
    qkv, conv_new = _causal_conv(parts['qkv_b'], conv_buf, conv_w)
    qb, kb, vb = jnp.split(qkv, [GDN_HEADS * GDN_DK, 2 * GDN_HEADS * GDN_DK], axis=-1)
    qb = _l2norm(qb.reshape(B, T, GDN_HEADS, GDN_DK)) * (GDN_DK ** -0.5)
    kb = _l2norm(kb.reshape(B, T, GDN_HEADS, GDN_DK))
    vb = vb.reshape(B, T, GDN_HEADS, GDN_DV)
    beta = jax.nn.sigmoid(parts['beta_b'].astype(jnp.float32))
    g = -jnp.exp(a_log.astype(jnp.float32)) * jax.nn.softplus(parts['a_b'].astype(jnp.float32) + dt_bias.astype(jnp.float32))
    o_b, ssm_new = _gated_delta(qb, kb, vb, g, beta, ssm0)
    z = parts['z_b'].reshape(B, T, GDN_HEADS, GDN_DV).astype(jnp.float32)
    o_b = (_rms_norm(o_b, gdn_norm_g) * jax.nn.silu(z)).reshape(B, T, D_MODEL).astype(x.dtype)
    merged = jax.nn.sigmoid(parts['gate_a']) * o_a + jax.nn.sigmoid(parts['gate_b']) * o_b
    x = _layer_norm(DN_ALPHA * x + merged @ w_o, ln2_g, ln2_b)
    x = _layer_norm(DN_ALPHA * x + 0.5 * _swiglu(x, ffn2_g, ffn2_u, ffn2_d), ln3_g, ln3_b)
    return x, (k, v, ki, ssm_new.astype(ssm0.dtype), conv_new)

def setup_inputs(seed: int = 0) -> dict:
    key = jax.random.key(seed)
    ks = iter(jax.random.split(key, 40))
    f32 = jnp.float32

    def nrm(shape, scale):
        return jax.random.normal(next(ks), shape, f32) * scale

    n_pages = PAST_LEN // PAGE_SIZE
    n_phys = (DEC_BATCH * n_pages * 5) // 4
    page_table = jax.random.permutation(next(ks), n_phys)[: DEC_BATCH * n_pages].reshape(DEC_BATCH, n_pages).astype(jnp.int32)
    dt = jnp.exp(jax.random.uniform(next(ks), (DEPTH, GDN_HEADS), f32, math.log(1e-3), math.log(1e-1)))
    a_log = jnp.log(jax.random.uniform(next(ks), (DEPTH, GDN_HEADS), f32, 1.0, 16.0))
    return {
        'x_prompt': nrm((BATCH, SEQ, D_MODEL), 1.0),
        'x_sample': nrm((DEC_BATCH, DEC_SEQ, D_MODEL), 1.0),
        'cache_k': nrm((DEPTH, n_phys, PAGE_SIZE, N_KV_HEADS, HEAD_DIM), 1.0),
        'cache_v': nrm((DEPTH, n_phys, PAGE_SIZE, N_KV_HEADS, HEAD_DIM), 1.0),
        'cache_idx_k': nrm((DEPTH, n_phys, PAGE_SIZE, IDX_DIM), 1.0),
        'state_ssm': nrm((DEPTH, DEC_BATCH, GDN_HEADS, GDN_DK, GDN_DV), 0.1),
        'state_conv': nrm((DEPTH, DEC_BATCH, CONV_W - 1, CONV_DIM), 1.0),
        'page_table': page_table,
        'ffn1_w_gate': nrm((DEPTH, D_MODEL, D_FF), D_MODEL ** -0.5),
        'ffn1_w_up': nrm((DEPTH, D_MODEL, D_FF), D_MODEL ** -0.5),
        'ffn1_w_down': nrm((DEPTH, D_FF, D_MODEL), DN_BETA * D_FF ** -0.5),
        'ln1_g': 1.0 + nrm((DEPTH, D_MODEL), 0.05),
        'ln1_b': nrm((DEPTH, D_MODEL), 0.05),
        'w_in': nrm((DEPTH, D_MODEL, IN_COLS), D_MODEL ** -0.5),
        'conv_w': nrm((DEPTH, CONV_W, CONV_DIM), CONV_W ** -0.5),
        'a_log': a_log,
        'dt_bias': jnp.log(jnp.expm1(dt)),
        'gdn_norm_g': 1.0 + nrm((DEPTH, GDN_DV), 0.05),
        'w_o': nrm((DEPTH, D_MODEL, D_MODEL), DN_BETA * D_MODEL ** -0.5),
        'ln2_g': 1.0 + nrm((DEPTH, D_MODEL), 0.05),
        'ln2_b': nrm((DEPTH, D_MODEL), 0.05),
        'ffn2_w_gate': nrm((DEPTH, D_MODEL, D_FF), D_MODEL ** -0.5),
        'ffn2_w_up': nrm((DEPTH, D_MODEL, D_FF), D_MODEL ** -0.5),
        'ffn2_w_down': nrm((DEPTH, D_FF, D_MODEL), DN_BETA * D_FF ** -0.5),
        'ln3_g': 1.0 + nrm((DEPTH, D_MODEL), 0.05),
        'ln3_b': nrm((DEPTH, D_MODEL), 0.05),
    }

def reference(x_prompt, x_sample, cache_k, cache_v, cache_idx_k, state_ssm, state_conv, page_table,
              ffn1_w_gate, ffn1_w_up, ffn1_w_down, ln1_g, ln1_b, w_in, conv_w, a_log, dt_bias,
              gdn_norm_g, w_o, ln2_g, ln2_b, ffn2_w_gate, ffn2_w_up, ffn2_w_down, ln3_g, ln3_b):
    B, S, _ = x_prompt.shape
    DB, T, _ = x_sample.shape
    pos_p = jnp.arange(S, dtype=jnp.int32)
    pos_s = PAST_LEN + jnp.arange(T, dtype=jnp.int32)
    yp, ys = x_prompt, x_sample
    outs_p, outs_s = [], []
    for l in range(DEPTH):
        w = (ffn1_w_gate[l], ffn1_w_up[l], ffn1_w_down[l], ln1_g[l], ln1_b[l], w_in[l], conv_w[l],
             a_log[l], dt_bias[l], gdn_norm_g[l], w_o[l], ln2_g[l], ln2_b[l],
             ffn2_w_gate[l], ffn2_w_up[l], ffn2_w_down[l], ln3_g[l], ln3_b[l])
        conv0 = jnp.zeros((B, CONV_W - 1, CONV_DIM), x_prompt.dtype)
        ssm0 = jnp.zeros((B, GDN_HEADS, GDN_DK, GDN_DV), state_ssm.dtype)
        yp, st_p = _layer(yp, pos_p, w, _dsa_prompt, conv0, ssm0)
        dsa_s = functools.partial(_dsa_sample, cache_k=cache_k[l], cache_v=cache_v[l],
                                  cache_ki=cache_idx_k[l], page_table=page_table)
        ys, st_s = _layer(ys, pos_s, w, dsa_s, state_conv[l], state_ssm[l])
        outs_p.append(st_p)
        outs_s.append(st_s)
    k_p, v_p, ki_p, ssm_p, conv_p = [jnp.stack(a) for a in zip(*outs_p)]
    k_s, v_s, ki_s, ssm_s, conv_s = [jnp.stack(a) for a in zip(*outs_s)]
    return (yp, ys, k_p, v_p, ki_p, ssm_p, conv_p, k_s, v_s, ki_s, ssm_s, conv_s)


_drawn_inputs = setup_inputs


def setup_inputs(seed=0):
    import zlib

    import numpy as np

    out = dict(_drawn_inputs(seed))
    spreads = {}
    factors = {'gdn_norm_g': 7.45, 'cache_k': 3.921, 'cache_v': 3.135, 'cache_idx_k': 3.356}
    for name, (base, spread) in spreads.items():
        noise = np.random.default_rng([zlib.crc32(name.encode()), seed]).standard_normal(out[name].shape)
        drawn = base * np.exp(spread * noise) if base else spread * noise
        out[name] = jnp.asarray(drawn.astype(out[name].dtype))
    for name, factor in factors.items():
        out[name] = (out[name] * factor).astype(out[name].dtype)
    return out
```

```python
from contextlib import ExitStack

import numpy as np
import concourse.bass as bass
from concourse import mybir

F32 = mybir.dt.float32
I32 = mybir.dt.int32
ALU = mybir.AluOpType
ACT = mybir.ActivationFunctionType
AX = mybir.AxisListType

P = 128
D, SEQ, DEC, PAST, PAGE = 2048, 256, 8, 2048, 128
T = SEQ + DEC
NH, NKV, DH = 16, 4, 128
GRP = NH // NKV
IDXH, IDXD = 16, 64
DFF, CHUNK, CONVW = 5632, 64, 4
KD, KF = D // P, DFF // P
PAGES = PAST // PAGE
TOPK_P, TOPK_S = min(256, SEQ // 4), min(256, (PAST + 1) // 4)
THETA = 500000.0
ALPHA = 2.0 ** 0.25
SCALE = DH ** -0.5
LN_EPS, NORM_EPS = 1e-5, 1e-6
RING, CRING = 4, 2
QD = KF // 4
U_UP1 = 0
U_DN1 = U_UP1 + 2 * KF
U_MISC = U_DN1 + 4 * KD
U_IDXQ = U_MISC + 1
U_K = U_IDXQ + 8
U_V = U_K + 4
U_Q = U_V + 4
U_GATE = U_Q + NH
U_HEAD = U_GATE + 2 * KD
U_WO = U_HEAD + 4 * NH
U_UP2 = U_WO + KD
U_DN2 = U_UP2 + 2 * KF
T_DN1 = 0
T_MISC = T_DN1 + KD
T_IDXQ = T_MISC + 1
T_K = T_IDXQ + 8
T_V = T_K + 4
T_Q = T_V + 4
T_GATE = T_Q + NH
T_HEAD = T_GATE + 2 * KD
T_WO = T_HEAD + 4 * NH
T_DN2 = T_WO + KD
R_W, R_A, R_B = IDXD, IDXD + IDXH, IDXD + IDXH + NH
C_KI, C_K, C_V = 0, DEC, DEC + 4 * DEC
NEG, GONE = -1e38, -3e38
OFF = 1e30
LEVELS = (2, 4, 8, 16, 32)

STEPS = ["conv", "qk", "ss", "mix", "pt", "xt", "outer", "w0", "pv", "x0", "w1", "x1", "v0", "w2", "x2",
         "v1", "w3", "x3", "w4", "x4", "uw", "c0a", "c0b", "c1a", "c1b", "c2a", "c2b", "c3a", "c3b", "ms"]
PE_STEPS = [s for s in STEPS if s != "conv"]
NPE = len(PE_STEPS)
DVE_STEPS = [s for s in STEPS if s != "v0"]
SMALL = [s for s in PE_STEPS if s[0] != "v"]
ASKS = ["silu", "soft", "rinv", "decay", "rms"]
NA = len(ASKS)


def answered(h, name):
    return h * len(DVE_STEPS) + (DVE_STEPS.index(name) + 1)


def multiplied(h, name):
    return h * len(SMALL) + (SMALL.index(name) + 1)


def asked_of_act(h, name):
    return h * NA + (ASKS.index(name) + 1)


CONSTS = ["ident", "ones", "lv1", "lv2", "lv4", "lv8", "lv16", "lv32", "incl"]
EARLY = ["cumul", "whole", "dup", "rotdup", "roth", "roti", "spread"]


def host_constants():
    i, j = np.meshgrid(np.arange(P), np.arange(P), indexing="ij")
    same = (i // CHUNK) == (j // CHUNK)
    m = {"ident": i == j, "ones": i >= 0}
    for lv in (1, 2, 4, 8, 16, 32):
        m[f"lv{lv}"] = (i // (2 * lv) == j // (2 * lv)) & (i // lv % 2 == 1) & (j // lv % 2 == 0)
    m["incl"] = same & (j >= i)
    m["cumul"] = same & (i <= j)
    m["whole"] = same
    m["dup"] = (i < IDXD) & (j % IDXD == i)
    m["spread"] = i == R_W + j % IDXH
    m = {k: v.astype(np.float32) for k, v in m.items()}

    def rot(dim, half):
        r = np.zeros((P, P), np.float32)
        for b in range(0, P, dim):
            for k in range(half):
                r[b + half + k, b + k] = -1.0
                r[b + k, b + half + k] = 1.0
        return r

    m["roth"], m["roti"] = rot(DH, DH // 8), rot(IDXD, IDXD // 8)
    m["rotdup"] = m["dup"] @ m["roti"]
    mats = np.stack([m[k] for k in CONSTS], 1)
    early = np.stack([m[k] for k in EARLY], 1)
    pos = np.concatenate([np.arange(SEQ), np.full(DEC, PAST)]).astype(np.float32)

    def tables(dim, half):
        inv = (np.float32(THETA) ** (-np.arange(half, dtype=np.float32) / half)).astype(np.float32)
        ang = pos[None, :] * inv[:, None]
        c, s = np.ones((P, T), np.float32), np.zeros((P, T), np.float32)
        for b in range(0, P, dim):
            for o in (0, half):
                c[b + o:b + o + half] = np.cos(ang)
                s[b + o:b + o + half] = np.sin(ang)
        return c, s

    rope = np.stack([*tables(DH, DH // 8), *tables(IDXD, IDXD // 8)], 1)
    t = np.arange(P)[:, None]
    caus = np.concatenate([t >= np.arange(P)[None], t + P >= np.arange(2 * P)[None]], 1).astype(np.float32)
    own = (np.arange(P)[:, None] // IDXH == np.arange(DEC)[None]).astype(np.float32)
    rowm = np.zeros((P, 3), np.float32)
    rowm[R_W:R_W + IDXH, 0] = (IDXH ** -0.5) * (IDXD ** -0.5)
    rowm[R_A:R_A + NH, 1] = 1.0
    rowm[R_B:R_B + NH, 2] = 1.0
    eps = np.tile(np.array([[LN_EPS, NORM_EPS]], np.float32), (P, 1))
    return {"c_mats": mats.reshape(P, -1), "c_early": early.reshape(P, -1), "c_rope": rope.reshape(P, -1), "c_caus": caus,
            "c_own": own, "c_rowm": rowm, "c_eps": eps}


def build(nc, din, dout):
    with ExitStack() as ctx:
        def sb(name, shape, dt=F32):
            return ctx.enter_context(nc.sbuf_tensor(name, shape, dt))

        sems = {}

        def S(name):
            if name not in sems:
                sems[name] = ctx.enter_context(nc.semaphore(name))
            return sems[name]

        wring = sb("wring", [P, RING, KD * P])
        cring = sb("cring", [P, CRING, KD * P])
        xT = sb("xT", [P, KD, T])
        big = sb("big", [P, KF * T])
        gates = sb("gates", [P, 2, KD, T])
        gA, gB = gates[:, 0], gates[:, 1]
        hT = big[:, :].rearrange("p (k t) -> p k t", k=KF)
        at = [0]

        def part(n):
            a = big[:, at[0]:at[0] + n]
            at[0] += n
            return a

        qT = part(NH * T).rearrange("p (h t) -> p h t", h=NH)
        kT = part(NKV * T).rearrange("p (h t) -> p h t", h=NKV)
        vT = part(NKV * T).rearrange("p (h t) -> p h t", h=NKV)
        vtok = part(2 * NKV * DH).rearrange("p (s d) -> p s d", s=2)
        low = at[0]
        qiT = part(8 * T).rearrange("p (j t) -> p j t", j=8)
        zq = part(DEC * P).rearrange("p (b c) -> p b c", b=DEC)
        assert at[0] <= KF * T
        at[0] = low
        y3 = part(3 * T).rearrange("p (j t) -> p j t", j=3)
        e4 = part(4 * T).rearrange("p (j t) -> p j t", j=4)
        sq = part(2 * SEQ + 24)
        rs = part(2 * SEQ + 16)
        dab = part(4 * P)
        oS = part(NH * NH).rearrange("p (u n) -> p u n", u=NH)
        sgs = part(2 * NH * DEC).rearrange("p (k h b) -> p k h b", k=2, h=NH)
        pn, rin = (part(DEC * NH).rearrange("p (b n) -> p b n", b=DEC) for _ in range(2))
        assert at[0] <= KF * T, at[0]
        pool = sb("pool", [P, 2 * (PAST + 8)])
        rl = pool[:, 0:PAST + 1]
        scS = pool[0:DEC, PAST + 8:2 * PAST + 9]
        at2 = [0]

        def part2(n):
            a = pool[:, at2[0]:at2[0] + n]
            at2[0] += n
            return a

        qkn = part2(2 * SEQ)
        kbe, kd, vb = (part2(2 * P).rearrange("p (a b) -> p a b", a=2) for _ in range(3))
        lf, lm, qkt, wt = (part2(2 * P).rearrange("p (a b) -> p a b", a=2) for _ in range(4))
        xx = part2(4 * P).rearrange("p (x a b) -> p x a b", x=2, a=2)
        eg, qe, nwt = part2(2 * P), part2(2 * P), part2(2 * P)
        assert at2[0] <= 2 * (PAST + 8), at2[0]
        knT = part2(P)[0:DEC]
        turn = sb("turn", [P, 2608])
        at3 = [0]

        def part3(n):
            a = turn[:, at3[0]:at3[0] + n]
            at3[0] += n
            return a

        rope = part3(4 * T).rearrange("p (a t) -> p a t", a=4)
        caus, pscore = part3(3 * P), part3(3 * P)
        msc, val = part3(T), part3(T)
        valk = part3(2 * P).rearrange("p (a b) -> p a b", a=2)
        assert at3[0] == 2608
        at3[0] = 0
        dg, vh = (part3(2 * P).rearrange("p (a b) -> p a b", a=2) for _ in range(2))
        qh, sm, pT = part3(2 * P), part3(3 * P), part3(3 * P)
        vn, St = part3(P), part3(P)
        ob, zs, osq = part3(T), part3(T), part3(T)
        assert at3[0] <= 2608
        rms, zraw = sb("rms", [P, T]), sb("zraw", [P, T])
        raw = sb("raw", [P, 3, SEQ + CONVW - 1])
        sst = sb("sst", [P, DEC, P])
        early = sst[:, 0:len(EARLY), :]
        vm = e4.rearrange("p j t -> p (j t)")[0:DEC, 0:DEC * P].rearrange("p (b e) -> p b e", b=DEC)
        sal = sb("sal", [P, 4 * DEC, 4, NH])
        mats = sb("mats", [P, len(CONSTS), P])
        M = {k: mats[:, n, :] for n, k in enumerate(CONSTS)}
        M.update({k: early[:, n, :] for n, k in enumerate(EARLY)})
        own, rowm, epsc = sb("own", [P, DEC]), sb("rowm", [P, 3]), sb("epsc", [P, 2])
        lnp = sb("lnp", [P, 6, KD])
        cw = sb("cw", [P, NH, 12])
        cs = sb("cs", [P, NH, 3, CONVW, DEC])
        cpb = sb("cpb", [P, NH, 3, CONVW - 1])
        gnorm, alog, dtb = sb("gnorm", [P, 1]), sb("alog", [P, 1]), sb("dtb", [P, 1])
        pt = sb("pt", [1, DEC * PAGES], I32)
        raw2 = sb("raw2", [P, 2, T])
        tmp = sb("tmp", [P, T])
        kiT = sb("kiT", [P, T])
        gsc = sb("gsc", [P, NH, 4, 2])
        w8 = sb("w8", [P, DEC])
        pbias = sb("pbias", [P, 3 * P])
        top8 = sb("top8", [P, 8])
        mbt = sb("mbt", [P, DEC, PAGES])
        nbt = sb("nbt", [P, DEC])
        sn, gmx = (sb(n, [P, DEC, NH]) for n in ("sn", "gmx"))
        hc, hw = sb("hc", [P, 4, 2]), sb("hw", [P, 12])
        hg = sb("hg", [P, 2, DEC])
        kq = sb("kq", [P, 2, DEC])
        s8 = sb("s8", [P, 6, DEC])
        at_s = sb("at_s", [P, 6])
        mean, rstd = tmp, rms
        sqr = gates[:, 0]
        bank = [ctx.enter_context(nc.psum_tensor(f"bank{i}", [P, 512], F32)) for i in range(8)]
        acc = bank[0:2]
        gT, gK, gG, gO, aS, aV = bank[2:8]
        upb = [(bank[0], bank[1]), (bank[2], bank[3])]
        sg = raw2

        block = ctx.enter_context(nc.Block())

        class Own:

            def __init__(self, eng, sem):
                self.eng, self.sem, self.base, self.k, self.it, self.per = eng, sem, 0, 0, 0, 0

            def __call__(self, ins):
                ins.then_inc(self.sem, 1)
                self.k += 1
                self.eng.wait_ge(self.sem, self.it * self.per + (self.base + self.k))

            def enter(self, it, per):
                self.base, self.k, self.it, self.per = self.base + self.k, 0, it, per

            def leave(self, n):
                assert self.k == self.per, (self.k, self.per)
                self.base, self.k, self.it, self.per = self.base + n * self.per, 0, 0, 0

        def unit_done(eng, n, it=0, per=0):
            eng.wait_ge(S("units_done"), it * per + (n + 1))

        def landed(eng, n0, it=0, per=4):
            eng.wait_ge(S(f"weights_in{n0 % RING}"), (it * (per // RING) + (n0 // RING + 1)) * 16)

        def pages_landed(eng, c0, it=0, per=2, dmas=4):
            n = c0 // CRING + 1
            ki = DEC // CRING
            eng.wait_ge(S(f"pages_in{c0 % CRING}"),
                        (it * (per // CRING) * dmas + (n * PAGES if c0 < C_K else ki * PAGES + (n - ki) * dmas)) * 16)

        @block.sync
        def _(sp):
            small = [(mats[:, :, :], "c_mats"), (early, "c_early"), (rope, "c_rope"), (caus, "c_caus"),
                     (own[:, :], "c_own"), (rowm[:, :], "c_rowm"), (epsc[:, :], "c_eps"),
                     (lnp[:, :, :], "lnp"), (cw[:, :, :], "cw"),
                     (gnorm[:, :], "gnorm"), (alog[:, :], "alog"), (dtb[:, :], "dtb")]

            def weights(n0, u, it, per, src, w=KD * P):
                if n0 + u >= RING:
                    sp.wait_ge(S("units_done"), it * per + (n0 + u + 1 - RING))
                sp.dma_start(wring[:, (n0 + u) % RING, 0:w], src).then_inc(S(f"weights_in{(n0 + u) % RING}"), 16)

            sp.dma_start(xT[:, :, :], din["xT"].rearrange("p (k t) -> p k t", k=KD)).then_inc(S("x_in"), 16)
            sp.dma_start(mats[:, :, :], din["c_mats"].rearrange("p (k t) -> p k t", k=len(CONSTS))).then_inc(S("small_in"), 16)

            def ffn_loads(n_up, n_dn, up, dn):
                with sp.Fori(0, 2 * KF // 4) as i:
                    for u in range(4):
                        weights(n_up, u, i, 4, up[i * 4 + u])
                with sp.Fori(0, KD // 2) as i:
                    for u in range(8):
                        weights(n_dn, u, i, 8, dn[i * 8 + u], QD * P)

            for u in range(4):
                weights(U_UP1, u, 0, 4, din["up1"][u])
            for dst, name in small[1:]:
                s = din[name]
                if len(dst.shape) == 3:
                    s = s.rearrange("p (a b) -> p a b", a=dst.shape[1])
                sp.dma_start(dst, s).then_inc(S("small_in"), 16)
            for h in range(NH):
                sp.dma_start(cs[:, h, :, 0:CONVW - 1, :],
                             din["convs"][:, h].rearrange("p j (t b) -> p j t b", b=DEC)).then_inc(S("small_in"), 16)
            sp.dma_start(pt[:, :], din["pt"]).then_inc(S("table_in"), 16)
            with sp.Fori(0, 2 * KF // 4 - 1) as i:
                for u in range(4):
                    weights(U_UP1 + 4, u, i, 4, din["up1"][i * 4 + (u + 4)])
            with sp.Fori(0, KD // 2) as i:
                for u in range(8):
                    weights(U_DN1, u, i, 8, din["dn1"][i * 8 + u], QD * P)

            w_in = din["w_in"]

            def pages(c0, it, per, first, dmas, cache, width):
                if c0 >= CRING:
                    sp.wait_ge(S("page_units_done"), it * per + (c0 + 1 - CRING))
                for g in range(dmas):
                    page = sp.value_load(pt[0:1, bass.ds(first + g, 1)], min_val=0, max_val=cache.shape[0] - 1)
                    sp.dma_start(cring[:, c0 % CRING, g * width:(g + 1) * width], cache[page]).then_inc(
                        S(f"pages_in{c0 % CRING}"), 16)

            weights(U_MISC, 0, 0, 0, w_in[0])
            with sp.Fori(0, 2) as i:
                for u in range(4):
                    weights(U_IDXQ, u, i, 4, w_in[i * 4 + (U_IDXQ - U_MISC + u)])
            sp.wait_ge(S("table_in"), 16)
            for u in range(CRING):
                pages(C_KI + u, 0, 2, u * PAGES, PAGES, din["cki"], PAGE)
            with sp.Fori(0, DEC // 2 - 1) as i:
                for u in range(2):
                    pages(C_KI + CRING + u, i, 2, (i * 2 + (u + CRING)) * PAGES, PAGES, din["cki"], PAGE)
            with sp.Fori(0, (2 * NKV + NH) // 4) as i:
                for u in range(4):
                    weights(U_K, u, i, 4, w_in[i * 4 + (U_K - U_MISC + u)])
            sp.wait_ge(S("kv_ready"), 3)
            sp.dma_start(dout["kT"].rearrange("p (a b) -> p a b", a=NKV), kT).then_inc(S("stored"), 16)
            sp.dma_start(dout["vT"].rearrange("p (a b) -> p a b", a=NKV), vT).then_inc(S("stored"), 16)
            sp.dma_start(dout["kiT"], kiT[0:IDXD, :]).then_inc(S("stored"), 16)
            with sp.Fori(0, DEC) as i:
                for u in range(4):
                    weights(U_GATE, u, i, 4, w_in[i * 4 + (U_GATE - U_MISC + u)])
                    pages(C_K + u, i, 4, i * PAGES + 4 * u, 4, din["ck"], NKV * DH)
            for u in range(4):
                weights(U_HEAD, u, 0, 0, w_in[U_HEAD - U_MISC + u])
            with sp.Fori(0, NH - 1) as i:
                for u in range(4):
                    weights(U_HEAD + 4, u, i, 4, w_in[i * 4 + (U_HEAD + 4 - U_MISC + u)])
                    if u % 2:
                        pages(C_V + u // 2, i, 2, i * 8 + 4 * (u // 2), 4, din["cv"], NKV * DH)
            for u in range(2):
                pages(C_V + 2 * (NH - 1) + u, 0, 0, 8 * (NH - 1) + 4 * u, 4, din["cv"], NKV * DH)
            with sp.Fori(0, KD // 4) as i:
                for u in range(4):
                    weights(U_WO, u, i, 4, din["w_o"][i * 4 + u])
            ffn_loads(U_UP2, U_DN2, din["up2"], din["dn2"])
            sp.wait_ge(S("head_over"), NH)
            sp.dma_start(dout["convp"], cpb[:, :, :, :].rearrange("p h j t -> p (h j t)")).then_inc(S("stored"), 16)
            sp.dma_start(dout["convs"], cs[:, :, :, :, :].rearrange("p h j t b -> p (h j t b)")).then_inc(S("stored"), 16)
            for k in range(KD):
                sp.wait_ge(S("y_out_ready"), k + 1)
                sp.dma_start(dout["yT"][:, k * T:(k + 1) * T], xT[:, k, :]).then_inc(S("stored"), 16)
            sp.wait_ge(S("stored"), (5 + KD) * 16)

        @block.gpsimd
        def _(pool_e):
            def state_in(h, n):
                pool_e.dma_start(sst[:, :, :], din["ssm"][h]).then_inc(S("state_in"), 16)

            def state_steps(h, more):
                pool_e.wait_ge(S("answered"), answered(h, "outer"))
                pool_e.dma_start(dout["ssm_s"][h], sst[:, :, :]).then_inc(S("state_out"), 16)
                pool_e.wait_ge(S("state_out"), h * 16 + 16)
                if more:
                    state_in(h + 1, 0)
                pool_e.wait_ge(S("answered"), answered(h, "c3b"))
                pool_e.dma_start(dout["ssm_p"][h], St[:, :]).then_inc(S("prompt_state_out"), 16)
                pool_e.wait_ge(S("prompt_state_out"), h * 16 + 16)

            pool_e.wait_ge(S("part_max"), 1)
            pool_e.partition_all_reduce(gmx[:, :, :].rearrange("p b n -> p (b n)"),
                                        gmx[:, :, :].rearrange("p b n -> p (b n)"), P,
                                        bass.bass_isa.ReduceOp.max).then_inc(S("all_max"), 1)
            state_in(0, 0)
            with pool_e.Fori(0, NH - 1) as h:
                state_steps(h, True)
            state_steps(NH - 1, False)

        @block.tensor
        def _(pe):
            mm = pe.matmul
            pe.wait_ge(S("x_in"), 16)

            def unit(n0, u, it, per, rhs, out, nk=KD, first=True, last=True, lo=0, hi=None):
                slot = (n0 + u) % RING
                hi = nk if hi is None else hi
                if lo == 0:
                    landed(pe, n0 + u, it, per)
                for k in range(lo, hi):
                    ins = mm(out, wring[:, slot, k * P:(k + 1) * P], rhs(k),
                             start=first and k == 0, stop=last and k == nk - 1)
                if hi == nk:
                    ins.then_inc(S("units_done"), 1)

            def tile(n0, t0, u, it, per, rhs, lo=0, hi=KD):
                a = acc[(t0 + u) % 2]
                if lo == 0:
                    pe.wait_ge(S("acc_free"), it * per + (t0 + u + 1))
                unit(n0, u, it, per, rhs, a[:, 0:T], lo=lo, hi=hi)

            def ffn_up(n_up, base):
                with pe.Fori(0, KF // 2) as i:
                    for f in range(2):
                        g, up = upb[f]
                        pe.wait_ge(S("pair_free"), i * 2 + (base + f + 1))
                        unit(n_up, 2 * f, i, 4, lambda k: xT[:, k, :], g[:, 0:T])
                        unit(n_up, 2 * f + 1, i, 4, lambda k: xT[:, k, :], up[:, 0:T])

            def ffn_down(n_dn, t0, base):
                pe.wait_ge(S("pair_free"), base + KF + 2)
                with pe.Fori(0, KD // 2) as i:
                    for c in range(2):
                        pe.wait_ge(S("acc_free"), i * 2 + (t0 + c + 1))
                        for q in range(4):
                            unit(n_dn, 4 * c + q, i, 8, lambda k, q=q: hT[:, QD * q + k, :],
                                 acc[(t0 + c) % 2][:, 0:T], nk=QD, first=q == 0, last=q == 3)

            def norm(n):
                pe.wait_ge(S("y_ready"), (n + 1) * KD)
                for k in range(KD):
                    ins = mm(gG[:, 0:T], M["ones"], xT[:, k, :], start=k == 0, stop=k == KD - 1)
                ins.then_inc(S("stat"), 1)
                for k in range(KD):
                    if k % 4 == 0:
                        pe.wait_ge(S("squares"), 4 * n + k // 4 + 1)
                    ins = mm(gO[:, 0:T], M["ones"], sqr[:, k, :], start=k == 0, stop=k == KD - 1)
                ins.then_inc(S("stat"), 1)
                pe.wait_ge(S("x_ready"), (n + 1) * KD)

            ffn_up(U_UP1, 0)
            ffn_down(U_DN1, T_DN1, 0)
            pe.wait_ge(S("small_in"), 16 * 28)
            norm(0)

            x = lambda k: xT[:, k, :]
            tile(U_MISC, T_MISC, 0, 0, 0, x)
            pe.wait_ge(S("misc_raw"), 1)
            mm(gT[:, 0:T], M["dup"], msc[:, :], start=True, stop=True)
            mm(gK[:, 0:T], M["rotdup"], msc[:, :], start=True, stop=True).then_inc(S("ki_rot"), 1)

            def rotate(r, it, m):
                pe.wait_ge(S("raw_ready"), it + (r + 1))
                pe.wait_ge(S("rope_free"), it + (r + 1))
                mm([gT, gK][r % 2][:, 0:T], m, raw2[:, r % 2, :], start=True, stop=True).then_inc(S("rotated"), 1)

            pe.wait_ge(S("ki_ready"), 1)
            with pe.Fori(0, 2) as i:
                for u in range(4):
                    tile(U_IDXQ, T_IDXQ, u, i, 4, x)
                    if u:
                        rotate(u - 1, i * 4, M["roti"])
                rotate(3, i * 4, M["roti"])
            pe.wait_ge(S("val_ready"), 1)
            for t in range(2):
                ins = pe.transpose(gG[:, t * P:(t + 1) * P], val[:, t * P:(t + 1) * P], M["ident"])
            ins.then_inc(S("val_turned"), 1)
            pe.wait_ge(S("picked"), 1)
            mm(gO[:, 0:2 * NH * DEC], M["ones"], rms[:, 0:2 * NH * DEC], start=True, stop=True)
            mm(gO[:, 256:256 + DEC], M["spread"], val[:, SEQ:T], start=True, stop=True).then_inc(S("rows_done"), 1)
            pe.wait_ge(S("valk_ready"), 1)
            pe.wait_ge(S("rope_free"), 2 + 8)
            for t in range(2):
                mm(gK[:, 32 * t:32 * t + 16], M["cumul"], valk[:, t, R_A:R_A + NH], start=True, stop=True)
                ins = mm(gK[:, 32 * t + 16:32 * t + 32], M["whole"], valk[:, t, R_A:R_A + NH], start=True, stop=True)
            ins.then_inc(S("decays"), 1)
            n = 0
            for h in range(IDXH):
                for t in range(2):
                    a, w = [aS, aV][n % 2], (t + 1) * P
                    r0 = IDXD * (h % 2)
                    pe.wait_ge(S("pidx_free"), n + 1)
                    mm(a[:, 0:w], qiT[r0:r0 + IDXD, h // 2, t * P:(t + 1) * P], kiT[r0:r0 + IDXD, 0:w],
                       start=True, stop=True).then_inc(S("pidx_done"), 1)
                    n += 1
            idx = [gT, gK, gG, gO]
            pe.wait_ge(S("zq_ready"), 1)
            pe.wait_ge(S("decays_read"), 1)
            pe.wait_ge(S("pidx_free"), 2 + 32)
            for b in range(DEC):
                pages_landed(pe, C_KI + b)
                for c in range(4):
                    mm(idx[c][:, :], zq[:, b, :], cring[:, b % CRING, c * 512:(c + 1) * 512],
                       start=b == 0, stop=b == DEC - 1)
                ins = mm(aS[:, 0:1], zq[:, b, :], kiT[:, SEQ + b:SEQ + b + 1], start=b == 0, stop=b == DEC - 1)
                ins.then_inc(S("page_units_done"), 1)
            for c in range(4):
                pe.wait_ge(S("rectified"), c + 1)
                mm(idx[c][0:DEC, :], w8[:, :], rl[:, c * 512:(c + 1) * 512], start=True, stop=True).then_inc(S("weighed"), 1)
            pe.wait_ge(S("rectified"), 5)
            mm(aS[0:DEC, 0:1], w8[:, :], rl[:, PAST:PAST + 1], start=True, stop=True).then_inc(S("weighed"), 1)
            pe.wait_ge(S("scored"), 5)
            for u in range(4):
                tile(U_K, T_K, u, 0, 0, x)
                if u:
                    rotate(8 + u - 1, 0, M["roth"])
            rotate(11, 0, M["roth"])
            for u in range(4):
                tile(U_V, T_V, u, 0, 0, x)
                pe.wait_ge(S("v_raw"), u + 1)
                for t in range(2):
                    ins = pe.transpose([gG, gO][t][:, u * P:(u + 1) * P], vT[:, u, t * P:(t + 1) * P], M["ident"])
            ins.then_inc(S("v_turned"), 1)
            with pe.Fori(0, 4) as i:
                for u in range(4):
                    tile(U_Q, T_Q, u, i, 4, x)
                    if u:
                        rotate(12 + u - 1, i * 4, M["roth"])
                rotate(15, i * 4, M["roth"])
            pe.wait_ge(S("rope_free"), 2 + 28)
            with pe.Fori(0, DEC) as i:
                for u in range(4):
                    tile(U_GATE, T_GATE, u, i, 4, x)
                    pages_landed(pe, C_K + u, i, 4)
                    pe.wait_ge(S("kscore_free"), i * 4 + (u + 1))
                    for g in range(4):
                        for kv in range(NKV):
                            o = g * NH + kv * GRP
                            ins = mm([aS, aV][u % 2][:, o:o + GRP],
                                     cring[:, u % CRING, (g * NKV + kv) * P:(g * NKV + kv + 1) * P],
                                     qT[:, kv * GRP:(kv + 1) * GRP, bass.ds(i + SEQ, 1)], start=True, stop=True)
                    ins.then_inc(S("page_units_done"), 1)
            pe.wait_ge(S("selected"), 1)
            for g in range(PAGES):
                ins = pe.transpose(gT[:, g * DEC:(g + 1) * DEC], scS[:, g * PAGE:(g + 1) * PAGE], M["ident"][0:DEC, 0:DEC])
            mm(gK[:, 0:DEC], M["ones"][0:DEC, :], s8[0:DEC, 0, :], start=True, stop=True)
            ins = mm(gG[:, 0:DEC * NH], M["ones"], sn[:, :, :].rearrange("p b n -> p (b n)"), start=True, stop=True)
            ins.then_inc(S("masks_turned"), 1)
            for u in range(4):
                tile(U_HEAD, T_HEAD, u, 0, 0, x)
            pe.wait_ge(S("expsum"), 1)
            mm(gG[:, 0:DEC * NH], M["ones"], rin[:, :, :].rearrange("p b n -> p (b n)"),
               start=True, stop=True).then_inc(S("denoms"), 1)
            pe.wait_ge(S("sample_soft"), 1)

            def step(h, name):
                def after(dep):
                    pe.wait_ge(S("answered"), answered(h, dep))

                if name == "qk":
                    pe.wait_ge(S("head_copied"), h + 1)
                    after("conv")
                    mm(aS[:, 0:P], qh[:, 0:P], kT[:, h // GRP, 0:P], start=True, stop=True)
                    ins = mm(aS[:, P:3 * P], qh[:, P:2 * P], kT[:, h // GRP, 0:2 * P], start=True, stop=True)
                elif name == "pt":
                    after("qk")
                    for s in range(3):
                        ins = pe.transpose(aS[:, s * P:(s + 1) * P], sm[:, s * P:(s + 1) * P], M["ident"])
                elif name == "pv":
                    after("pt")
                    mm(aS[:, 0:P], vh[:, 0, :], pT[:, 0:P], start=True, stop=True)
                    mm(aS[:, P:2 * P], vh[:, 0, :], pT[:, P:2 * P], start=True, stop=False)
                    ins = mm(aS[:, P:2 * P], vh[:, 1, :], pT[:, 2 * P:3 * P], start=False, stop=True)
                elif name in ("v0", "v1"):
                    u = int(name[1])
                    if u == 0:
                        after("conv")
                    pages_landed(pe, C_V + u, h, 2)
                    for g in range(4):
                        for kv in range(NKV):
                            ins = mm(aV[:, kv * GRP:(kv + 1) * GRP],
                                     cring[:, u, (g * NKV + kv) * P:(g * NKV + kv + 1) * P],
                                     sal[:, 2 * h + u, g, kv * GRP:(kv + 1) * GRP],
                                     start=u == 0 and g == 0 and kv == 0, stop=u == 1 and g == 3,
                                     skip_group_check=True)
                    ins.then_inc(S("page_units_done"), 1)
                    return
                elif name == "ss":
                    after("conv")
                    mm(gT[:, :], M["ones"], sq[:, 0:2 * SEQ], start=True, stop=True)
                    ins = mm(gG[:, 0:24], M["ones"], sq[:, 2 * SEQ:2 * SEQ + 24], start=True, stop=True)
                elif name == "mix":
                    after("ss")
                    pe.wait_ge(S("state_in"), h * 16 + 16)
                    for p in range(2):
                        c = slice(p * P, (p + 1) * P)
                        pe.transpose(gT[:, c], qkn[:, SEQ + p * P:SEQ + (p + 1) * P], M["ident"])
                        pe.transpose(gT[:, SEQ + p * P:SEQ + (p + 1) * P], y3[:, 2, c], M["ident"])
                    for p in range(2):
                        kn = qkn[:, SEQ + p * P:SEQ + (p + 1) * P]
                        mm(gK[:, p * P:(p + 1) * P], kn, kn, start=True, stop=True)
                        mm(gK[:, SEQ + p * P:SEQ + (p + 1) * P], kn, qkn[:, p * P:(p + 1) * P], start=True, stop=True)
                    mm(gG[:, 0:2 * P], M["ones"], dg[:, :, :].rearrange("p a b -> p (a b)"), start=True, stop=True)
                    for b in range(DEC):
                        mm(gG[:, 256 + 2 * b:258 + 2 * b], sst[:, b, :], kq[:, :, b], start=True, stop=True)
                    ins = pe.transpose(gG[0:DEC, 384:512], kq[:, 0, :], M["ident"])
                elif name == "xt":
                    after("mix")
                    for p in range(2):
                        pe.transpose(gT[:, p * P:(p + 1) * P], xx[:, 0, p, :], M["ident"])
                    ins = pe.transpose(gT[0:DEC, 256:384], s8[:, 1, :], M["ident"])
                elif name == "outer":
                    after("xt")
                    mm(gT[:, :], knT[:, :], vm[:, 0:4, :].rearrange("p a b -> p (a b)"), start=True, stop=True)
                    ins = mm(gO[:, :], knT[:, :], vm[:, 4:8, :].rearrange("p a b -> p (a b)"), start=True, stop=True)
                elif name[0] == "w":
                    n = int(name[1])
                    after("xt" if n == 0 else f"x{n - 1}")
                    for p in range(2):
                        ins = mm(gK[:, p * P:(p + 1) * P], lm[:, p, :], xx[:, 1, p, :], start=True, stop=True)
                elif name[0] == "x":
                    after(f"w{name[1]}")
                    for p in range(2):
                        mm(gG[:, p * P:(p + 1) * P], wt[:, p, :], xx[:, 0, p, :], start=True, stop=True)
                        ins = mm(gG[:, (2 + p) * P:(3 + p) * P], xx[:, 0, p, :], wt[:, p, :], start=True, stop=True)
                elif name == "uw":
                    after("x4")
                    for p in range(2):
                        ins = mm(gK[:, p * P:(p + 1) * P], kbe[:, p, :], xx[:, 1, p, :], start=True, stop=True)
                elif name[0] == "c":
                    c = int(name[1])
                    p, r0 = c // 2, CHUNK * (c % 2)
                    rows = slice(r0, r0 + CHUNK)
                    if name[2] == "a":
                        after("uw" if c == 0 else f"c{c - 1}b")
                        o = gT[rows, c * P:(c + 1) * P]
                        mm(o, xx[:, 1, p, rows], vb[:, p, :], start=True, stop=False)
                        ins = mm(o, nwt[:, c * CHUNK:(c + 1) * CHUNK], St[:, :], start=False, stop=True)
                    else:
                        after(f"c{c}a")
                        o = gO[:, c * CHUNK:(c + 1) * CHUNK]
                        mm(o, St[:, :], qe[:, c * CHUNK:(c + 1) * CHUNK], start=True, stop=False)
                        mm(o, vn[rows, :], qkt[rows, p, rows], start=False, stop=True)
                        ins = mm(gG[:, 0:P], kd[rows, p, :], vn[rows, :], start=True, stop=True)
                elif name == "ms":
                    after("c3b")
                    ins = mm(gK[:, 0:T], M["ones"], osq[:, :], start=True, stop=True)
                ins.then_inc(S("multiplied"), 1)

            def head(h, more):
                n = 0
                for s in range(2 * KD):
                    if more:
                        u, half = s // 8, s % 8
                        tile(U_HEAD + 4, T_HEAD + 4, u, h, 4, x, lo=2 * half, hi=2 * half + 2)
                    while n < NPE and (n * 2 * KD) // NPE <= s:
                        step(h, PE_STEPS[n])
                        n += 1

            with pe.Fori(0, NH - 1) as h:
                head(h, True)
            head(NH - 1, False)
            with pe.Fori(0, KD // 4) as i:
                for u in range(4):
                    if u == 0:
                        pe.wait_ge(S("merged"), 1)
                    tile(U_WO, T_WO, u, i, 4, lambda k: gA[:, k, :])
            norm(1)
            ffn_up(U_UP2, KF)
            ffn_down(U_DN2, T_DN2, KF)
            norm(2)

        @block.scalar
        def _(act):
            do = act.activation
            own_a = Own(act, S("act_own"))

            def silu_gates(n_up, base):
                with act.Fori(0, KF // 2) as i:
                    for f in range(2):
                        unit_done(act, n_up + 2 * f, i, 4)
                        act.wait_ge(S("pair_free"), i * 2 + (base + f + 1))
                        do(sg[:, f, :], upb[f][0][:, 0:T], ACT.Silu).then_inc(S("silu_done"), 1)

            def norm(n):
                for k in range(0, KD, 4):
                    act.wait_ge(S("centred"), 4 * n + k // 4 + 1)
                    do(sqr[:, k:k + 4, :], xT[:, k:k + 4, :], ACT.Square).then_inc(S("squares"), 1)
                act.wait_ge(S("stat"), 2 * n + 2)
                do(rstd[:, :], gO[:, 0:T], ACT.Sqrt, bias=epsc[:, 0:1], scale=1.0 / D).then_inc(S("deviation"), 1)
                for k in range(KD):
                    act.wait_ge(S("scaled"), n * KD + k + 1)
                    do(xT[:, k, :], xT[:, k, :], ACT.Identity, bias=lnp[:, 2 * n + 1, k:k + 1],
                       scale=lnp[:, 2 * n, k:k + 1]).then_inc(S("x_ready"), 1)
                    if n == 2:
                        act.wait_ge(S("x_ready"), n * KD + k + 1)
                        act.sem_inc(S("y_out_ready"), 1)

            silu_gates(U_UP1, 0)
            act.wait_ge(S("small_in"), 16 * 28)
            norm(0)
            unit_done(act, U_MISC)
            do(msc[:, :], acc[T_MISC % 2][:, 0:T], ACT.Copy).then_inc(S("misc_raw"), 1)
            act.wait_ge(S("misc_raw"), 1)
            act.sem_inc(S("acc_free"), 1)
            own_a(do(raw2[:, 0, :], msc[:, :], ACT.Exp, scale=-1.0))
            act.sem_inc(S("misc_exp"), 1)
            own_a(do(val[:, :], msc[:, :], ACT.Abs, bias=dtb[:, 0:1]))
            own_a(do(val[:, :], val[:, :], ACT.Exp, scale=-1.0))
            own_a(do(val[:, :], val[:, :], ACT.Ln, bias=1.0))
            own_a(do(alog[:, :], alog[:, :], ACT.Exp))
            act.sem_inc(S("misc_exp"), 1)

            def evacuate(n0, t0, u, it, per, outs):
                unit_done(act, n0 + u, it, per)
                a = acc[(t0 + u) % 2]
                for dst, cols, func in outs:
                    own_a(do(dst, a[:, cols], func))
                act.sem_inc(S("acc_free"), 1)

            def raw_tile(n0, t0, r0, u, it):
                act.wait_ge(S("rope_free"), it * 4 + (r0 + u + 1))
                evacuate(n0, t0, u, it, 4, [(raw2[:, (r0 + u) % 2, :], slice(0, T), ACT.Copy)])
                act.sem_inc(S("raw_ready"), 1)

            with act.Fori(0, 2) as i:
                own_a.enter(i, 4)
                for u in range(4):
                    raw_tile(U_IDXQ, T_IDXQ, 0, u, i)
            own_a.leave(2)
            act.wait_ge(S("val_turned"), 1)
            do(valk[:, :, :], gG[:, 0:2 * P].rearrange("p (a b) -> p a b", a=2), ACT.Copy).then_inc(S("valk_ready"), 1)
            act.wait_ge(S("rows_done"), 1)
            own_a(do(sgs[:, 0, :, :], gO[:, 0:P].rearrange("p (h b) -> p h b", b=DEC), ACT.Exp))
            own_a(do(sgs[:, 1, :, :], gO[:, P:2 * P].rearrange("p (h b) -> p h b", b=DEC), ACT.Copy))
            act.sem_inc(S("rows_read"), 1)
            act.wait_ge(S("exponents"), 1)
            for kind in (2, 3):
                own_a(do(gsc[:, :, kind, :], gsc[:, :, kind, :], ACT.Exp))
            act.sem_inc(S("factors"), 1)
            n = 0
            for h in range(IDXH):
                for t in range(2):
                    w = (t + 1) * P
                    act.wait_ge(S("pidx_done"), n + 1)
                    act.wait_ge(S("pterm_free"), n + 1)
                    own_a(do(rl[:, (n % 2) * 256:(n % 2) * 256 + w], [aS, aV][n % 2][:, 0:w], ACT.Relu))
                    act.sem_inc(S("pidx_free"), 1)
                    act.sem_inc(S("pterm"), 1)
                    n += 1
            act.wait_ge(S("page_units_done"), C_K)
            act.wait_ge(S("pterm_free"), 2 + 32)
            for c, b in enumerate((gT, gK, gG, gO)):
                do(rl[:, c * 512:(c + 1) * 512], b[:, :], ACT.Relu).then_inc(S("rectified"), 1)
            do(rl[:, PAST:PAST + 1], aS[:, 0:1], ACT.Relu).then_inc(S("rectified"), 1)
            for c, b in enumerate((gT, gK, gG, gO)):
                act.wait_ge(S("weighed"), c + 1)
                do(scS[:, c * 512:(c + 1) * 512], b[0:DEC, :], ACT.Copy).then_inc(S("scored"), 1)
            act.wait_ge(S("weighed"), 5)
            do(scS[:, PAST:PAST + 1], aS[0:DEC, 0:1], ACT.Copy).then_inc(S("scored"), 1)
            for u in range(4):
                raw_tile(U_K, T_K, 8, u, 0)
            for u in range(4):
                evacuate(U_V, T_V, u, 0, 0, [(vT[:, u, :], slice(0, T), ACT.Copy)])
                act.sem_inc(S("v_raw"), 1)
            act.wait_ge(S("v_turned"), 1)
            own_a(do(vtok[:, 0, :], gG[:, :], ACT.Copy))
            own_a(do(vtok[:, 1, :], gO[:, :], ACT.Copy))
            act.sem_inc(S("kv_ready"), 1)
            with act.Fori(0, 4) as i:
                own_a.enter(i, 4)
                for u in range(4):
                    raw_tile(U_Q, T_Q, 12, u, i)
            own_a.leave(4)
            flat = gates[:, :, :, :].rearrange("p g k t -> p (g k) t")
            with act.Fori(0, DEC) as i:
                own_a.enter(i, 8)
                for u in range(4):
                    evacuate(U_GATE, T_GATE, u, i, 4, [(flat[:, i * 4 + u, :], slice(0, T), ACT.Sigmoid)])
                    act.wait_ge(S("page_units_done"), i * 4 + (C_K + u + 1))
                    own_a(do(sal[:, i * 4 + u, :, :], [aS, aV][u % 2][:, 0:64].rearrange("p (g n) -> p g n", g=4),
                             ACT.Copy, scale=SCALE))
                    act.sem_inc(S("kscore_free"), 1)
            own_a.leave(DEC)
            act.sem_inc(S("past_scored"), 1)

            def qkvz(h, u, it):
                more = 0 if it is None else 4
                if u < 3:
                    if u == 0 and it is not None:
                        act.wait_ge(S("answered"), answered(it, "conv"))
                    evacuate(U_HEAD + more, T_HEAD + more, u, 0 if it is None else it, 4,
                             [(raw[:, u, CONVW - 1:], slice(0, SEQ), ACT.Copy),
                              (cs[:, h, u, CONVW - 1, :], slice(SEQ, T), ACT.Copy)])
                else:
                    evacuate(U_HEAD + more, T_HEAD + more, u, 0 if it is None else it, 4,
                             [(zraw[:, :], slice(0, T), ACT.Copy)])
                    act.sem_inc(S("head_raw"), 1)

            for u in range(4):
                qkvz(0, u, None)
            act.wait_ge(S("shifted"), 1)
            own_a(do(sal[:, :, :, :], sal[:, :, :, :], ACT.Exp))
            own_a(do(pn[:, :, :], pn[:, :, :], ACT.Exp))
            act.sem_inc(S("soft_exp"), 1)

            def answer(h, name):
                act.wait_ge(S("asked"), asked_of_act(h, name))
                if name == "silu":
                    own_a(do(e4[:, 0:3, :], y3, ACT.Exp, scale=-1.0))
                    own_a(do(e4[:, 3, :], zraw[:, :], ACT.Exp, scale=-1.0))
                elif name == "rinv":
                    act.wait_ge(S("multiplied"), multiplied(h, "ss"))
                    own_a(do(rs[:, 0:512], gT[:, :], ACT.Ln, bias=epsc[:, 1:2]))
                    own_a(do(rs[:, 512:528], gG[:, 0:16], ACT.Ln, bias=epsc[:, 1:2]))
                    own_a(do(rs[:, :], rs[:, :], ACT.Exp, scale=-0.5))
                elif name == "soft":
                    own_a(do(sm[:, 0:P], sm[:, 0:P], ACT.Exp, bias=at_s[:, 2:3], accum_out=at_s[:, 4:5]))
                    own_a(do(sm[:, P:3 * P], sm[:, P:3 * P], ACT.Exp, bias=at_s[:, 3:4], accum_out=at_s[:, 5:6]))
                elif name == "decay":
                    own_a(do(dab[:, 0:256], dab[:, 0:256], ACT.Exp, scale=-1.0))
                    own_a(do(dab[:, 256:512], dab[:, 256:512], ACT.Exp))
                    own_a(do(eg, gG[:, 0:256], ACT.Exp))
                elif name == "rms":
                    act.wait_ge(S("multiplied"), multiplied(h, "ms"))
                    own_a(do(rms[:, :], gK[:, 0:T], ACT.Ln, bias=epsc[:, 1:2], scale=1.0 / P))
                    own_a(do(rms[:, :], rms[:, :], ACT.Exp, scale=-0.5))
                act.sem_inc(S("act_answered"), 1)

            ANSWER_AT = {"silu": "conv", "soft": "qk", "rinv": "ss", "decay": "mix", "rms": "ms"}
            COUNT = 2 + 2 + 3 + 3 + 2

            def head(h, more):
                if h is not NH - 1 or True:
                    own_a(do(qh[:, :], qT[:, h, 0:SEQ], ACT.Copy))
                    own_a(do(vh[:, :, :], vtok.rearrange("p s (k d) -> p s k d", k=NKV)[:, :, h // GRP, :], ACT.Copy))
                    act.sem_inc(S("head_copied"), 1)
                n, done = 0, set()
                answer(h, "silu")
                for s in range(2 * KD):
                    while n < NPE and (n * 2 * KD) // NPE <= s:
                        for a, st in ANSWER_AT.items():
                            if st == PE_STEPS[n]:
                                answer(h, a)
                        n += 1
                    if more and s % 8 == 7:
                        qkvz(h + 1, s // 8, h)

            with act.Fori(0, NH - 1) as h:
                own_a.enter(h, COUNT + 2 + 7)
                head(h, True)
            own_a.leave(NH - 1)
            head(NH - 1, False)
            norm(1)
            silu_gates(U_UP2, KF)
            norm(2)

        @block.vector
        def _(v):
            own_v = Own(v, S("dve_own"))
            ts, stt, tt, cp = v.tensor_scalar, v.scalar_tensor_tensor, v.tensor_tensor, v.tensor_copy

            def bc(ap, shape):
                return ap.to_broadcast(shape)

            v.sem_inc(S("pair_free"), 2)
            v.sem_inc(S("acc_free"), 2)
            v.sem_inc(S("rope_free"), 2)
            v.sem_inc(S("pidx_free"), 2)
            v.sem_inc(S("pterm_free"), 2)
            v.sem_inc(S("kscore_free"), 2)

            def products(n_up, base):
                with v.Fori(0, KF // 2) as i:
                    for f in range(2):
                        unit_done(v, n_up + 2 * f + 1, i, 4)
                        v.wait_ge(S("silu_done"), i * 2 + (base + f + 1))
                        stt(out=hT[:, i * 2 + f, :], in0=upb[f][1][:, 0:T], scalar=0.5, in1=sg[:, f, :],
                            op0=ALU.mult, op1=ALU.mult).then_inc(S("pair_free"), 1)

            def residual(n0, units, t0, n):
                with v.Fori(0, KD // 2) as i:
                    for c in range(2):
                        unit_done(v, n0 + units * (c + 1) - 1, i, 2 * units)
                        stt(out=xT[:, i * 2 + c, :], in0=xT[:, i * 2 + c, :], scalar=ALPHA, in1=acc[(t0 + c) % 2][:, 0:T],
                            op0=ALU.mult, op1=ALU.add).then_inc(S("y_ready"), 1)
                        v.wait_ge(S("y_ready"), i * 2 + (n * KD + c + 1))
                        v.sem_inc(S("acc_free"), 1)

            def norm(n):
                v.wait_ge(S("stat"), 2 * n + 1)
                own_v(ts(mean[:, :], gG[:, 0:T], 1.0 / D, None, ALU.mult))
                for k in range(0, KD, 4):
                    tt(xT[:, k:k + 4, :], xT[:, k:k + 4, :], mean[:, :].unsqueeze(1).to_broadcast([P, 4, T]),
                       ALU.subtract).then_inc(S("centred"), 1)
                v.wait_ge(S("centred"), 4 * n + 4)
                v.wait_ge(S("deviation"), n + 1)
                own_v(v.reciprocal(rstd[:, :], rstd[:, :]))
                v.wait_ge(S("squares"), 4 * n + 4)
                for k in range(KD):
                    tt(xT[:, k, :], xT[:, k, :], rstd[:, :], ALU.mult).then_inc(S("scaled"), 1)

            products(U_UP1, 0)
            residual(U_DN1, 4, T_DN1, 0)
            norm(0)
            v.wait_ge(S("small_in"), 16 * 28)
            own_v(v.memset(raw[:, :, 0:CONVW - 1], 0.0))
            v.wait_ge(S("ki_rot"), 1)
            v.wait_ge(S("misc_raw"), 1)
            own_v(tt(kiT[:, :], gT[:, 0:T], rope[:, 2, :], ALU.mult))
            own_v(tt(tmp[:, :], gK[:, 0:T], rope[:, 3, :], ALU.mult))
            own_v(tt(kiT[:, :], kiT[:, :], tmp[:, :], ALU.add))
            v.sem_inc(S("kv_ready"), 1)
            v.wait_ge(S("misc_exp"), 2)
            own_v(ts(raw2[:, 0, :], raw2[:, 0, :], 1.0, None, ALU.add))
            own_v(v.reciprocal(raw2[:, 0, :], raw2[:, 0, :]))
            own_v(ts(raw2[:, 0, :], raw2[:, 0, :], rowm[:, 2:3], None, ALU.mult))
            own_v(ts(alog[:, :], alog[:, :], -1.0, rowm[:, 1:2], ALU.mult, ALU.mult))
            own_v(ts(tmp[:, :], msc[:, :], dtb[:, 0:1], 0.0, ALU.add, ALU.max))
            own_v(tt(val[:, :], val[:, :], tmp[:, :], ALU.add))
            own_v(stt(out=val[:, :], in0=val[:, :], scalar=alog[:, 0:1], in1=raw2[:, 0, :], op0=ALU.mult, op1=ALU.add))
            own_v(stt(out=val[:, :], in0=msc[:, :], scalar=rowm[:, 0:1], in1=val[:, :], op0=ALU.mult, op1=ALU.add))
            v.sem_inc(S("val_ready"), 1)
            own_v(tt(rms[:, 0:256].rearrange("p (k b) -> p k b", b=DEC),
                     M["ident"][:, R_A:R_A + 2 * NH].unsqueeze(2).to_broadcast([P, 2 * NH, DEC]),
                     val[:, SEQ:T].unsqueeze(1).to_broadcast([P, 2 * NH, DEC]), ALU.mult))
            v.sem_inc(S("picked"), 1)
            v.sem_inc(S("ki_ready"), 1)

            def roped(r0, u, it, dst, table):
                v.wait_ge(S("rotated"), it * 4 + (r0 + u + 1))
                r = r0 + u
                own_v(tt(dst, raw2[:, r % 2, :], rope[:, table, :], ALU.mult))
                own_v(tt(tmp[:, :], [gT, gK][r % 2][:, 0:T], rope[:, table + 1, :], ALU.mult))
                own_v(tt(dst, dst, tmp[:, :], ALU.add))
                v.sem_inc(S("rope_free"), 1)

            with v.Fori(0, 2) as i:
                own_v.enter(i, 12)
                for u in range(4):
                    roped(0, u, i, qiT[:, i * 4 + u, :], 2)
            own_v.leave(2)
            own_v(v.memset(zq[:, :, :], 0.0))
            for h2 in range(2):
                rows = slice(h2 * IDXD, (h2 + 1) * IDXD)
                for b in range(DEC):
                    own_v(cp(zq[rows, b, b * IDXH + h2:(b + 1) * IDXH:2], qiT[rows, :, SEQ + b]))
            v.sem_inc(S("zq_ready"), 1)
            v.wait_ge(S("decays"), 1)
            v.wait_ge(S("rows_done"), 1)
            v.wait_ge(S("valk_ready"), 1)
            v.wait_ge(S("rows_read"), 1)
            own_v(tt(w8[:, :], gO[:, 256:256 + DEC], own[:, :], ALU.mult))
            for t in range(2):
                own_v(cp(gsc[:, :, 0, t], gK[:, 32 * t:32 * t + 16]))
                own_v(cp(gsc[:, :, 1, t], valk[:, t, R_B:R_B + NH]))
                own_v(cp(gsc[:, :, 2, t], gK[:, 32 * t:32 * t + 16]))
                own_v(tt(gsc[:, :, 3, t], gK[:, 32 * t + 16:32 * t + 32], gsc[:, :, 0, t], ALU.subtract))
            v.sem_inc(S("exponents"), 1)
            v.wait_ge(S("factors"), 1)
            own_v(tt(gsc[:, :, 2, :], gsc[:, :, 2, :], gsc[:, :, 1, :], ALU.mult))
            v.sem_inc(S("decays_read"), 1)
            own_v(v.memset(pscore[:, :], 0.0))
            n = 0
            for h in range(IDXH):
                for t in range(2):
                    w, c = (t + 1) * P, slice(t * P, 3 * P if t else P)
                    v.wait_ge(S("pterm"), n + 1)
                    own_v(stt(out=pscore[:, c], in0=rl[:, (n % 2) * 256:(n % 2) * 256 + w],
                              scalar=valk[:, t, R_W + h:R_W + h + 1], in1=pscore[:, c], op0=ALU.mult, op1=ALU.add))
                    v.sem_inc(S("pterm_free"), 1)
                    n += 1
            for u in range(4):
                roped(8, u, 0, kT[:, u, :], 0)
            v.sem_inc(S("kv_ready"), 1)
            with v.Fori(0, 4) as i:
                own_v.enter(i, 12)
                for u in range(4):
                    roped(12, u, i, qT[:, i * 4 + u, :], 0)
            own_v.leave(4)
            own_v(tt(pscore[:, :], pscore[:, :], caus[:, :], ALU.mult))
            own_v(ts(pbias[:, :], caus[:, :], -1.0, -NEG, ALU.add, ALU.mult))
            own_v(tt(pscore[:, :], pscore[:, :], pbias[:, :], ALU.add))
            for t in range(2):
                c = slice(t * P, 3 * P if t else P)
                for _r in range(TOPK_P // 8):
                    own_v(v.max(out=top8[:, :], in_=pscore[:, c]))
                    own_v(v.match_replace(out=pscore[:, c], in_to_replace=top8[:, :], in_values=pscore[:, c], imm_value=GONE))
            own_v(stt(out=pbias[:, :], in0=pscore[:, :], scalar=GONE, in1=caus[:, :], op0=ALU.is_equal, op1=ALU.mult))
            own_v(ts(pbias[:, :], pbias[:, :], -1.0, OFF, ALU.add, ALU.mult))
            v.wait_ge(S("scored"), 5)
            for _r in range(TOPK_S // 8):
                own_v(v.max(out=top8[0:DEC, :], in_=scS[:, :]))
                own_v(v.match_replace(out=scS[:, :], in_to_replace=top8[0:DEC, :], in_values=scS[:, :], imm_value=GONE))
            own_v(ts(scS[:, :], scS[:, :], GONE, None, ALU.is_equal))
            own_v(ts(s8[0:DEC, 0, :], M["ident"][0:DEC, 0:DEC], scS[:, PAST:PAST + 1], None, ALU.mult))
            for kv in range(NKV):
                own_v(tt(sn[:, :, kv * GRP:(kv + 1) * GRP].rearrange("p b g -> p g b"),
                         qT[:, kv * GRP:(kv + 1) * GRP, SEQ:T],
                         kT[:, kv, SEQ:T].unsqueeze(1).to_broadcast([P, GRP, DEC]), ALU.mult))
            v.sem_inc(S("selected"), 1)
            v.wait_ge(S("masks_turned"), 1)
            own_v(ts(mbt[:, :, :].rearrange("p b g -> p g b"), gT[:, 0:P].rearrange("p (g b) -> p g b", b=DEC),
                     -1.0, OFF, ALU.add, ALU.mult))
            own_v(ts(nbt[:, :], gK[:, 0:DEC], -1.0, OFF, ALU.add, ALU.mult))
            own_v(ts(sn[:, :, :], gG[:, 0:P].rearrange("p (b n) -> p b n", n=NH), SCALE, None, ALU.mult))
            own_v(tt(sn[:, :, :], sn[:, :, :], nbt[:, :].unsqueeze(2).to_broadcast([P, DEC, NH]), ALU.add))
            v.wait_ge(S("past_scored"), 1)
            salf = sal[:, :, :, :].rearrange("p u g n -> p (u g) n")
            own_v(tt(salf, salf, mbt[:, :, :].rearrange("p b g -> p (b g)").unsqueeze(2).to_broadcast([P, P, NH]), ALU.add))
            bgn = sal[:, :, :, :].rearrange("p (b q) g n -> p b n (q g)", b=DEC)
            own_v(v.tensor_reduce(gmx[:, :, :], bgn, AX.X, ALU.max))
            v.sem_inc(S("part_max"), 1)
            v.wait_ge(S("all_max"), 1)
            own_v(tt(gmx[:, :, :], gmx[:, :, :], sn[:, :, :], ALU.max))
            for b in range(DEC):
                own_v(tt(salf[:, b * PAGES:(b + 1) * PAGES, :], salf[:, b * PAGES:(b + 1) * PAGES, :],
                         gmx[:, b, :].unsqueeze(1).to_broadcast([P, PAGES, NH]), ALU.subtract))
            own_v(tt(pn[:, :, :], sn[:, :, :], gmx[:, :, :], ALU.subtract))
            v.sem_inc(S("shifted"), 1)
            v.wait_ge(S("soft_exp"), 1)
            own_v(v.tensor_reduce(rin[:, :, :], bgn, AX.X, ALU.add))
            v.sem_inc(S("expsum"), 1)
            v.wait_ge(S("denoms"), 1)
            own_v(tt(rin[:, :, :], gG[:, 0:P].rearrange("p (b n) -> p b n", n=NH), pn[:, :, :], ALU.add))
            own_v(v.reciprocal(rin[:, :, :], rin[:, :, :]))
            v.sem_inc(S("sample_soft"), 1)

            def ask(h, name, wait=True):
                v.sem_inc(S("asked"), 1)
                if wait:
                    v.wait_ge(S("act_answered"), asked_of_act(h, name))

            def two(ap):
                return ap.unsqueeze(1).to_broadcast([P, 2, P])

            def step(h, name):
                if name == "v1":
                    v.wait_ge(S("page_units_done"), h * 2 + (C_V + 2))
                elif name != "conv":
                    v.wait_ge(S("multiplied"), multiplied(h, name))
                if name == "conv":
                    v.wait_ge(S("head_raw"), h + 1)
                    own_v(cp(hw[:, :], cw[:, h, :]))
                    own_v(cp(hc[:, :, :], gsc[:, h, :, :]))
                    own_v(cp(hg[:, :, :], sgs[:, :, h, :]))
                    own_v(cp(cpb[:, h, :, :], raw[:, :, SEQ:]))
                    for j in range(3):
                        own_v(ts(y3[:, j, 0:SEQ], raw[:, j, 0:SEQ], hw[:, 4 * j:4 * j + 1], None, ALU.mult))
                        own_v(ts(y3[:, j, SEQ:T], cs[:, h, j, 0, :], hw[:, 4 * j:4 * j + 1], None, ALU.mult))
                        for k in range(1, CONVW):
                            w = hw[:, 4 * j + k:4 * j + k + 1]
                            own_v(stt(out=y3[:, j, 0:SEQ], in0=raw[:, j, k:k + SEQ], scalar=w, in1=y3[:, j, 0:SEQ],
                                      op0=ALU.mult, op1=ALU.add))
                            own_v(stt(out=y3[:, j, SEQ:T], in0=cs[:, h, j, k, :], scalar=w, in1=y3[:, j, SEQ:T],
                                      op0=ALU.mult, op1=ALU.add))
                    ask(h, "silu")
                    own_v(ts(e4, e4, 1.0, None, ALU.add))
                    own_v(v.reciprocal(e4, e4))
                    own_v(tt(y3, y3, e4[:, 0:3, :], ALU.mult))
                    own_v(tt(zs[:, :], zraw[:, :], e4[:, 3, :], ALU.mult))
                    own_v(tt(sq[:, 0:2 * SEQ].rearrange("p (a b) -> p a b", a=2), y3[:, 0:2, 0:SEQ], y3[:, 0:2, 0:SEQ], ALU.mult))
                    own_v(tt(sq[:, 512:528].rearrange("p (a b) -> p a b", a=2), y3[:, 0:2, SEQ:T], y3[:, 0:2, SEQ:T], ALU.mult))
                    own_v(tt(sq[:, 528:536], y3[:, 0, SEQ:T], y3[:, 1, SEQ:T], ALU.mult))
                    for p in range(2):
                        own_v(ts(dg[:, p, :], M["ident"], hc[:, 0, p:p + 1], None, ALU.mult))
                elif name == "ss":
                    ask(h, "rinv")
                    own_v(stt(out=qkn[:, 0:SEQ], in0=y3[:, 0, 0:SEQ], scalar=SCALE, in1=rs[:, 0:SEQ], op0=ALU.mult, op1=ALU.mult))
                    own_v(tt(qkn[:, SEQ:512], y3[:, 1, 0:SEQ], rs[:, SEQ:512], ALU.mult))
                    own_v(tt(kq[:, 0, :], y3[:, 1, SEQ:T], rs[:, 520:528], ALU.mult))
                    own_v(stt(out=kq[:, 1, :], in0=y3[:, 0, SEQ:T], scalar=SCALE, in1=rs[:, 512:520], op0=ALU.mult, op1=ALU.mult))
                    own_v(stt(out=s8[:, 2, :], in0=gG[:, 16:24], scalar=SCALE, in1=rs[:, 512:520], op0=ALU.mult, op1=ALU.mult))
                    own_v(tt(s8[:, 2, :], s8[:, 2, :], rs[:, 520:528], ALU.mult))
                elif name == "mix":
                    for p in range(2):
                        c = slice(p * P, (p + 1) * P)
                        own_v(ts(dab[:, c], gG[:, c], hc[:, 0, p:p + 1], 0.0, ALU.subtract, ALU.max))
                        own_v(ts(dab[:, 256 + p * P:256 + (p + 1) * P], gG[:, c], hc[:, 0, p:p + 1], 0.0, ALU.subtract, ALU.min))
                    ask(h, "decay", wait=False)
                    for p in range(2):
                        c = slice(p * P, (p + 1) * P)
                        own_v(ts(kbe[:, p, :], gT[:, c], hc[:, 2, p:p + 1], None, ALU.mult))
                        own_v(ts(kd[:, p, :], gT[:, c], hc[:, 3, p:p + 1], None, ALU.mult))
                        own_v(ts(vb[:, p, :], gT[:, 256 + p * P:256 + (p + 1) * P], hc[:, 1, p:p + 1], None, ALU.mult))
                    v.wait_ge(S("act_answered"), asked_of_act(h, "decay"))
                    for p in range(2):
                        c = slice(p * P, (p + 1) * P)
                        own_v(stt(out=lf[:, p, :], in0=gK[:, c], scalar=hc[:, 1, p:p + 1], in1=dab[:, c],
                                  op0=ALU.mult, op1=ALU.mult))
                    own_v(tt(qkt, gK[:, 256:512].rearrange("p (a b) -> p a b", a=2),
                             dab[:, 256:512].rearrange("p (a b) -> p a b", a=2), ALU.mult))
                    own_v(tt(qkt, qkt, two(M["incl"]), ALU.mult))
                    own_v(tt(qe, qkn[:, 0:SEQ], eg, ALU.mult))
                    own_v(tt(lm, lf, two(M["lv1"]), ALU.mult))
                    own_v(tt(xx[:, 0], two(M["ident"]), lm, ALU.subtract))
                    own_v(tt(lm, lf, two(M["lv2"]), ALU.mult))
                    st = gG[:, 256:272].rearrange("p (b c) -> p c b", c=2)
                    own_v(tt(s8[:, 3, :], st[:, 0, :], hg[:, 0, :], ALU.mult))
                    own_v(tt(s8[:, 3, :], y3[:, 2, SEQ:T], s8[:, 3, :], ALU.subtract))
                    own_v(tt(s8[:, 1, :], s8[:, 3, :], hg[:, 1, :], ALU.mult))
                    own_v(tt(s8[:, 4, :], st[:, 1, :], hg[:, 0, :], ALU.mult))
                    own_v(tt(s8[:, 5, :], s8[:, 2, :], s8[:, 1, :], ALU.mult))
                    own_v(tt(ob[:, SEQ:T], s8[:, 4, :], s8[:, 5, :], ALU.add))
                elif name == "xt":
                    own_v(cp(xx[:, 1], gT[:, 0:256].rearrange("p (a b) -> p a b", a=2)))
                    own_v(cp(knT[:, :], gG[0:DEC, 384:512]))
                    own_v(tt(vm, M["ident"][0:DEC, 0:DEC].unsqueeze(2).to_broadcast([DEC, DEC, P]), gT[0:DEC, 256:384].unsqueeze(1).to_broadcast([DEC, DEC, P]), ALU.mult))
                elif name == "outer":
                    own_v(tt(sst[:, :, :], sst[:, :, :], hg[:, 0, :].unsqueeze(2).to_broadcast([P, DEC, P]), ALU.mult))
                    for q, b in enumerate((gT, gO)):
                        own_v(tt(sst[:, 4 * q:4 * q + 4, :], sst[:, 4 * q:4 * q + 4, :],
                                 b[:, :].rearrange("p (a b) -> p a b", a=4), ALU.add))
                elif name[0] == "w":
                    own_v(cp(wt, gK[:, 0:256].rearrange("p (a b) -> p a b", a=2)))
                elif name[0] == "x":
                    n = int(name[1])
                    if n + 1 < len(LEVELS):
                        own_v(tt(lm, lf, two(M[f"lv{LEVELS[n + 1]}"]), ALU.mult))
                    flat = xx.rearrange("p x a b -> p (x a b)")
                    own_v(tt(flat, flat, gG[:, :], ALU.subtract))
                elif name == "uw":
                    own_v(ts(nwt, gK[:, 0:256], -1.0, None, ALU.mult))
                    v.wait_ge(S("prompt_state_out"), h * 16)
                    own_v(v.memset(St[:, :], 0.0))
                elif name[0] == "c":
                    c = int(name[1])
                    r0 = CHUNK * (c % 2)
                    if name[2] == "a":
                        own_v(cp(vn[r0:r0 + CHUNK, :], gT[r0:r0 + CHUNK, c * P:(c + 1) * P]))
                    else:
                        own_v(stt(out=St[:, :], in0=St[:, :], scalar=eg[:, (c + 1) * CHUNK - 1:(c + 1) * CHUNK],
                                  in1=gG[:, 0:P], op0=ALU.mult, op1=ALU.add))
                        if c == 3:
                            own_v(cp(ob[:, 0:SEQ], gO[:, 0:SEQ]))
                            own_v(tt(osq[:, :], ob[:, :], ob[:, :], ALU.mult))
                elif name == "ms":
                    ask(h, "rms")
                    own_v(stt(out=ob[:, :], in0=ob[:, :], scalar=gnorm[:, 0:1], in1=rms[:, :], op0=ALU.mult, op1=ALU.mult))
                    own_v(tt(ob[:, :], ob[:, :], zs[:, :], ALU.mult))
                    own_v(tt(gB[:, h, :], gB[:, h, :], ob[:, :], ALU.mult))
                elif name == "qk":
                    own_v(stt(out=sm[:, :], in0=aS[:, 0:3 * P], scalar=SCALE, in1=pbias[:, :], op0=ALU.mult, op1=ALU.add))
                    own_v(v.tensor_reduce(at_s[:, 0:1], sm[:, 0:P], AX.X, ALU.max))
                    own_v(v.tensor_reduce(at_s[:, 1:2], sm[:, P:3 * P], AX.X, ALU.max))
                    own_v(ts(at_s[:, 2:4], at_s[:, 0:2], -1.0, None, ALU.mult))
                    ask(h, "soft")
                    own_v(v.reciprocal(at_s[:, 4:6], at_s[:, 4:6]))
                    own_v(ts(sm[:, 0:P], sm[:, 0:P], at_s[:, 4:5], None, ALU.mult))
                    own_v(ts(sm[:, P:3 * P], sm[:, P:3 * P], at_s[:, 5:6], None, ALU.mult))
                elif name == "pt":
                    own_v(cp(pT[:, :], aS[:, 0:3 * P]))
                elif name == "pv":
                    own_v(tt(gA[:, h, 0:SEQ], gA[:, h, 0:SEQ], aS[:, 0:SEQ], ALU.mult))
                elif name == "v1":
                    own_v(cp(oS[:, h, :], aV[:, 0:NH]))
                v.sem_inc(S("answered"), 1)
                if name == "ms":
                    v.sem_inc(S("head_over"), 1)

            per = [0]

            def head(h):
                for name in DVE_STEPS:
                    step(h, name)

            with v.Fori(0, NH - 1) as h:
                own_v.enter(h, PER_HEAD)
                head(h)
            own_v.leave(NH - 1)
            head(NH - 1)
            pair = oS[:, :, :].rearrange("p (b u) n -> p b u n", u=2)
            own_v(tt(sn[:, :, :], pair[:, :, 0, :], pair[:, :, 1, :], ALU.add))
            for kv in range(NKV):
                g = slice(kv * GRP, (kv + 1) * GRP)
                own_v(tt(gmx[:, :, g], pn[:, :, g], vT[:, kv, SEQ:T].unsqueeze(2).to_broadcast([P, DEC, GRP]), ALU.mult))
            own_v(tt(sn[:, :, :], sn[:, :, :], gmx[:, :, :], ALU.add))
            own_v(tt(sn[:, :, :], sn[:, :, :], rin[:, :, :], ALU.mult))
            own_v(tt(gA[:, :, SEQ:T], gA[:, :, SEQ:T], sn[:, :, :].rearrange("p b n -> p n b"), ALU.mult))
            own_v(tt(gA, gA, gB, ALU.add))
            v.sem_inc(S("merged"), 1)
            residual(U_WO, 1, T_WO, 1)
            norm(1)
            products(U_UP2, KF)
            residual(U_DN2, 4, T_DN2, 2)
            norm(2)


PER_HEAD = 112
_OUTS = [("yT", (P, KD * T)), ("kT", (P, NKV * T)), ("vT", (P, NKV * T)), ("kiT", (IDXD, T)),
         ("ssm_p", (NH, P, P)), ("ssm_s", (NH, P, DEC, P)), ("convp", (P, NH * 9)), ("convs", (P, NH * 96))]


def lay_out(a):
    f = lambda n: np.asarray(a[n])
    x = np.concatenate([f("x_prompt")[0], f("x_sample")[:, 0]], 0)

    def units(w, nk):
        k, n = w.shape
        return w.reshape(k // P // nk, nk, P, n // P, P).transpose(3, 0, 2, 1, 4)

    def up(g, u):
        return np.stack([units(g, KD)[:, 0], units(u, KD)[:, 0]], 1).reshape(2 * KF, P, KD * P)

    def down(w):
        return np.ascontiguousarray(units(w, QD)).reshape(4 * KD, P, QD * P)

    w = f("w_in")[0]
    names = [("q", 2048), ("k", 512), ("v", 512), ("qi", 1024), ("ki", 64), ("wi", 16), ("qkv", 6144),
             ("a", 16), ("b", 16), ("z", 2048), ("ga", 2048), ("gb", 2048)]
    s, at = {}, 0
    for n, c in names:
        s[n] = w[:, at:at + c]
        at += c
    heads = []
    for h in range(NH):
        c = slice(h * P, (h + 1) * P)
        heads += [s["qkv"][:, 0:2048][:, c], s["qkv"][:, 2048:4096][:, c], s["qkv"][:, 4096:][:, c], s["z"][:, c]]
    pad = np.zeros((D, P - 112), np.float32)
    w_in = np.concatenate([s["ki"], s["wi"], s["a"], s["b"], pad, s["qi"], s["k"], s["v"], s["q"], s["ga"], s["gb"]] + heads, 1)
    cols = lambda m: np.ascontiguousarray(m.reshape(KD, P).T)
    place = lambda m: np.concatenate([np.zeros(R_A, np.float32), m, np.zeros(P - R_A - NH, np.float32)]).reshape(P, 1)
    conv = f("conv_w")[0].reshape(CONVW, 3, NH, P).transpose(3, 2, 1, 0)
    sconv = f("state_conv")[0].reshape(DEC, CONVW - 1, 3, NH, P).transpose(4, 3, 2, 1, 0)
    ki = f("cache_idx_k")[0].transpose(0, 2, 1)
    d = {
        "xT": x.T.reshape(KD, P, T).transpose(1, 0, 2).reshape(P, KD * T),
        "up1": up(f("ffn1_w_gate")[0], f("ffn1_w_up")[0]), "dn1": down(f("ffn1_w_down")[0]),
        "up2": up(f("ffn2_w_gate")[0], f("ffn2_w_up")[0]), "dn2": down(f("ffn2_w_down")[0]),
        "w_in": units(w_in, KD)[:, 0].reshape(-1, P, KD * P), "w_o": units(f("w_o")[0], KD)[:, 0].reshape(KD, P, KD * P),
        "cki": np.concatenate([ki, ki], 1), "ck": f("cache_k")[0].transpose(0, 3, 2, 1).reshape(-1, P, NKV * DH),
        "cv": f("cache_v")[0].reshape(-1, P, NKV * DH),
        "ssm": f("state_ssm")[0].transpose(1, 2, 0, 3),
        "lnp": np.stack([cols(f(n)[0]) for n in ("ln1_g", "ln1_b", "ln2_g", "ln2_b", "ln3_g", "ln3_b")], 1).reshape(P, -1),
        "cw": conv.reshape(P, -1), "convs": sconv.reshape(P, NH, 3, -1),
        "gnorm": f("gdn_norm_g")[0].reshape(P, 1), "alog": place(f("a_log")[0]), "dtb": place(f("dt_bias")[0]),
        "pt": f("page_table").reshape(1, -1),
    }
    d.update(host_constants())
    return {k: np.ascontiguousarray(m) for k, m in d.items()}


def kernel(**inputs):
    import concourse.bacc as bacc
    from concourse.bass_utils import run_bass_kernel_spmd

    nc = bacc.Bacc("TRN2", target_bir_lowering=False, num_devices=1)
    arrays = lay_out(inputs)
    din = {k: nc.dram_tensor(f"in_{k}", a.shape, mybir.dt.from_np(a.dtype), kind="ExternalInput").ap() for k, a in arrays.items()}
    dout = {k: nc.dram_tensor(f"out_{k}", s, F32, kind="ExternalOutput").ap() for k, s in _OUTS}
    build(nc, din, dout)
    r = run_bass_kernel_spmd(nc, [{f"in_{k}": a for k, a in arrays.items()}], core_ids=[0]).results[0]
    o = {k: np.asarray(r[f"out_{k}"]) for k, _ in _OUTS}
    y = o["yT"].reshape(P, KD, T).transpose(2, 1, 0).reshape(T, D)
    kv = {k: o[k].reshape(P, NKV, T).transpose(2, 1, 0) for k in ("kT", "vT")}
    ki = o["kiT"].T
    ssm_s = o["ssm_s"].transpose(2, 0, 1, 3)
    convp = o["convp"].reshape(P, NH, 3, CONVW - 1).transpose(3, 2, 1, 0).reshape(CONVW - 1, -1)
    convs = o["convs"].reshape(P, NH, 3, CONVW, DEC)[:, :, :, 1:].transpose(4, 3, 2, 1, 0).reshape(DEC, CONVW - 1, -1)
    c = np.ascontiguousarray
    return (c(y[None, :SEQ]), c(y[SEQ:, None]),
            c(kv["kT"][None, None, :SEQ]), c(kv["vT"][None, None, :SEQ]), c(ki[None, None, :SEQ]),
            c(o["ssm_p"][None, None]), c(convp[None, None]),
            c(kv["kT"][None, SEQ:, None]), c(kv["vT"][None, SEQ:, None]), c(ki[None, SEQ:, None]),
            c(ssm_s[None]), c(convs[None]))
```

```python
from contextlib import ExitStack

import numpy as np
import concourse.bass as bass
from concourse import mybir

F32 = mybir.dt.float32
I32 = mybir.dt.int32
ALU = mybir.AluOpType
ACT = mybir.ActivationFunctionType
AX = mybir.AxisListType

P = 128
D, SEQ, DEC, PAST, PAGE = 2048, 256, 8, 2048, 128
T = SEQ + DEC
NH, NKV, DH = 16, 4, 128
GRP = NH // NKV
IDXH, IDXD = 16, 64
DFF, CHUNK, CONVW = 5632, 64, 4
KD, KF = D // P, DFF // P
PAGES = PAST // PAGE
TOPK_P, TOPK_S = min(256, SEQ // 4), min(256, (PAST + 1) // 4)
THETA = 500000.0
ALPHA = 2.0 ** 0.25
SCALE = DH ** -0.5
LN_EPS, NORM_EPS = 1e-5, 1e-6
RING, CRING, AHEAD = 4, 2, 2
QD = KF // 4
U_UP1 = 0
U_DN1 = U_UP1 + 2 * KF
U_MISC = U_DN1 + 4 * KD
U_IDXQ = U_MISC + 1
U_K = U_IDXQ + 8
U_V = U_K + 4
U_Q = U_V + 4
U_GATE = U_Q + NH
U_HEAD = U_GATE + 2 * KD
U_WO = U_HEAD + 4 * NH
U_UP2 = U_WO + KD
U_DN2 = U_UP2 + 2 * KF
T_DN1 = 0
T_MISC = T_DN1 + KD
T_IDXQ = T_MISC + 1
T_K = T_IDXQ + 8
T_V = T_K + 4
T_Q = T_V + 4
T_GATE = T_Q + NH
T_HEAD = T_GATE + 2 * KD
T_WO = T_HEAD + 4 * NH
T_DN2 = T_WO + KD
R_W, R_A, R_B = IDXD, IDXD + IDXH, IDXD + IDXH + NH
C_KI, C_K, C_V = 0, DEC, DEC + 4 * DEC
NEG, GONE = -1e38, -3e38
OFF = 1e30
LEVELS = (2, 4, 8, 16, 32)

TURN = ("mix P P P P P P xt mix2 V w0 P x0 vm V P e0 w1 qk P x1 lift V P w2 soft P outer x2 share P V w3 pt P "
        "x3 added P w4 pv P x4 conv0a P P e1 uw conv0b V c0a P sig0 P c0b silu0 P conv1a c1a P c1b conv1b V P c2a P "
        "sig1 P e2 c2b silu1 V c3a conv2a P c3b conv2b P ss V vout sig2 P ms P norm P P P P e3 sig3 gated").split()
NEXT = {"P", "ss", "norm", *[f"{e}{j}" for e in ("e", "sig") for j in range(4)], "silu0", "silu1",
        *[f"conv{j}{c}" for j in range(3) for c in "ab"]}
LAST_TURN = [e for e in TURN if e not in NEXT]
FIRST = ("e0 e1 e2 conv0a conv0b sig0 silu0 conv1a conv1b e3 sig1 silu1 conv2a conv2b ss sig2 sig3 "
         "norm").split()
assert TURN.count("P") == 2 * KD and TURN.count("V") == 8
SOLVE_W, SOLVE_X = [f"w{n}" for n in range(5)], [f"x{n}" for n in range(5)]
CHUNKS_A, CHUNKS_B = [f"c{n}a" for n in range(4)], [f"c{n}b" for n in range(4)]


def in_turn(*names):
    return [e for e in TURN if e in names]


BY_PE = in_turn("mix", "qk", "xt", "outer", "pt", "pv", "uw", "ms", *SOLVE_W, *SOLVE_X, *CHUNKS_A, *CHUNKS_B)
BY_DVE = in_turn("mix", "mix2", "share", "added", "pv", "vout", "uw", "gated", *SOLVE_X, *CHUNKS_B)
BY_ACT = ["eg", "ktok", "decay"] + in_turn("soft", "pt", "xt", "uw", "c3b", "ms", *SOLVE_W, *CHUNKS_A)
ASKS = ["decay", "soft"]
ASKS_NEXT = ["conv0", "conv1", "conv2"]
DONE_NEXT = in_turn("sig0", "sig1", "sig2", "ss")


def count(names, name, h):
    return h * len(names) + (names.index(name) + 1)


CONSTS = ["ident", "ones", "lv1", "lv2", "lv4", "lv8", "lv16", "lv32", "incl"]
EARLY = ["cumul", "whole", "dup", "rotdup", "roth", "roti", "spread"]


def host_constants():
    i, j = np.meshgrid(np.arange(P), np.arange(P), indexing="ij")
    same = (i // CHUNK) == (j // CHUNK)
    m = {"ident": i == j, "ones": i >= 0}
    for lv in (1, 2, 4, 8, 16, 32):
        m[f"lv{lv}"] = (i // (2 * lv) == j // (2 * lv)) & (i // lv % 2 == 1) & (j // lv % 2 == 0)
    m["incl"] = same & (j >= i)
    m["cumul"] = same & (i <= j)
    m["whole"] = same
    m["dup"] = (i < IDXD) & (j % IDXD == i)
    m["spread"] = i == R_W + j % IDXH
    m = {k: v.astype(np.float32) for k, v in m.items()}

    def rot(dim, half):
        r = np.zeros((P, P), np.float32)
        for b in range(0, P, dim):
            for k in range(half):
                r[b + half + k, b + k] = -1.0
                r[b + k, b + half + k] = 1.0
        return r

    m["roth"], m["roti"] = rot(DH, DH // 8), rot(IDXD, IDXD // 8)
    m["rotdup"] = m["dup"] @ m["roti"]
    mats = np.stack([m[k] for k in CONSTS], 1)
    early = np.stack([m[k] for k in EARLY], 1)
    pos = np.concatenate([np.arange(SEQ), np.full(DEC, PAST)]).astype(np.float32)

    def tables(dim, half):
        inv = (np.float32(THETA) ** (-np.arange(half, dtype=np.float32) / half)).astype(np.float32)
        ang = pos[None, :] * inv[:, None]
        c, s = np.ones((P, T), np.float32), np.zeros((P, T), np.float32)
        for b in range(0, P, dim):
            for o in (0, half):
                c[b + o:b + o + half] = np.cos(ang)
                s[b + o:b + o + half] = np.sin(ang)
        return c, s

    rope = np.stack([*tables(DH, DH // 8), *tables(IDXD, IDXD // 8)], 1)
    t = np.arange(P)[:, None]
    caus = np.concatenate([t >= np.arange(P)[None], t + P >= np.arange(2 * P)[None]], 1).astype(np.float32)
    own = (np.arange(P)[:, None] // IDXH == np.arange(DEC)[None]).astype(np.float32)
    rowm = np.zeros((P, 3), np.float32)
    rowm[R_W:R_W + IDXH, 0] = (IDXH ** -0.5) * (IDXD ** -0.5)
    rowm[R_A:R_A + NH, 1] = 1.0
    rowm[R_B:R_B + NH, 2] = 1.0
    eps = np.tile(np.array([[LN_EPS, NORM_EPS]], np.float32), (P, 1))
    return {"c_mats": mats.reshape(P, -1), "c_early": early.reshape(P, -1), "c_rope": rope.reshape(P, -1), "c_caus": caus,
            "c_own": own, "c_rowm": rowm, "c_eps": eps}


def build(nc, din, dout):
    with ExitStack() as ctx:
        def sb(name, shape, dt=F32):
            return ctx.enter_context(nc.sbuf_tensor(name, shape, dt))

        sems = {}

        def S(name):
            if name not in sems:
                sems[name] = ctx.enter_context(nc.semaphore(name))
            return sems[name]

        wring = sb("wring", [P, RING, KD * P])
        cring = sb("cring", [P, CRING, KD * P])
        xT = sb("xT", [P, KD, T])
        big = sb("big", [P, KF * T])
        gates = sb("gates", [P, 2, KD, T])
        gA, gB = gates[:, 0], gates[:, 1]
        hT = big[:, :].rearrange("p (k t) -> p k t", k=KF)
        at = [0]

        def part(n):
            a = big[:, at[0]:at[0] + n]
            at[0] += n
            return a

        qT = part(NH * T).rearrange("p (h t) -> p h t", h=NH)
        kT = part(NKV * T).rearrange("p (h t) -> p h t", h=NKV)
        vT = part(NKV * T).rearrange("p (h t) -> p h t", h=NKV)
        vtok = part(2 * NKV * DH).rearrange("p (s d) -> p s d", s=2)
        low = at[0]
        qiT = part(8 * T).rearrange("p (j t) -> p j t", j=8)
        zq = part(DEC * P).rearrange("p (b c) -> p b c", b=DEC)
        assert at[0] <= KF * T
        at[0] = low
        y3 = part(3 * T).rearrange("p (j t) -> p j t", j=3)
        e4 = part(4 * T).rearrange("p (j t) -> p j t", j=4)
        sq = part(2 * SEQ + 24)
        rs = part(2 * SEQ + 16)
        dab = part(4 * P)
        oS = part(NH * NH).rearrange("p (u n) -> p u n", u=NH)
        sgs = part(2 * NH * DEC).rearrange("p (k h b) -> p k h b", k=2, h=NH)
        pn, rin = (part(DEC * NH).rearrange("p (b n) -> p b n", b=DEC) for _ in range(2))
        assert at[0] <= KF * T, at[0]
        pool = sb("pool", [P, 2 * (PAST + 8)])
        rl = pool[:, 0:PAST + 1]
        scS = pool[0:DEC, PAST + 8:2 * PAST + 9]
        at2 = [0]

        def part2(n):
            a = pool[:, at2[0]:at2[0] + n]
            at2[0] += n
            return a

        qkn = part2(2 * SEQ)
        kbe, kd, vb = (part2(2 * P).rearrange("p (a b) -> p a b", a=2) for _ in range(3))
        lf, lm0, lm1, qkt, wt = (part2(2 * P).rearrange("p (a b) -> p a b", a=2) for _ in range(5))
        lm = (lm0, lm1)
        xx = part2(4 * P).rearrange("p (x a b) -> p x a b", x=2, a=2)
        eg, qe, nwt = part2(2 * P), part2(2 * P), part2(2 * P)
        assert at2[0] <= 2 * (PAST + 8), at2[0]
        knT = part2(P)[0:DEC]
        turn = sb("turn", [P, 2608])
        at3 = [0]

        def part3(n):
            a = turn[:, at3[0]:at3[0] + n]
            at3[0] += n
            return a

        rope = part3(4 * T).rearrange("p (a t) -> p a t", a=4)
        caus, pscore = part3(3 * P), part3(3 * P)
        msc, val = part3(T), part3(T)
        valk = part3(2 * P).rearrange("p (a b) -> p a b", a=2)
        assert at3[0] == 2608
        at3[0] = 0
        dg, vh = (part3(2 * P).rearrange("p (a b) -> p a b", a=2) for _ in range(2))
        qh, sm, pT = part3(2 * P), part3(3 * P), part3(3 * P)
        vn, St = part3(P), part3(P)
        ob, zs, osq = part3(T), part3(T), part3(T)
        assert at3[0] <= 2608
        rms, zraw = sb("rms", [P, T]), sb("zraw", [P, T])
        raw = sb("raw", [P, 3, SEQ + CONVW - 1])
        sst = sb("sst", [P, DEC, P])
        early = sst[:, 0:len(EARLY), :]
        vm = e4.rearrange("p j t -> p (j t)")[0:DEC, 0:DEC * P].rearrange("p (b e) -> p b e", b=DEC)
        sal = sb("sal", [P, 4 * DEC, 4, NH])
        mats = sb("mats", [P, len(CONSTS), P])
        M = {k: mats[:, n, :] for n, k in enumerate(CONSTS)}
        M.update({k: early[:, n, :] for n, k in enumerate(EARLY)})
        own, rowm, epsc = sb("own", [P, DEC]), sb("rowm", [P, 3]), sb("epsc", [P, 2])
        lnp = sb("lnp", [P, 6, KD])
        cw = sb("cw", [P, NH, 12])
        cs = sb("cs", [P, NH, 3, CONVW, DEC])
        cpb = sb("cpb", [P, NH, 3, CONVW - 1])
        gnorm, alog, dtb = sb("gnorm", [P, 1]), sb("alog", [P, 1]), sb("dtb", [P, 1])
        pt = sb("pt", [1, DEC * PAGES], I32)
        raw2 = sb("raw2", [P, 2, T])
        tmp = sb("tmp", [P, T])
        kiT = sb("kiT", [P, T])
        gsc = sb("gsc", [P, NH, 4, 2])
        w8 = sb("w8", [P, DEC])
        pbias = sb("pbias", [P, 3 * P])
        top8 = sb("top8", [P, 8])
        mbt = sb("mbt", [P, DEC, PAGES])
        nbt = sb("nbt", [P, DEC])
        sn, gmx = (sb(n, [P, DEC, NH]) for n in ("sn", "gmx"))
        hc, hw = sb("hc", [P, 4, 2]), sb("hw", [P, 12])
        hg = sb("hg", [P, 2, DEC])
        kq = sb("kq", [P, 2, DEC])
        s8 = sb("s8", [P, 6, DEC])
        at_s = sb("at_s", [P, 6])
        mean, rstd = tmp, rms
        sqr = gates[:, 0]
        bank = [ctx.enter_context(nc.psum_tensor(f"bank{i}", [P, 512], F32)) for i in range(8)]
        acc = bank[0:2]
        gT, gK, gG, gO, aS, aV = bank[2:8]
        upb = [(bank[0], bank[1]), (bank[2], bank[3])]
        sg = raw2

        ki_dram = nc.dram_tensor("ki_ordered", (DEC, P, PAST), F32, kind="Internal").ap()

        block = ctx.enter_context(nc.Block())

        class Own:

            def __init__(self, eng, sem):
                self.eng, self.sem, self.base, self.k, self.it, self.per = eng, sem, 0, 0, 0, 0

            def __call__(self, ins, lag=0):
                ins.then_inc(self.sem, 1)
                self.k += 1
                self.eng.wait_ge(self.sem, self.it * self.per + (self.base + self.k - lag))

            def enter(self, it, per):
                self.base, self.k, self.it, self.per = self.base + self.k, 0, it, per

            def leave(self, n):
                assert self.k == self.per, (self.k, self.per)
                self.base, self.k, self.it, self.per = self.base + n * self.per, 0, 0, 0

        def unit_done(eng, n, it=0, per=0):
            eng.wait_ge(S("units_done"), it * per + (n + 1))

        def landed(eng, n0, it=0, per=4):
            eng.wait_ge(S(f"weights_in{n0 % RING}"), (it * (per // RING) + (n0 // RING + 1)) * 16)

        def multiplied(eng, h, name):
            eng.wait_ge(S("multiplied"), count(BY_PE, name, h))

        def answered(eng, h, name):
            eng.wait_ge(S("answered"), count(BY_DVE, name, h))

        def act_done(eng, h, name):
            eng.wait_ge(S("act_done"), count(BY_ACT, name, h))

        def act_done_next(eng, g, name):
            eng.wait_ge(S("act_done_next"), count(DONE_NEXT, name, g))

        def pages_landed(eng, c0, it=0, per=2, dmas=4):
            n = c0 // CRING + 1
            ki = DEC // CRING
            eng.wait_ge(S(f"pages_in{c0 % CRING}"),
                        (it * (per // CRING) * dmas + (n if c0 < C_K else ki + (n - ki) * dmas)) * 16)

        @block.sync
        def _(sp):
            small = [(mats[:, :, :], "c_mats"), (early, "c_early"), (rope, "c_rope"), (caus, "c_caus"),
                     (own[:, :], "c_own"), (rowm[:, :], "c_rowm"), (epsc[:, :], "c_eps"),
                     (lnp[:, :, :], "lnp"), (cw[:, :, :], "cw"),
                     (gnorm[:, :], "gnorm"), (alog[:, :], "alog"), (dtb[:, :], "dtb")]

            def weights(n0, u, it, per, src, w=KD * P):
                if n0 + u >= RING:
                    sp.wait_ge(S("units_done"), it * per + (n0 + u + 1 - RING))
                sp.dma_start(wring[:, (n0 + u) % RING, 0:w], src).then_inc(S(f"weights_in{(n0 + u) % RING}"), 16)

            sp.dma_start(xT[:, :, :], din["xT"].rearrange("p (k t) -> p k t", k=KD)).then_inc(S("x_in"), 16)
            sp.dma_start(mats[:, :, :], din["c_mats"].rearrange("p (k t) -> p k t", k=len(CONSTS))).then_inc(S("small_in"), 16)

            def ffn_loads(n_up, n_dn, up, dn):
                with sp.Fori(0, 2 * KF // 4) as i:
                    for u in range(4):
                        weights(n_up, u, i, 4, up[i * 4 + u])
                with sp.Fori(0, KD // 2) as i:
                    for u in range(8):
                        weights(n_dn, u, i, 8, dn[i * 8 + u], QD * P)

            for u in range(4):
                weights(U_UP1, u, 0, 4, din["up1"][u])
            for dst, name in small[1:]:
                s = din[name]
                if len(dst.shape) == 3:
                    s = s.rearrange("p (a b) -> p a b", a=dst.shape[1])
                sp.dma_start(dst, s).then_inc(S("small_in"), 16)
            for h in range(NH):
                sp.dma_start(cs[:, h, :, 0:CONVW - 1, :],
                             din["convs"][:, h].rearrange("p j (t b) -> p j t b", b=DEC)).then_inc(S("small_in"), 16)
            sp.dma_start(pt[:, :], din["pt"]).then_inc(S("table_in"), 16)
            with sp.Fori(0, 2 * KF // 4 - 1) as i:
                for u in range(4):
                    weights(U_UP1 + 4, u, i, 4, din["up1"][i * 4 + (u + 4)])
            with sp.Fori(0, KD // 2) as i:
                for u in range(8):
                    weights(U_DN1, u, i, 8, din["dn1"][i * 8 + u], QD * P)

            w_in = din["w_in"]

            def pages(c0, it, per, first, dmas, cache, width):
                if c0 >= CRING:
                    sp.wait_ge(S("page_units_done"), it * per + (c0 + 1 - CRING))
                for g in range(dmas):
                    page = sp.value_load(pt[0:1, bass.ds(first + g, 1)], min_val=0, max_val=cache.shape[0] - 1)
                    sp.dma_start(cring[:, c0 % CRING, g * width:(g + 1) * width], cache[page]).then_inc(
                        S(f"pages_in{c0 % CRING}"), 16)

            weights(U_MISC, 0, 0, 0, w_in[0])
            with sp.Fori(0, 2) as i:
                for u in range(4):
                    weights(U_IDXQ, u, i, 4, w_in[i * 4 + (U_IDXQ - U_MISC + u)])
            sp.wait_ge(S("table_in"), 16)
            sp.wait_ge(S("keys_ordered"), DEC * PAGES * 16)
            for b in range(DEC):
                if b >= CRING:
                    sp.wait_ge(S("page_units_done"), b + 1 - CRING)
                sp.dma_start(cring[:, b % CRING, :], ki_dram[b]).then_inc(S(f"pages_in{b % CRING}"), 16)
            with sp.Fori(0, (2 * NKV + NH) // 4) as i:
                for u in range(4):
                    weights(U_K, u, i, 4, w_in[i * 4 + (U_K - U_MISC + u)])
            sp.wait_ge(S("kv_ready"), 3)
            sp.dma_start(dout["kT"].rearrange("p (a b) -> p a b", a=NKV), kT).then_inc(S("stored"), 16)
            sp.dma_start(dout["vT"].rearrange("p (a b) -> p a b", a=NKV), vT).then_inc(S("stored"), 16)
            sp.dma_start(dout["kiT"], kiT[0:IDXD, :]).then_inc(S("stored"), 16)
            for u in range(AHEAD):
                weights(U_GATE, u, 0, 0, w_in[U_GATE - U_MISC + u])
            with sp.Fori(0, DEC) as i:
                for u in range(4):
                    weights(U_GATE + AHEAD, u, i, 4, w_in[i * 4 + (U_GATE + AHEAD - U_MISC + u)])
                    pages(C_K + u, i, 4, i * PAGES + 4 * u, 4, din["ck"], NKV * DH)
            for u in range(AHEAD, 4):
                weights(U_HEAD, u, 0, 0, w_in[U_HEAD - U_MISC + u])
            for u in range(AHEAD):
                weights(U_HEAD + 4, u, 0, 0, w_in[U_HEAD + 4 - U_MISC + u])
            with sp.Fori(0, NH - 2) as i:
                for u in range(4):
                    weights(U_HEAD + 4 + AHEAD, u, i, 4, w_in[i * 4 + (U_HEAD + 4 + AHEAD - U_MISC + u)])
                    if u % 2 == 0:
                        pages(C_V + u // 2, i, 2, i * 8 + 4 * (u // 2), 4, din["cv"], NKV * DH)
            for u in range(AHEAD, 4):
                weights(U_HEAD + 4 * (NH - 1), u, 0, 0, w_in[U_HEAD + 4 * (NH - 1) - U_MISC + u])
                pages(C_V + 2 * (NH - 2) + u - AHEAD, 0, 0, 4 * (2 * (NH - 2) + u - AHEAD), 4, din["cv"], NKV * DH)
            for c in range(2 * (NH - 1), 2 * NH):
                pages(C_V + c, 0, 0, 4 * c, 4, din["cv"], NKV * DH)
            with sp.Fori(0, KD // 4) as i:
                for u in range(4):
                    weights(U_WO, u, i, 4, din["w_o"][i * 4 + u])
            ffn_loads(U_UP2, U_DN2, din["up2"], din["dn2"])
            sp.wait_ge(S("head_over"), NH)
            sp.dma_start(dout["convp"], cpb[:, :, :, :].rearrange("p h j t -> p (h j t)")).then_inc(S("stored"), 16)
            sp.dma_start(dout["convs"], cs[:, :, :, :, :].rearrange("p h j t b -> p (h j t b)")).then_inc(S("stored"), 16)
            for k in range(KD):
                sp.wait_ge(S("y_out_ready"), k + 1)
                sp.dma_start(dout["yT"][:, k * T:(k + 1) * T], xT[:, k, :]).then_inc(S("stored"), 16)
            sp.wait_ge(S("stored"), (5 + KD) * 16)

        @block.gpsimd
        def _(pool_e):
            def state_in(h, n):
                pool_e.dma_start(sst[:, :, :], din["ssm"][h]).then_inc(S("state_in"), 16)

            def state_steps(h, more):
                multiplied(pool_e, h, "mix")
                pool_e.tensor_tensor(sst[:, :, :], sst[:, :, :], hg[:, 0, :].unsqueeze(2).to_broadcast([P, DEC, P]),
                                     ALU.mult).then_inc(S("state_scaled"), 1)
                answered(pool_e, h, "added")
                pool_e.dma_start(dout["ssm_s"][h], sst[:, :, :]).then_inc(S("state_out"), 16)
                pool_e.wait_ge(S("state_out"), h * 16 + 16)
                if more:
                    state_in(h + 1, 0)
                answered(pool_e, h, "c3b")
                pool_e.dma_start(dout["ssm_p"][h], St[:, :]).then_inc(S("prompt_state_out"), 16)
                pool_e.wait_ge(S("prompt_state_out"), h * 16 + 16)
                pool_e.sem_inc(S("prompt_state_free"), 1)

            pool_e.sem_inc(S("prompt_state_free"), 1)
            pool_e.wait_ge(S("table_in"), 16)
            with pool_e.Fori(0, DEC) as b:
                for g in range(PAGES):
                    page = pool_e.value_load(pt[0:1, bass.ds(b * PAGES + g, 1)], min_val=0, max_val=din["cki"].shape[0] - 1)
                    pool_e.dma_start(ki_dram[b, :, g * PAGE:(g + 1) * PAGE], din["cki"][page]).then_inc(S("keys_ordered"), 16)
            pool_e.wait_ge(S("part_max"), 1)
            pool_e.partition_all_reduce(gmx[:, :, :].rearrange("p b n -> p (b n)"),
                                        gmx[:, :, :].rearrange("p b n -> p (b n)"), P,
                                        bass.bass_isa.ReduceOp.max).then_inc(S("all_max"), 1)
            state_in(0, 0)
            with pool_e.Fori(0, NH - 1) as h:
                state_steps(h, True)
            state_steps(NH - 1, False)

        @block.tensor
        def _(pe):
            mm = pe.matmul
            pe.wait_ge(S("x_in"), 16)

            def unit(n0, u, it, per, rhs, out, nk=KD, first=True, last=True, lo=0, hi=None):
                slot = (n0 + u) % RING
                hi = nk if hi is None else hi
                if lo == 0:
                    landed(pe, n0 + u, it, per)
                for k in range(lo, hi):
                    ins = mm(out, wring[:, slot, k * P:(k + 1) * P], rhs(k),
                             start=first and k == 0, stop=last and k == nk - 1)
                if hi == nk:
                    ins.then_inc(S("units_done"), 1)

            def tile(n0, t0, u, it, per, rhs, lo=0, hi=KD):
                a = acc[(t0 + u) % 2]
                if lo == 0:
                    pe.wait_ge(S("acc_free"), it * per + (t0 + u + 1))
                unit(n0, u, it, per, rhs, a[:, 0:T], lo=lo, hi=hi)

            def ffn_up(n_up, base):
                with pe.Fori(0, KF // 2) as i:
                    for f in range(2):
                        g, up = upb[f]
                        pe.wait_ge(S("pair_free"), i * 2 + (base + f + 1))
                        unit(n_up, 2 * f, i, 4, lambda k: xT[:, k, :], g[:, 0:T])
                        unit(n_up, 2 * f + 1, i, 4, lambda k: xT[:, k, :], up[:, 0:T])

            def ffn_down(n_dn, t0, base):
                pe.wait_ge(S("pair_free"), base + KF + 2)
                with pe.Fori(0, KD // 2) as i:
                    for c in range(2):
                        pe.wait_ge(S("acc_free"), i * 2 + (t0 + c + 1))
                        for q in range(4):
                            unit(n_dn, 4 * c + q, i, 8, lambda k, q=q: hT[:, QD * q + k, :],
                                 acc[(t0 + c) % 2][:, 0:T], nk=QD, first=q == 0, last=q == 3)

            def norm(n):
                pe.wait_ge(S("y_ready"), (n + 1) * KD)
                for k in range(KD):
                    ins = mm(gG[:, 0:T], M["ones"], xT[:, k, :], start=k == 0, stop=k == KD - 1)
                ins.then_inc(S("stat"), 1)
                for k in range(KD):
                    if k % 4 == 0:
                        pe.wait_ge(S("squares"), 4 * n + k // 4 + 1)
                    ins = mm(gO[:, 0:T], M["ones"], sqr[:, k, :], start=k == 0, stop=k == KD - 1)
                ins.then_inc(S("stat"), 1)
                pe.wait_ge(S("x_ready"), (n + 1) * KD)

            ffn_up(U_UP1, 0)
            ffn_down(U_DN1, T_DN1, 0)
            pe.wait_ge(S("small_in"), 16 * 28)
            norm(0)

            x = lambda k: xT[:, k, :]
            tile(U_MISC, T_MISC, 0, 0, 0, x)
            pe.wait_ge(S("misc_raw"), 1)
            mm(gT[:, 0:T], M["dup"], msc[:, :], start=True, stop=True)
            mm(gK[:, 0:T], M["rotdup"], msc[:, :], start=True, stop=True).then_inc(S("ki_rot"), 1)

            def rotate(r, it, m):
                pe.wait_ge(S("raw_ready"), it + (r + 1))
                pe.wait_ge(S("rope_free"), it + (r + 1))
                mm([gT, gK][r % 2][:, 0:T], m, raw2[:, r % 2, :], start=True, stop=True).then_inc(S("rotated"), 1)

            pe.wait_ge(S("ki_ready"), 1)
            with pe.Fori(0, 2) as i:
                for u in range(4):
                    tile(U_IDXQ, T_IDXQ, u, i, 4, x)
                    if u:
                        rotate(u - 1, i * 4, M["roti"])
                rotate(3, i * 4, M["roti"])
            pe.wait_ge(S("val_ready"), 1)
            for t in range(2):
                ins = pe.transpose(gG[:, t * P:(t + 1) * P], val[:, t * P:(t + 1) * P], M["ident"])
            ins.then_inc(S("val_turned"), 1)
            pe.wait_ge(S("picked"), 1)
            mm(gO[:, 0:2 * NH * DEC], M["ones"], rms[:, 0:2 * NH * DEC], start=True, stop=True)
            mm(gO[:, 256:256 + DEC], M["spread"], val[:, SEQ:T], start=True, stop=True).then_inc(S("rows_done"), 1)
            pe.wait_ge(S("valk_ready"), 1)
            pe.wait_ge(S("rope_free"), 2 + 8)
            for t in range(2):
                mm(gK[:, 32 * t:32 * t + 16], M["cumul"], valk[:, t, R_A:R_A + NH], start=True, stop=True)
                ins = mm(gK[:, 32 * t + 16:32 * t + 32], M["whole"], valk[:, t, R_A:R_A + NH], start=True, stop=True)
            ins.then_inc(S("decays"), 1)
            n = 0
            for h in range(IDXH):
                for t in range(2):
                    a, w = [aS, aV][n % 2], (t + 1) * P
                    r0 = IDXD * (h % 2)
                    pe.wait_ge(S("pidx_free"), n + 1)
                    mm(a[:, 0:w], qiT[r0:r0 + IDXD, h // 2, t * P:(t + 1) * P], kiT[r0:r0 + IDXD, 0:w],
                       start=True, stop=True).then_inc(S("pidx_done"), 1)
                    n += 1
            idx = [gT, gK, gG, gO]
            pe.wait_ge(S("zq_ready"), 1)
            pe.wait_ge(S("decays_read"), 1)
            pe.wait_ge(S("pidx_free"), 2 + 32)
            for b in range(DEC):
                pages_landed(pe, C_KI + b)
                for c in range(4):
                    mm(idx[c][:, :], zq[:, b, :], cring[:, b % CRING, c * 512:(c + 1) * 512],
                       start=b == 0, stop=b == DEC - 1)
                ins = mm(aS[:, 0:1], zq[:, b, :], kiT[:, SEQ + b:SEQ + b + 1], start=b == 0, stop=b == DEC - 1)
                ins.then_inc(S("page_units_done"), 1)
            for c in range(4):
                pe.wait_ge(S("rectified"), c + 1)
                mm(idx[c][0:DEC, :], w8[:, :], rl[:, c * 512:(c + 1) * 512], start=True, stop=True).then_inc(S("weighed"), 1)
            pe.wait_ge(S("rectified"), 5)
            mm(aS[0:DEC, 0:1], w8[:, :], rl[:, PAST:PAST + 1], start=True, stop=True).then_inc(S("weighed"), 1)
            pe.wait_ge(S("scored"), 5)
            for u in range(4):
                tile(U_K, T_K, u, 0, 0, x)
                if u:
                    rotate(8 + u - 1, 0, M["roth"])
            rotate(11, 0, M["roth"])
            for u in range(4):
                tile(U_V, T_V, u, 0, 0, x)
                pe.wait_ge(S("v_raw"), u + 1)
                for t in range(2):
                    ins = pe.transpose([gG, gO][t][:, u * P:(u + 1) * P], vT[:, u, t * P:(t + 1) * P], M["ident"])
            ins.then_inc(S("v_turned"), 1)
            with pe.Fori(0, 4) as i:
                for u in range(4):
                    tile(U_Q, T_Q, u, i, 4, x)
                    if u:
                        rotate(12 + u - 1, i * 4, M["roth"])
                rotate(15, i * 4, M["roth"])
            pe.wait_ge(S("rope_free"), 2 + 28)
            with pe.Fori(0, DEC) as i:
                for u in range(4):
                    tile(U_GATE, T_GATE, u, i, 4, x)
                    pages_landed(pe, C_K + u, i, 4)
                    pe.wait_ge(S("kscore_free"), i * 4 + (u + 1))
                    for g in range(4):
                        for kv in range(NKV):
                            o = g * NH + kv * GRP
                            ins = mm([aS, aV][u % 2][:, o:o + GRP],
                                     cring[:, u % CRING, (g * NKV + kv) * P:(g * NKV + kv + 1) * P],
                                     qT[:, kv * GRP:(kv + 1) * GRP, bass.ds(i + SEQ, 1)], start=True, stop=True)
                    ins.then_inc(S("page_units_done"), 1)
            pe.wait_ge(S("selected"), 1)
            for g in range(PAGES):
                ins = pe.transpose(gT[:, g * DEC:(g + 1) * DEC], scS[:, g * PAGE:(g + 1) * PAGE], M["ident"][0:DEC, 0:DEC])
            mm(gK[:, 0:DEC], M["ones"][0:DEC, :], s8[0:DEC, 0, :], start=True, stop=True)
            ins = mm(gG[:, 0:DEC * NH], M["ones"], sn[:, :, :].rearrange("p b n -> p (b n)"), start=True, stop=True)
            ins.then_inc(S("masks_turned"), 1)
            for u in range(4):
                tile(U_HEAD, T_HEAD, u, 0, 0, x)
            pe.wait_ge(S("expsum"), 1)
            mm(gG[:, 0:DEC * NH], M["ones"], rin[:, :, :].rearrange("p b n -> p (b n)"),
               start=True, stop=True).then_inc(S("denoms"), 1)

            def norms(g):
                pe.wait_ge(S("squared"), g + 1)
                mm(gT[:, :], M["ones"], sq[:, 0:2 * SEQ], start=True, stop=True)
                mm(aS[:, 0:24], M["ones"], sq[:, 2 * SEQ:2 * SEQ + 24], start=True, stop=True).then_inc(S("summed"), 1)

            def step(h, e, v=0):
                if e == "mix":
                    pe.wait_ge(S("normalized"), h + 1)
                    pe.wait_ge(S("state_in"), h * 16 + 16)
                    mm(gG[:, 0:2 * P], M["ones"], dg.rearrange("p a b -> p (a b)"), start=True, stop=True)
                    for b in range(DEC):
                        mm(gG[:, 256 + 2 * b:258 + 2 * b], sst[:, b, :], kq[:, :, b], start=True, stop=True)
                    pe.transpose(gG[0:DEC, 384:512], kq[:, 0, :], M["ident"])
                    for p in range(2):
                        c = slice(p * P, (p + 1) * P)
                        pe.transpose(gT[:, c], qkn[:, SEQ + p * P:SEQ + (p + 1) * P], M["ident"])
                        pe.transpose(gT[:, SEQ + p * P:SEQ + (p + 1) * P], y3[:, 2, c], M["ident"])
                    for p in range(2):
                        kn = qkn[:, SEQ + p * P:SEQ + (p + 1) * P]
                        mm(gK[:, p * P:(p + 1) * P], kn, kn, start=True, stop=True)
                        ins = mm(gK[:, SEQ + p * P:SEQ + (p + 1) * P], kn, qkn[:, p * P:(p + 1) * P], start=True, stop=True)
                elif e == "qk":
                    pe.wait_ge(S("head_copied"), h + 1)
                    mm(aS[:, 0:P], qh[:, 0:P], kT[:, h // GRP, 0:P], start=True, stop=True)
                    ins = mm(aS[:, P:3 * P], qh[:, P:2 * P], kT[:, h // GRP, 0:2 * P], start=True, stop=True)
                elif e == "pt":
                    answered(pe, h, "share")
                    for s in range(3):
                        ins = pe.transpose(aS[:, s * P:(s + 1) * P], sm[:, s * P:(s + 1) * P], M["ident"])
                elif e == "pv":
                    act_done(pe, h, "pt")
                    mm(aS[:, 0:P], vh[:, 0, :], pT[:, 0:P], start=True, stop=True)
                    mm(aS[:, P:2 * P], vh[:, 0, :], pT[:, P:2 * P], start=True, stop=False)
                    ins = mm(aS[:, P:2 * P], vh[:, 1, :], pT[:, 2 * P:3 * P], start=False, stop=True)
                elif e == "V":
                    u, g = v // 4, v % 4
                    if v == 0:
                        answered(pe, h, "mix")
                    if g == 0:
                        pages_landed(pe, C_V + u, h, 2)
                    for kv in range(NKV):
                        ins = mm(aV[:, kv * GRP:(kv + 1) * GRP], cring[:, u, (g * NKV + kv) * P:(g * NKV + kv + 1) * P],
                                 sal[:, 2 * h + u, g, kv * GRP:(kv + 1) * GRP],
                                 start=v == 0 and kv == 0, stop=v == 7, skip_group_check=True)
                    if g == 3:
                        ins.then_inc(S("page_units_done"), 1)
                    return
                elif e == "xt":
                    answered(pe, h, "mix")
                    act_done(pe, h, "ktok")
                    for p in range(2):
                        pe.transpose(gT[:, p * P:(p + 1) * P], xx[:, 0, p, :], M["ident"])
                    ins = pe.transpose(gT[0:DEC, 256:384], s8[:, 1, :], M["ident"])
                elif e == "outer":
                    pe.wait_ge(S("vm_ready"), h + 1)
                    mm(gT[:, :], knT[:, :], vm[:, 0:4, :].rearrange("p a b -> p (a b)"), start=True, stop=True)
                    ins = mm(gO[:, :], knT[:, :], vm[:, 4:8, :].rearrange("p a b -> p (a b)"), start=True, stop=True)
                elif e in SOLVE_W:
                    n = int(e[1])
                    answered(pe, h, "mix2" if n == 0 else f"x{n - 1}")
                    act_done(pe, h, "xt" if n == 0 else f"w{n - 1}")
                    for p in range(2):
                        ins = mm(gK[:, p * P:(p + 1) * P], lm[n % 2][:, p, :], xx[:, 1, p, :], start=True, stop=True)
                elif e in SOLVE_X:
                    act_done(pe, h, f"w{e[1]}")
                    for p in range(2):
                        mm(gG[:, p * P:(p + 1) * P], wt[:, p, :], xx[:, 0, p, :], start=True, stop=True)
                        ins = mm(gG[:, (2 + p) * P:(3 + p) * P], xx[:, 0, p, :], wt[:, p, :], start=True, stop=True)
                elif e == "uw":
                    answered(pe, h, "x4")
                    for p in range(2):
                        ins = mm(gK[:, p * P:(p + 1) * P], kbe[:, p, :], xx[:, 1, p, :], start=True, stop=True)
                elif e in CHUNKS_A or e in CHUNKS_B:
                    c = int(e[1])
                    p, r0 = c // 2, CHUNK * (c % 2)
                    rows = slice(r0, r0 + CHUNK)
                    if e[2] == "a":
                        answered(pe, h, "uw" if c == 0 else f"c{c - 1}b")
                        if c == 0:
                            act_done(pe, h, "uw")
                        o = gT[rows, c * P:(c + 1) * P]
                        mm(o, xx[:, 1, p, rows], vb[:, p, :], start=True, stop=False)
                        ins = mm(o, nwt[:, c * CHUNK:(c + 1) * CHUNK], St[:, :], start=False, stop=True)
                    else:
                        act_done(pe, h, f"c{c}a")
                        mm(gG[:, 0:P], kd[rows, p, :], vn[rows, :], start=True, stop=True)
                        o = gO[:, c * CHUNK:(c + 1) * CHUNK]
                        mm(o, St[:, :], qe[:, c * CHUNK:(c + 1) * CHUNK], start=True, stop=False)
                        ins = mm(o, vn[rows, :], qkt[rows, p, rows], start=False, stop=True)
                elif e == "ms":
                    act_done(pe, h, "c3b")
                    ins = mm(gK[:, 0:T], M["ones"], osq[:, :], start=True, stop=True)
                ins.then_inc(S("multiplied"), 1)

            norms(0)
            pe.wait_ge(S("sample_soft"), 1)

            def turn(h, events):
                n = v = 0
                for e in events:
                    if e == "P":
                        tile(U_HEAD + 4, T_HEAD + 4, n // 8, h, 4, x, lo=2 * (n % 8), hi=2 * (n % 8) + 2)
                        n += 1
                    elif e == "ss":
                        answered(pe, h, "pv")
                        norms(h + 1)
                    elif e == "V":
                        step(h, e, v)
                        v += 1
                    elif e in BY_PE:
                        step(h, e)
                act_done(pe, h, "ms")

            with pe.Fori(0, NH - 1) as h:
                turn(h, TURN)
            turn(NH - 1, LAST_TURN)
            with pe.Fori(0, KD // 4) as i:
                for u in range(4):
                    if u == 0:
                        pe.wait_ge(S("merged"), 1)
                    tile(U_WO, T_WO, u, i, 4, lambda k: gA[:, k, :])
            norm(1)
            ffn_up(U_UP2, KF)
            ffn_down(U_DN2, T_DN2, KF)
            norm(2)

        @block.scalar
        def _(act):
            do = act.activation
            own_a = Own(act, S("act_own"))

            def silu_gates(n_up, base):
                with act.Fori(0, KF // 2) as i:
                    for f in range(2):
                        unit_done(act, n_up + 2 * f, i, 4)
                        act.wait_ge(S("pair_free"), i * 2 + (base + f + 1))
                        do(sg[:, f, :], upb[f][0][:, 0:T], ACT.Silu).then_inc(S("silu_done"), 1)

            def norm(n):
                for k in range(0, KD, 4):
                    act.wait_ge(S("centred"), 4 * n + k // 4 + 1)
                    do(sqr[:, k:k + 4, :], xT[:, k:k + 4, :], ACT.Square).then_inc(S("squares"), 1)
                act.wait_ge(S("stat"), 2 * n + 2)
                do(rstd[:, :], gO[:, 0:T], ACT.Sqrt, bias=epsc[:, 0:1], scale=1.0 / D).then_inc(S("deviation"), 1)
                for k in range(KD):
                    act.wait_ge(S("scaled"), n * KD + k + 1)
                    do(xT[:, k, :], xT[:, k, :], ACT.Identity, bias=lnp[:, 2 * n + 1, k:k + 1],
                       scale=lnp[:, 2 * n, k:k + 1]).then_inc(S("x_ready"), 1)
                    if n == 2:
                        act.wait_ge(S("x_ready"), n * KD + k + 1)
                        act.sem_inc(S("y_out_ready"), 1)

            silu_gates(U_UP1, 0)
            act.wait_ge(S("small_in"), 16 * 28)
            norm(0)
            unit_done(act, U_MISC)
            do(msc[:, :], acc[T_MISC % 2][:, 0:T], ACT.Copy).then_inc(S("misc_raw"), 1)
            act.wait_ge(S("misc_raw"), 1)
            act.sem_inc(S("acc_free"), 1)
            own_a(do(raw2[:, 0, :], msc[:, :], ACT.Exp, scale=-1.0))
            act.sem_inc(S("misc_exp"), 1)
            own_a(do(val[:, :], msc[:, :], ACT.Abs, bias=dtb[:, 0:1]))
            own_a(do(val[:, :], val[:, :], ACT.Exp, scale=-1.0))
            own_a(do(val[:, :], val[:, :], ACT.Ln, bias=1.0))
            own_a(do(alog[:, :], alog[:, :], ACT.Exp))
            act.sem_inc(S("misc_exp"), 1)

            def evacuate(n0, t0, u, it, per, outs):
                unit_done(act, n0 + u, it, per)
                a = acc[(t0 + u) % 2]
                for dst, cols, func in outs:
                    own_a(do(dst, a[:, cols], func))
                act.sem_inc(S("acc_free"), 1)

            def raw_tile(n0, t0, r0, u, it):
                act.wait_ge(S("rope_free"), it * 4 + (r0 + u + 1))
                evacuate(n0, t0, u, it, 4, [(raw2[:, (r0 + u) % 2, :], slice(0, T), ACT.Copy)])
                act.sem_inc(S("raw_ready"), 1)

            with act.Fori(0, 2) as i:
                own_a.enter(i, 4)
                for u in range(4):
                    raw_tile(U_IDXQ, T_IDXQ, 0, u, i)
            own_a.leave(2)
            act.wait_ge(S("val_turned"), 1)
            do(valk[:, :, :], gG[:, 0:2 * P].rearrange("p (a b) -> p a b", a=2), ACT.Copy).then_inc(S("valk_ready"), 1)
            act.wait_ge(S("rows_done"), 1)
            own_a(do(sgs[:, 0, :, :], gO[:, 0:P].rearrange("p (h b) -> p h b", b=DEC), ACT.Exp))
            own_a(do(sgs[:, 1, :, :], gO[:, P:2 * P].rearrange("p (h b) -> p h b", b=DEC), ACT.Copy))
            act.sem_inc(S("rows_read"), 1)
            act.wait_ge(S("exponents"), 1)
            for kind in (2, 3):
                own_a(do(gsc[:, :, kind, :], gsc[:, :, kind, :], ACT.Exp))
            act.sem_inc(S("factors"), 1)
            n = 0
            for h in range(IDXH):
                for t in range(2):
                    w = (t + 1) * P
                    act.wait_ge(S("pidx_done"), n + 1)
                    act.wait_ge(S("pterm_free"), n + 1)
                    own_a(do(rl[:, (n % 2) * 256:(n % 2) * 256 + w], [aS, aV][n % 2][:, 0:w], ACT.Relu))
                    act.sem_inc(S("pidx_free"), 1)
                    act.sem_inc(S("pterm"), 1)
                    n += 1
            act.wait_ge(S("page_units_done"), C_K)
            act.wait_ge(S("pterm_free"), 2 + 32)
            for c, b in enumerate((gT, gK, gG, gO)):
                do(rl[:, c * 512:(c + 1) * 512], b[:, :], ACT.Relu).then_inc(S("rectified"), 1)
            do(rl[:, PAST:PAST + 1], aS[:, 0:1], ACT.Relu).then_inc(S("rectified"), 1)
            for c, b in enumerate((gT, gK, gG, gO)):
                act.wait_ge(S("weighed"), c + 1)
                do(scS[:, c * 512:(c + 1) * 512], b[0:DEC, :], ACT.Copy).then_inc(S("scored"), 1)
            act.wait_ge(S("weighed"), 5)
            do(scS[:, PAST:PAST + 1], aS[0:DEC, 0:1], ACT.Copy).then_inc(S("scored"), 1)
            for u in range(4):
                raw_tile(U_K, T_K, 8, u, 0)
            for u in range(4):
                evacuate(U_V, T_V, u, 0, 0, [(vT[:, u, :], slice(0, T), ACT.Copy)])
                act.sem_inc(S("v_raw"), 1)
            act.wait_ge(S("v_turned"), 1)
            own_a(do(vtok[:, 0, :], gG[:, :], ACT.Copy))
            own_a(do(vtok[:, 1, :], gO[:, :], ACT.Copy))
            act.sem_inc(S("kv_ready"), 1)
            with act.Fori(0, 4) as i:
                own_a.enter(i, 4)
                for u in range(4):
                    raw_tile(U_Q, T_Q, 12, u, i)
            own_a.leave(4)
            flat = gates[:, :, :, :].rearrange("p g k t -> p (g k) t")
            with act.Fori(0, DEC) as i:
                own_a.enter(i, 8)
                for u in range(4):
                    evacuate(U_GATE, T_GATE, u, i, 4, [(flat[:, i * 4 + u, :], slice(0, T), ACT.Sigmoid)])
                    act.wait_ge(S("page_units_done"), i * 4 + (C_K + u + 1))
                    own_a(do(sal[:, i * 4 + u, :, :], [aS, aV][u % 2][:, 0:64].rearrange("p (g n) -> p g n", g=4),
                             ACT.Copy, scale=SCALE))
                    act.sem_inc(S("kscore_free"), 1)
            own_a.leave(DEC)
            act.sem_inc(S("past_scored"), 1)

            act.preload_act_table_set("natural_log_exp_and_others")

            def head_copy(g):
                own_a(do(qh, qT[:, g, 0:SEQ], ACT.Copy), lag=1)
                own_a(do(vh, vtok.rearrange("p s (k d) -> p s k d", k=NKV)[:, :, g // GRP, :], ACT.Copy))
                act.sem_inc(S("head_copied"), 1)

            def sigmoid(dst, src):
                own_a(do(dst, src, ACT.Exp, scale=-1.0))
                own_a(do(dst, dst, ACT.Ln, bias=1.0))
                own_a(do(dst, dst, ACT.Exp, scale=-1.0))

            def prepare(g, e, n0, t0, it):
                if e[0] == "e":
                    u = int(e[1])
                    unit_done(act, n0 + u, it, 4)
                    a = acc[(t0 + u) % 2]
                    if u < 3:
                        own_a(do(raw[:, u, CONVW - 1:], a[:, 0:SEQ], ACT.Copy), lag=1)
                        own_a(do(cs[:, g, u, CONVW - 1, :], a[:, SEQ:T], ACT.Copy))
                        act.sem_inc(S("head_raw"), 1)
                    else:
                        own_a(do(zraw[:, :], a[:, 0:T], ACT.Copy))
                    act.sem_inc(S("acc_free"), 1)
                elif e == "sig3":
                    sigmoid(e4[:, 3, :], zraw[:, :])
                    act.sem_inc(S("z_ready"), 1)
                elif e[0:3] == "sig":
                    j = int(e[3])
                    act.wait_ge(S("asked_next"), count(ASKS_NEXT, f"conv{j}", g))
                    sigmoid(e4[:, j, :], y3[:, j, :])
                    act.sem_inc(S("act_done_next"), 1)
                elif e == "ss":
                    act.wait_ge(S("summed"), g + 1)
                    own_a(do(rs[:, 0:512], gT[:, :], ACT.Ln, bias=epsc[:, 1:2]), lag=1)
                    own_a(do(rs[:, 512:528], aS[:, 0:16], ACT.Ln, bias=epsc[:, 1:2]))
                    own_a(do(rs[:, :], rs[:, :], ACT.Exp, scale=-0.5))
                    act.sem_inc(S("act_done_next"), 1)

            def step(h, e):
                def done():
                    act.sem_inc(S("act_done"), 1)

                if e == "mix":
                    multiplied(act, h, "mix")
                    own_a(do(eg, gG[:, 0:256], ACT.Exp))
                    done()
                    for p in range(2):
                        c = slice(p * P, (p + 1) * P)
                        own_a(do(kbe[:, p, :], gT[:, c], ACT.Copy, scale=hc[:, 2, p:p + 1]), lag=1)
                        own_a(do(kd[:, p, :], gT[:, c], ACT.Copy, scale=hc[:, 3, p:p + 1]), lag=1)
                        own_a(do(vb[:, p, :], gT[:, 256 + p * P:256 + (p + 1) * P], ACT.Copy, scale=hc[:, 1, p:p + 1]), lag=1 - p)
                    done()
                    act.wait_ge(S("asked"), count(ASKS, "decay", h))
                    own_a(do(dab[:, 0:256], dab[:, 0:256], ACT.Exp, scale=-1.0), lag=1)
                    own_a(do(dab[:, 256:512], dab[:, 256:512], ACT.Exp))
                    done()
                elif e == "soft":
                    act.wait_ge(S("asked"), count(ASKS, "soft", h))
                    own_a(do(sm[:, 0:P], sm[:, 0:P], ACT.Exp, bias=at_s[:, 2:3], accum_out=at_s[:, 4:5]), lag=1)
                    own_a(do(sm[:, P:3 * P], sm[:, P:3 * P], ACT.Exp, bias=at_s[:, 3:4], accum_out=at_s[:, 5:6]))
                    done()
                elif e == "pt":
                    multiplied(act, h, "pt")
                    own_a(do(pT, aS[:, 0:3 * P], ACT.Copy))
                    done()
                elif e == "xt":
                    multiplied(act, h, "xt")
                    own_a(do(xx[:, 1], gT[:, 0:256].rearrange("p (a b) -> p a b", a=2), ACT.Copy), lag=1)
                    own_a(do(knT[:, :], gG[0:DEC, 384:512], ACT.Copy))
                    done()
                elif e in SOLVE_W:
                    multiplied(act, h, e)
                    own_a(do(wt, gK[:, 0:256].rearrange("p (a b) -> p a b", a=2), ACT.Copy))
                    done()
                elif e == "uw":
                    multiplied(act, h, "uw")
                    own_a(do(nwt, gK[:, 0:256], ACT.Copy, scale=-1.0))
                    done()
                elif e in CHUNKS_A:
                    c = int(e[1])
                    r0 = CHUNK * (c % 2)
                    multiplied(act, h, e)
                    own_a(do(vn[r0:r0 + CHUNK, :], gT[r0:r0 + CHUNK, c * P:(c + 1) * P], ACT.Copy))
                    done()
                elif e == "c3b":
                    multiplied(act, h, e)
                    own_a(do(ob[:, 0:SEQ], gO[:, 0:SEQ], ACT.Copy), lag=1)
                    own_a(do(osq[:, 0:SEQ], gO[:, 0:SEQ], ACT.Square), lag=1)
                    own_a(do(osq[:, SEQ:T], ob[:, SEQ:T], ACT.Square))
                    done()
                elif e == "ms":
                    multiplied(act, h, "ms")
                    own_a(do(rms[:, :], gK[:, 0:T], ACT.Ln, bias=epsc[:, 1:2], scale=1.0 / P))
                    own_a(do(rms[:, :], rms[:, :], ACT.Exp, scale=-0.5))
                    done()

            for e in FIRST:
                if e == "sig0":
                    act.wait_ge(S("shifted"), 1)
                    own_a(do(sal[:, :, :, :], sal[:, :, :, :], ACT.Exp))
                    own_a(do(pn[:, :, :], pn[:, :, :], ACT.Exp))
                    act.sem_inc(S("soft_exp"), 1)
                prepare(0, e, U_HEAD, T_HEAD, 0)
            head_copy(0)

            def turn(h, events):
                for e in events:
                    if e in NEXT:
                        prepare(h + 1, e, U_HEAD + 4, T_HEAD + 4, h)
                        if e == "e3":
                            head_copy(h + 1)
                    else:
                        step(h, e)

            with act.Fori(0, NH - 1) as h:
                own_a.enter(h, ACT_PER_HEAD)
                turn(h, TURN)
            own_a.leave(NH - 1)
            turn(NH - 1, LAST_TURN)
            norm(1)
            silu_gates(U_UP2, KF)
            norm(2)

        @block.vector
        def _(v):
            own_v = Own(v, S("dve_own"))
            ts, stt, tt, cp = v.tensor_scalar, v.scalar_tensor_tensor, v.tensor_tensor, v.tensor_copy

            def bc(ap, shape):
                return ap.to_broadcast(shape)

            v.sem_inc(S("pair_free"), 2)
            v.sem_inc(S("acc_free"), 2)
            v.sem_inc(S("rope_free"), 2)
            v.sem_inc(S("pidx_free"), 2)
            v.sem_inc(S("pterm_free"), 2)
            v.sem_inc(S("kscore_free"), 2)

            def products(n_up, base):
                with v.Fori(0, KF // 2) as i:
                    for f in range(2):
                        unit_done(v, n_up + 2 * f + 1, i, 4)
                        v.wait_ge(S("silu_done"), i * 2 + (base + f + 1))
                        stt(out=hT[:, i * 2 + f, :], in0=upb[f][1][:, 0:T], scalar=0.5, in1=sg[:, f, :],
                            op0=ALU.mult, op1=ALU.mult).then_inc(S("pair_free"), 1)

            def residual(n0, units, t0, n):
                with v.Fori(0, KD // 2) as i:
                    for c in range(2):
                        unit_done(v, n0 + units * (c + 1) - 1, i, 2 * units)
                        stt(out=xT[:, i * 2 + c, :], in0=xT[:, i * 2 + c, :], scalar=ALPHA, in1=acc[(t0 + c) % 2][:, 0:T],
                            op0=ALU.mult, op1=ALU.add).then_inc(S("y_ready"), 1)
                        v.wait_ge(S("y_ready"), i * 2 + (n * KD + c + 1))
                        v.sem_inc(S("acc_free"), 1)

            def norm(n):
                v.wait_ge(S("stat"), 2 * n + 1)
                own_v(ts(mean[:, :], gG[:, 0:T], 1.0 / D, None, ALU.mult))
                for k in range(0, KD, 4):
                    tt(xT[:, k:k + 4, :], xT[:, k:k + 4, :], mean[:, :].unsqueeze(1).to_broadcast([P, 4, T]),
                       ALU.subtract).then_inc(S("centred"), 1)
                v.wait_ge(S("centred"), 4 * n + 4)
                v.wait_ge(S("deviation"), n + 1)
                own_v(v.reciprocal(rstd[:, :], rstd[:, :]))
                v.wait_ge(S("squares"), 4 * n + 4)
                for k in range(KD):
                    tt(xT[:, k, :], xT[:, k, :], rstd[:, :], ALU.mult).then_inc(S("scaled"), 1)

            products(U_UP1, 0)
            residual(U_DN1, 4, T_DN1, 0)
            norm(0)
            v.wait_ge(S("small_in"), 16 * 28)
            own_v(v.memset(raw[:, :, 0:CONVW - 1], 0.0))
            v.wait_ge(S("ki_rot"), 1)
            v.wait_ge(S("misc_raw"), 1)
            own_v(tt(kiT[:, :], gT[:, 0:T], rope[:, 2, :], ALU.mult))
            own_v(tt(tmp[:, :], gK[:, 0:T], rope[:, 3, :], ALU.mult))
            own_v(tt(kiT[:, :], kiT[:, :], tmp[:, :], ALU.add))
            v.sem_inc(S("kv_ready"), 1)
            v.wait_ge(S("misc_exp"), 2)
            own_v(ts(raw2[:, 0, :], raw2[:, 0, :], 1.0, None, ALU.add))
            own_v(v.reciprocal(raw2[:, 0, :], raw2[:, 0, :]))
            own_v(ts(raw2[:, 0, :], raw2[:, 0, :], rowm[:, 2:3], None, ALU.mult))
            own_v(ts(alog[:, :], alog[:, :], -1.0, rowm[:, 1:2], ALU.mult, ALU.mult))
            own_v(ts(tmp[:, :], msc[:, :], dtb[:, 0:1], 0.0, ALU.add, ALU.max))
            own_v(tt(val[:, :], val[:, :], tmp[:, :], ALU.add))
            own_v(stt(out=val[:, :], in0=val[:, :], scalar=alog[:, 0:1], in1=raw2[:, 0, :], op0=ALU.mult, op1=ALU.add))
            own_v(stt(out=val[:, :], in0=msc[:, :], scalar=rowm[:, 0:1], in1=val[:, :], op0=ALU.mult, op1=ALU.add))
            v.sem_inc(S("val_ready"), 1)
            own_v(tt(rms[:, 0:256].rearrange("p (k b) -> p k b", b=DEC),
                     M["ident"][:, R_A:R_A + 2 * NH].unsqueeze(2).to_broadcast([P, 2 * NH, DEC]),
                     val[:, SEQ:T].unsqueeze(1).to_broadcast([P, 2 * NH, DEC]), ALU.mult))
            v.sem_inc(S("picked"), 1)
            v.sem_inc(S("ki_ready"), 1)

            def roped(r0, u, it, dst, table):
                v.wait_ge(S("rotated"), it * 4 + (r0 + u + 1))
                r = r0 + u
                own_v(tt(dst, raw2[:, r % 2, :], rope[:, table, :], ALU.mult))
                own_v(tt(tmp[:, :], [gT, gK][r % 2][:, 0:T], rope[:, table + 1, :], ALU.mult))
                own_v(tt(dst, dst, tmp[:, :], ALU.add))
                v.sem_inc(S("rope_free"), 1)

            with v.Fori(0, 2) as i:
                own_v.enter(i, 12)
                for u in range(4):
                    roped(0, u, i, qiT[:, i * 4 + u, :], 2)
            own_v.leave(2)
            own_v(v.memset(zq[:, :, :], 0.0))
            for h2 in range(2):
                rows = slice(h2 * IDXD, (h2 + 1) * IDXD)
                for b in range(DEC):
                    own_v(cp(zq[rows, b, b * IDXH + h2:(b + 1) * IDXH:2], qiT[rows, :, SEQ + b]))
            v.sem_inc(S("zq_ready"), 1)
            v.wait_ge(S("decays"), 1)
            v.wait_ge(S("rows_done"), 1)
            v.wait_ge(S("valk_ready"), 1)
            v.wait_ge(S("rows_read"), 1)
            own_v(tt(w8[:, :], gO[:, 256:256 + DEC], own[:, :], ALU.mult))
            for t in range(2):
                own_v(cp(gsc[:, :, 0, t], gK[:, 32 * t:32 * t + 16]))
                own_v(cp(gsc[:, :, 1, t], valk[:, t, R_B:R_B + NH]))
                own_v(cp(gsc[:, :, 2, t], gK[:, 32 * t:32 * t + 16]))
                own_v(tt(gsc[:, :, 3, t], gK[:, 32 * t + 16:32 * t + 32], gsc[:, :, 0, t], ALU.subtract))
            v.sem_inc(S("exponents"), 1)
            v.wait_ge(S("factors"), 1)
            own_v(tt(gsc[:, :, 2, :], gsc[:, :, 2, :], gsc[:, :, 1, :], ALU.mult))
            v.sem_inc(S("decays_read"), 1)
            own_v(v.memset(pscore[:, :], 0.0))
            n = 0
            for h in range(IDXH):
                for t in range(2):
                    w, c = (t + 1) * P, slice(t * P, 3 * P if t else P)
                    v.wait_ge(S("pterm"), n + 1)
                    own_v(stt(out=pscore[:, c], in0=rl[:, (n % 2) * 256:(n % 2) * 256 + w],
                              scalar=valk[:, t, R_W + h:R_W + h + 1], in1=pscore[:, c], op0=ALU.mult, op1=ALU.add))
                    v.sem_inc(S("pterm_free"), 1)
                    n += 1
            for u in range(4):
                roped(8, u, 0, kT[:, u, :], 0)
            v.sem_inc(S("kv_ready"), 1)
            with v.Fori(0, 4) as i:
                own_v.enter(i, 12)
                for u in range(4):
                    roped(12, u, i, qT[:, i * 4 + u, :], 0)
            own_v.leave(4)
            own_v(tt(pscore[:, :], pscore[:, :], caus[:, :], ALU.mult))
            own_v(ts(pbias[:, :], caus[:, :], -1.0, -NEG, ALU.add, ALU.mult))
            own_v(tt(pscore[:, :], pscore[:, :], pbias[:, :], ALU.add))
            for t in range(2):
                c = slice(t * P, 3 * P if t else P)
                for _r in range(TOPK_P // 8):
                    own_v(v.max(out=top8[:, :], in_=pscore[:, c]))
                    own_v(v.match_replace(out=pscore[:, c], in_to_replace=top8[:, :], in_values=pscore[:, c], imm_value=GONE))
            own_v(stt(out=pbias[:, :], in0=pscore[:, :], scalar=GONE, in1=caus[:, :], op0=ALU.is_equal, op1=ALU.mult))
            own_v(ts(pbias[:, :], pbias[:, :], -1.0, OFF, ALU.add, ALU.mult))
            v.wait_ge(S("scored"), 5)
            for _r in range(TOPK_S // 8):
                own_v(v.max(out=top8[0:DEC, :], in_=scS[:, :]))
                own_v(v.match_replace(out=scS[:, :], in_to_replace=top8[0:DEC, :], in_values=scS[:, :], imm_value=GONE))
            own_v(ts(scS[:, :], scS[:, :], GONE, None, ALU.is_equal))
            own_v(ts(s8[0:DEC, 0, :], M["ident"][0:DEC, 0:DEC], scS[:, PAST:PAST + 1], None, ALU.mult))
            for kv in range(NKV):
                own_v(tt(sn[:, :, kv * GRP:(kv + 1) * GRP].rearrange("p b g -> p g b"),
                         qT[:, kv * GRP:(kv + 1) * GRP, SEQ:T],
                         kT[:, kv, SEQ:T].unsqueeze(1).to_broadcast([P, GRP, DEC]), ALU.mult))
            v.sem_inc(S("selected"), 1)
            v.wait_ge(S("masks_turned"), 1)
            own_v(ts(mbt[:, :, :].rearrange("p b g -> p g b"), gT[:, 0:P].rearrange("p (g b) -> p g b", b=DEC),
                     -1.0, OFF, ALU.add, ALU.mult))
            own_v(ts(nbt[:, :], gK[:, 0:DEC], -1.0, OFF, ALU.add, ALU.mult))
            own_v(ts(sn[:, :, :], gG[:, 0:P].rearrange("p (b n) -> p b n", n=NH), SCALE, None, ALU.mult))
            own_v(tt(sn[:, :, :], sn[:, :, :], nbt[:, :].unsqueeze(2).to_broadcast([P, DEC, NH]), ALU.add))
            v.wait_ge(S("past_scored"), 1)
            salf = sal[:, :, :, :].rearrange("p u g n -> p (u g) n")
            own_v(tt(salf, salf, mbt[:, :, :].rearrange("p b g -> p (b g)").unsqueeze(2).to_broadcast([P, P, NH]), ALU.add))
            bgn = sal[:, :, :, :].rearrange("p (b q) g n -> p b n (q g)", b=DEC)
            own_v(v.tensor_reduce(gmx[:, :, :], bgn, AX.X, ALU.max))
            v.sem_inc(S("part_max"), 1)
            v.wait_ge(S("all_max"), 1)
            own_v(tt(gmx[:, :, :], gmx[:, :, :], sn[:, :, :], ALU.max))
            for b in range(DEC):
                own_v(tt(salf[:, b * PAGES:(b + 1) * PAGES, :], salf[:, b * PAGES:(b + 1) * PAGES, :],
                         gmx[:, b, :].unsqueeze(1).to_broadcast([P, PAGES, NH]), ALU.subtract))
            own_v(tt(pn[:, :, :], sn[:, :, :], gmx[:, :, :], ALU.subtract))
            v.sem_inc(S("shifted"), 1)
            v.wait_ge(S("soft_exp"), 1)
            own_v(v.tensor_reduce(rin[:, :, :], bgn, AX.X, ALU.add))
            v.sem_inc(S("expsum"), 1)
            v.wait_ge(S("denoms"), 1)
            own_v(tt(rin[:, :, :], gG[:, 0:P].rearrange("p (b n) -> p b n", n=NH), pn[:, :, :], ALU.add))
            own_v(v.reciprocal(rin[:, :, :], rin[:, :, :]))
            v.sem_inc(S("sample_soft"), 1)

            def two(ap):
                return ap.unsqueeze(1).to_broadcast([P, 2, P])

            def take(dst, src):
                return ts(dst, src, 1.0, None, ALU.mult)

            def factors(g):
                own_v(take(hc[:, :, :], gsc[:, g, :, :]), lag=1)
                own_v(take(hg[:, :, :], sgs[:, :, g, :]), lag=1)
                own_v(cp(dg[:, 0, :], M["ident"]), lag=1)
                own_v(cp(dg[:, 1, :], M["ident"]))
                for p in range(2):
                    own_v(ts(dg[:, p, :], dg[:, p, :], hc[:, 0, p:p + 1], None, ALU.mult), lag=1 - p)

            def prepare(g, e):
                if e[0:4] == "conv":
                    j = int(e[4])
                    if e[5] == "a":
                        v.wait_ge(S("head_raw"), g * 3 + (j + 1))
                        own_v(take(hw[:, :], cw[:, g, :]), lag=1)
                        own_v(take(cpb[:, g, j, :], raw[:, j, SEQ:]))
                    for k in (0, 1) if e[5] == "a" else (2, 3):
                        w = hw[:, 4 * j + k:4 * j + k + 1]
                        if k == 0:
                            own_v(ts(y3[:, j, 0:SEQ], raw[:, j, 0:SEQ], w, None, ALU.mult), lag=1)
                            own_v(ts(y3[:, j, SEQ:T], cs[:, g, j, 0, :], w, None, ALU.mult), lag=1)
                        else:
                            own_v(stt(out=y3[:, j, 0:SEQ], in0=raw[:, j, k:k + SEQ], scalar=w, in1=y3[:, j, 0:SEQ],
                                      op0=ALU.mult, op1=ALU.add), lag=1)
                            own_v(stt(out=y3[:, j, SEQ:T], in0=cs[:, g, j, k, :], scalar=w, in1=y3[:, j, SEQ:T],
                                      op0=ALU.mult, op1=ALU.add), lag=0 if k % 2 else 1)
                    if e[5] == "b":
                        v.sem_inc(S("asked_next"), 1)
                elif e[0:4] == "silu":
                    j = int(e[4])
                    act_done_next(v, g, f"sig{j}")
                    own_v(tt(y3[:, j, :], y3[:, j, :], e4[:, j, :], ALU.mult))
                    own_v(tt(sq[:, j * SEQ:(j + 1) * SEQ], y3[:, j, 0:SEQ], y3[:, j, 0:SEQ], ALU.mult), lag=1)
                    own_v(tt(sq[:, 512 + 8 * j:520 + 8 * j], y3[:, j, SEQ:T], y3[:, j, SEQ:T], ALU.mult))
                    if j == 1:
                        own_v(tt(sq[:, 528:536], y3[:, 0, SEQ:T], y3[:, 1, SEQ:T], ALU.mult))
                        v.sem_inc(S("squared"), 1)
                elif e == "norm":
                    act_done_next(v, g, "sig2")
                    own_v(tt(y3[:, 2, :], y3[:, 2, :], e4[:, 2, :], ALU.mult), lag=1)
                    factors(g)
                    act_done_next(v, g, "ss")
                    own_v(stt(out=qkn[:, 0:SEQ], in0=y3[:, 0, 0:SEQ], scalar=SCALE, in1=rs[:, 0:SEQ], op0=ALU.mult, op1=ALU.mult), lag=1)
                    own_v(tt(qkn[:, SEQ:512], y3[:, 1, 0:SEQ], rs[:, SEQ:512], ALU.mult), lag=1)
                    own_v(tt(kq[:, 0, :], y3[:, 1, SEQ:T], rs[:, 520:528], ALU.mult), lag=1)
                    own_v(stt(out=kq[:, 1, :], in0=y3[:, 0, SEQ:T], scalar=SCALE, in1=rs[:, 512:520], op0=ALU.mult, op1=ALU.mult), lag=1)
                    own_v(stt(out=s8[:, 2, :], in0=aS[:, 16:24], scalar=SCALE, in1=rs[:, 512:520], op0=ALU.mult, op1=ALU.mult))
                    own_v(tt(s8[:, 2, :], s8[:, 2, :], rs[:, 520:528], ALU.mult))
                    v.sem_inc(S("normalized"), 1)

            def step(h, e):
                def answer():
                    v.sem_inc(S("answered"), 1)

                if e == "mix":
                    multiplied(v, h, "mix")
                    act_done(v, h, "eg")
                    for p in range(2):
                        c = slice(p * P, (p + 1) * P)
                        own_v(ts(dab[:, c], gG[:, c], hc[:, 0, p:p + 1], 0.0, ALU.subtract, ALU.max), lag=1)
                        own_v(ts(dab[:, 256 + p * P:256 + (p + 1) * P], gG[:, c], hc[:, 0, p:p + 1], 0.0,
                                 ALU.subtract, ALU.min), lag=1 - p)
                    v.sem_inc(S("asked"), 1)
                    st = gG[:, 256:272].rearrange("p (b c) -> p c b", c=2)
                    own_v(tt(s8[:, 3, :], st[:, 0, :], hg[:, 0, :], ALU.mult), lag=1)
                    own_v(tt(s8[:, 4, :], st[:, 1, :], hg[:, 0, :], ALU.mult), lag=1)
                    own_v(tt(s8[:, 3, :], y3[:, 2, SEQ:T], s8[:, 3, :], ALU.subtract))
                    own_v(tt(s8[:, 1, :], s8[:, 3, :], hg[:, 1, :], ALU.mult))
                    act_done(v, h, "decay")
                    for p in range(2):
                        own_v(stt(out=lf[:, p, :], in0=gK[:, p * P:(p + 1) * P], scalar=hc[:, 1, p:p + 1],
                                  in1=dab[:, p * P:(p + 1) * P], op0=ALU.mult, op1=ALU.mult), lag=1 - p)
                    own_v(tt(wt, lf, two(M["lv1"]), ALU.mult))
                    own_v(tt(xx[:, 0], two(M["ident"]), wt, ALU.subtract))
                    answer()
                    v.wait_ge(S("z_ready"), h + 1)
                    own_v(tt(zs, zraw[:, :], e4[:, 3, :], ALU.mult))
                elif e == "lift":
                    multiplied(v, h, "qk")
                    own_v(stt(out=sm, in0=aS[:, 0:3 * P], scalar=SCALE, in1=pbias[:, :], op0=ALU.mult, op1=ALU.add))
                    own_v(v.tensor_reduce(at_s[:, 0:1], sm[:, 0:P], AX.X, ALU.max), lag=1)
                    own_v(v.tensor_reduce(at_s[:, 1:2], sm[:, P:3 * P], AX.X, ALU.max))
                    own_v(ts(at_s[:, 2:4], at_s[:, 0:2], -1.0, None, ALU.mult))
                    v.sem_inc(S("asked"), 1)
                elif e == "mix2":
                    own_v(tt(qkt, gK[:, 256:512].rearrange("p (a b) -> p a b", a=2),
                             dab[:, 256:512].rearrange("p (a b) -> p a b", a=2), ALU.mult), lag=1)
                    own_v(tt(lm[0], lf, two(M["lv2"]), ALU.mult))
                    answer()
                    own_v(tt(lm[1], lf, two(M["lv4"]), ALU.mult), lag=1)
                    own_v(tt(qe, qkn[:, 0:SEQ], eg, ALU.mult))
                    own_v(tt(qkt, qkt, two(M["incl"]), ALU.mult), lag=1)
                    own_v(tt(s8[:, 5, :], s8[:, 2, :], s8[:, 1, :], ALU.mult))
                    own_v(tt(ob[:, SEQ:T], s8[:, 4, :], s8[:, 5, :], ALU.add), lag=1)
                elif e == "share":
                    act_done(v, h, "soft")
                    own_v(v.reciprocal(at_s[:, 4:6], at_s[:, 4:6]))
                    own_v(ts(sm[:, 0:P], sm[:, 0:P], at_s[:, 4:5], None, ALU.mult), lag=1)
                    own_v(ts(sm[:, P:3 * P], sm[:, P:3 * P], at_s[:, 5:6], None, ALU.mult))
                    answer()
                elif e == "pv":
                    multiplied(v, h, e)
                    own_v(tt(gA[:, h, 0:SEQ], gA[:, h, 0:SEQ], aS[:, 0:SEQ], ALU.mult))
                    answer()
                elif e == "vout":
                    v.wait_ge(S("page_units_done"), h * 2 + (C_V + 2))
                    own_v(take(oS[:, h, :], aV[:, 0:NH]))
                    answer()
                elif e == "vm":
                    act_done(v, h, "xt")
                    own_v(tt(vm, M["ident"][0:DEC, 0:DEC].unsqueeze(2).to_broadcast([DEC, DEC, P]),
                             gT[0:DEC, 256:384].unsqueeze(1).to_broadcast([DEC, DEC, P]), ALU.mult))
                    v.sem_inc(S("vm_ready"), 1)
                elif e == "added":
                    multiplied(v, h, "outer")
                    v.wait_ge(S("state_scaled"), h + 1)
                    for q, b in enumerate((gT, gO)):
                        own_v(tt(sst[:, 4 * q:4 * q + 4, :], sst[:, 4 * q:4 * q + 4, :],
                                 b[:, :].rearrange("p (a b) -> p a b", a=4), ALU.add), lag=1 - q)
                    answer()
                elif e in SOLVE_X:
                    n = int(e[1])
                    multiplied(v, h, e)
                    flat = xx.rearrange("p x a b -> p (x a b)")
                    own_v(tt(flat, flat, gG[:, :], ALU.subtract))
                    answer()
                    if n + 2 < len(LEVELS):
                        own_v(tt(lm[n % 2], lf, two(M[f"lv{LEVELS[n + 2]}"]), ALU.mult))
                elif e == "uw":
                    v.wait_ge(S("prompt_state_free"), h + 1)
                    own_v(v.memset(St, 0.0))
                    answer()
                elif e in CHUNKS_B:
                    c = int(e[1])
                    multiplied(v, h, e)
                    own_v(stt(out=St, in0=St, scalar=eg[:, (c + 1) * CHUNK - 1:(c + 1) * CHUNK],
                              in1=gG[:, 0:P], op0=ALU.mult, op1=ALU.add))
                    answer()
                elif e == "gated":
                    act_done(v, h, "ms")
                    own_v(stt(out=ob, in0=ob, scalar=gnorm[:, 0:1], in1=rms[:, :], op0=ALU.mult, op1=ALU.mult))
                    own_v(tt(ob, ob, zs, ALU.mult))
                    own_v(tt(gB[:, h, :], gB[:, h, :], ob, ALU.mult))
                    answer()
                    v.sem_inc(S("head_over"), 1)

            for e in FIRST:
                prepare(0, e)

            def turn(h, events):
                for e in events:
                    if e in NEXT:
                        prepare(h + 1, e)
                    else:
                        step(h, e)

            with v.Fori(0, NH - 1) as h:
                own_v.enter(h, DVE_PER_HEAD)
                turn(h, TURN)
            own_v.leave(NH - 1)
            turn(NH - 1, LAST_TURN)
            pair = oS[:, :, :].rearrange("p (b u) n -> p b u n", u=2)
            own_v(tt(sn[:, :, :], pair[:, :, 0, :], pair[:, :, 1, :], ALU.add))
            for kv in range(NKV):
                g = slice(kv * GRP, (kv + 1) * GRP)
                own_v(tt(gmx[:, :, g], pn[:, :, g], vT[:, kv, SEQ:T].unsqueeze(2).to_broadcast([P, DEC, GRP]), ALU.mult))
            own_v(tt(sn[:, :, :], sn[:, :, :], gmx[:, :, :], ALU.add))
            own_v(tt(sn[:, :, :], sn[:, :, :], rin[:, :, :], ALU.mult))
            own_v(tt(gA[:, :, SEQ:T], gA[:, :, SEQ:T], sn[:, :, :].rearrange("p b n -> p n b"), ALU.mult))
            own_v(tt(gA, gA, gB, ALU.add))
            v.sem_inc(S("merged"), 1)
            residual(U_WO, 1, T_WO, 1)
            norm(1)
            products(U_UP2, KF)
            residual(U_DN2, 4, T_DN2, 2)
            norm(2)


DVE_PER_HEAD, ACT_PER_HEAD = 98, 53
_OUTS = [("yT", (P, KD * T)), ("kT", (P, NKV * T)), ("vT", (P, NKV * T)), ("kiT", (IDXD, T)),
         ("ssm_p", (NH, P, P)), ("ssm_s", (NH, P, DEC, P)), ("convp", (P, NH * 9)), ("convs", (P, NH * 96))]


def lay_out(a):
    f = lambda n: np.asarray(a[n])
    x = np.concatenate([f("x_prompt")[0], f("x_sample")[:, 0]], 0)

    def units(w, nk):
        k, n = w.shape
        return w.reshape(k // P // nk, nk, P, n // P, P).transpose(3, 0, 2, 1, 4)

    def up(g, u):
        return np.stack([units(g, KD)[:, 0], units(u, KD)[:, 0]], 1).reshape(2 * KF, P, KD * P)

    def down(w):
        return np.ascontiguousarray(units(w, QD)).reshape(4 * KD, P, QD * P)

    w = f("w_in")[0]
    names = [("q", 2048), ("k", 512), ("v", 512), ("qi", 1024), ("ki", 64), ("wi", 16), ("qkv", 6144),
             ("a", 16), ("b", 16), ("z", 2048), ("ga", 2048), ("gb", 2048)]
    s, at = {}, 0
    for n, c in names:
        s[n] = w[:, at:at + c]
        at += c
    heads = []
    for h in range(NH):
        c = slice(h * P, (h + 1) * P)
        heads += [s["qkv"][:, 0:2048][:, c], s["qkv"][:, 2048:4096][:, c], s["qkv"][:, 4096:][:, c], s["z"][:, c]]
    pad = np.zeros((D, P - 112), np.float32)
    w_in = np.concatenate([s["ki"], s["wi"], s["a"], s["b"], pad, s["qi"], s["k"], s["v"], s["q"], s["ga"], s["gb"]] + heads, 1)
    cols = lambda m: np.ascontiguousarray(m.reshape(KD, P).T)
    place = lambda m: np.concatenate([np.zeros(R_A, np.float32), m, np.zeros(P - R_A - NH, np.float32)]).reshape(P, 1)
    conv = f("conv_w")[0].reshape(CONVW, 3, NH, P).transpose(3, 2, 1, 0)
    sconv = f("state_conv")[0].reshape(DEC, CONVW - 1, 3, NH, P).transpose(4, 3, 2, 1, 0)
    ki = f("cache_idx_k")[0].transpose(0, 2, 1)
    d = {
        "xT": x.T.reshape(KD, P, T).transpose(1, 0, 2).reshape(P, KD * T),
        "up1": up(f("ffn1_w_gate")[0], f("ffn1_w_up")[0]), "dn1": down(f("ffn1_w_down")[0]),
        "up2": up(f("ffn2_w_gate")[0], f("ffn2_w_up")[0]), "dn2": down(f("ffn2_w_down")[0]),
        "w_in": units(w_in, KD)[:, 0].reshape(-1, P, KD * P), "w_o": units(f("w_o")[0], KD)[:, 0].reshape(KD, P, KD * P),
        "cki": np.concatenate([ki, ki], 1), "ck": f("cache_k")[0].transpose(0, 3, 2, 1).reshape(-1, P, NKV * DH),
        "cv": f("cache_v")[0].reshape(-1, P, NKV * DH),
        "ssm": f("state_ssm")[0].transpose(1, 2, 0, 3),
        "lnp": np.stack([cols(f(n)[0]) for n in ("ln1_g", "ln1_b", "ln2_g", "ln2_b", "ln3_g", "ln3_b")], 1).reshape(P, -1),
        "cw": conv.reshape(P, -1), "convs": sconv.reshape(P, NH, 3, -1),
        "gnorm": f("gdn_norm_g")[0].reshape(P, 1), "alog": place(f("a_log")[0]), "dtb": place(f("dt_bias")[0]),
        "pt": f("page_table").reshape(1, -1),
    }
    d.update(host_constants())
    return {k: np.ascontiguousarray(m) for k, m in d.items()}


def kernel(**inputs):
    import concourse.bacc as bacc
    from concourse.bass_utils import run_bass_kernel_spmd

    nc = bacc.Bacc("TRN2", target_bir_lowering=False, num_devices=1)
    arrays = lay_out(inputs)
    din = {k: nc.dram_tensor(f"in_{k}", a.shape, mybir.dt.from_np(a.dtype), kind="ExternalInput").ap() for k, a in arrays.items()}
    dout = {k: nc.dram_tensor(f"out_{k}", s, F32, kind="ExternalOutput").ap() for k, s in _OUTS}
    build(nc, din, dout)
    r = run_bass_kernel_spmd(nc, [{f"in_{k}": a for k, a in arrays.items()}], core_ids=[0]).results[0]
    o = {k: np.asarray(r[f"out_{k}"]) for k, _ in _OUTS}
    y = o["yT"].reshape(P, KD, T).transpose(2, 1, 0).reshape(T, D)
    kv = {k: o[k].reshape(P, NKV, T).transpose(2, 1, 0) for k in ("kT", "vT")}
    ki = o["kiT"].T
    ssm_s = o["ssm_s"].transpose(2, 0, 1, 3)
    convp = o["convp"].reshape(P, NH, 3, CONVW - 1).transpose(3, 2, 1, 0).reshape(CONVW - 1, -1)
    convs = o["convs"].reshape(P, NH, 3, CONVW, DEC)[:, :, :, 1:].transpose(4, 3, 2, 1, 0).reshape(DEC, CONVW - 1, -1)
    c = np.ascontiguousarray
    return (c(y[None, :SEQ]), c(y[SEQ:, None]),
            c(kv["kT"][None, None, :SEQ]), c(kv["vT"][None, None, :SEQ]), c(ki[None, None, :SEQ]),
            c(o["ssm_p"][None, None]), c(convp[None, None]),
            c(kv["kT"][None, SEQ:, None]), c(kv["vT"][None, SEQ:, None]), c(ki[None, SEQ:, None]),
            c(ssm_s[None]), c(convs[None]))
```

```python
from contextlib import ExitStack

import numpy as np
import concourse.bass as bass
from concourse import mybir

F32 = mybir.dt.float32
I32 = mybir.dt.int32
ALU = mybir.AluOpType
ACT = mybir.ActivationFunctionType
AX = mybir.AxisListType

P = 128
D, SEQ, DEC, PAST, PAGE = 2048, 256, 8, 2048, 128
T = SEQ + DEC
NH, NKV, DH = 16, 4, 128
GRP = NH // NKV
IDXH, IDXD = 16, 64
DFF, CHUNK, CONVW = 5632, 64, 4
KD, KF = D // P, DFF // P
PAGES = PAST // PAGE
TOPK_P, TOPK_S = min(256, SEQ // 4), min(256, (PAST + 1) // 4)
THETA = 500000.0
ALPHA = 2.0 ** 0.25
SCALE = DH ** -0.5
LN_EPS, NORM_EPS = 1e-5, 1e-6
RING, CRING, AHEAD = 4, 2, 2
QD = KF // 4
U_UP1 = 0
U_DN1 = U_UP1 + 2 * KF
U_MISC = U_DN1 + 4 * KD
U_IDXQ = U_MISC + 1
U_K = U_IDXQ + 8
U_V = U_K + 4
U_Q = U_V + 4
U_GATE = U_Q + NH
U_HEAD = U_GATE + 2 * KD
U_WO = U_HEAD + 4 * NH
U_UP2 = U_WO + KD
U_DN2 = U_UP2 + 2 * KF
T_DN1 = 0
T_MISC = T_DN1 + KD
T_IDXQ = T_MISC + 1
T_K = T_IDXQ + 8
T_V = T_K + 4
T_Q = T_V + 4
T_GATE = T_Q + NH
T_HEAD = T_GATE + 2 * KD
T_WO = T_HEAD + 4 * NH
T_DN2 = T_WO + KD
R_W, R_A, R_B = IDXD, IDXD + IDXH, IDXD + IDXH + NH
C_KI, C_K, C_V = 0, DEC, DEC + 4 * DEC
NEG, GONE = -1e38, -3e38
OFF = 1e30
LEVELS = (2, 4, 8, 16, 32)

TURN = ("mix P P P P P P xt mix2 V w0 P x0 vm V P e0 w1 qk P x1 lift V P w2 soft P outer x2 share P V w3 pt P "
        "x3 added P w4 pv P x4 conv0a P P e1 uw conv0b V c0a P sig0 P c0b silu0 P conv1a c1a P c1b conv1b V P c2a P "
        "sig1 P e2 c2b silu1 V c3a conv2a P c3b conv2b P ss V vout sig2 P ms P norm P P P P e3 sig3 gated").split()
NEXT = {"P", "ss", "norm", *[f"{e}{j}" for e in ("e", "sig") for j in range(4)], "silu0", "silu1",
        *[f"conv{j}{c}" for j in range(3) for c in "ab"]}
LAST_TURN = ("mix V V V V V V xt V V mix2 w0 x0 attend vm w1 W qk x1 lift W w2 soft outer x2 share W w3 pt W x3 added w4 "
             "pv W x4 W uw W c0a W c0b c1a W c1b c2a W c2b c3a c3b vout ms gated").split()
W_PART = (NH - 1) // 5
FIRST = ("e0 e1 conv0a conv0b conv1a conv1b sig0 sig1 shift exps silu0 silu1 e2 e3 conv2a conv2b sig2 sum ss "
         "norm divide sig3").split()
assert TURN.count("P") == 2 * KD and TURN.count("V") == 8
SOLVE_W, SOLVE_X = [f"w{n}" for n in range(5)], [f"x{n}" for n in range(5)]
CHUNKS_A, CHUNKS_B = [f"c{n}a" for n in range(4)], [f"c{n}b" for n in range(4)]


def in_turn(*names):
    return [e for e in TURN if e in names]


BY_PE = in_turn("mix", "qk", "xt", "outer", "pt", "pv", "uw", "ms", *SOLVE_W, *SOLVE_X, *CHUNKS_A, *CHUNKS_B)
BY_DVE = in_turn("mix", "mix2", "share", "added", "pv", "vout", "uw", "gated", *SOLVE_X, *CHUNKS_B)
BY_ACT = ["eg", "ktok", "decay"] + in_turn("soft", "pt", "xt", "uw", "c3b", "ms", *SOLVE_W, *CHUNKS_A)
ASKS = ["decay", "soft"]
ASKS_NEXT = ["conv0", "conv1", "conv2"]
DONE_NEXT = in_turn("sig0", "sig1", "sig2", "ss")

assert all([e for e in LAST_TURN if e in by] == by for by in (BY_PE, BY_DVE)) and LAST_TURN.count("W") == 10

BESIDE, SCORES = [], 2 * IDXH
for j in range(1, 2 * NKV):
    for c in range(8):
        BESIDE.append(("part", j, c))
        s0, s1 = (((j - 1) * 8 + c + d) * SCORES // (8 * (2 * NKV - 1)) for d in (0, 1))
        BESIDE += [("score", n, 0) for n in range(s0, s1)]
    BESIDE.append(("tile", j, 0))


def count(names, name, h):
    return h * len(names) + (names.index(name) + 1)


CONSTS = ["ident", "ones", "lv1", "lv2", "lv4", "lv8", "lv16", "lv32", "incl"]
EARLY = ["cumul", "whole", "dup", "rotdup", "roth", "roti", "spread"]


def host_constants():
    i, j = np.meshgrid(np.arange(P), np.arange(P), indexing="ij")
    same = (i // CHUNK) == (j // CHUNK)
    m = {"ident": i == j, "ones": i >= 0}
    for lv in (1, 2, 4, 8, 16, 32):
        m[f"lv{lv}"] = (i // (2 * lv) == j // (2 * lv)) & (i // lv % 2 == 1) & (j // lv % 2 == 0)
    m["incl"] = same & (j >= i)
    m["cumul"] = same & (i <= j)
    m["whole"] = same
    m["dup"] = (i < IDXD) & (j % IDXD == i)
    m["spread"] = i == R_W + j % IDXH
    m = {k: v.astype(np.float32) for k, v in m.items()}

    def rot(dim, half):
        r = np.zeros((P, P), np.float32)
        for b in range(0, P, dim):
            for k in range(half):
                r[b + half + k, b + k] = -1.0
                r[b + k, b + half + k] = 1.0
        return r

    m["roth"], m["roti"] = rot(DH, DH // 8), rot(IDXD, IDXD // 8)
    m["rotdup"] = m["dup"] @ m["roti"]
    mats = np.stack([m[k] for k in CONSTS], 1)
    early = np.stack([m[k] for k in EARLY], 1)
    pos = np.concatenate([np.arange(SEQ), np.full(DEC, PAST)]).astype(np.float32)

    def tables(dim, half):
        inv = (np.float32(THETA) ** (-np.arange(half, dtype=np.float32) / half)).astype(np.float32)
        ang = pos[None, :] * inv[:, None]
        c, s = np.ones((P, T), np.float32), np.zeros((P, T), np.float32)
        for b in range(0, P, dim):
            for o in (0, half):
                c[b + o:b + o + half] = np.cos(ang)
                s[b + o:b + o + half] = np.sin(ang)
        return c, s

    rope = np.stack([*tables(DH, DH // 8), *tables(IDXD, IDXD // 8)], 1)
    t = np.arange(P)[:, None]
    caus = np.concatenate([t >= np.arange(P)[None], t + P >= np.arange(2 * P)[None]], 1).astype(np.float32)
    own = (np.arange(P)[:, None] // IDXH == np.arange(DEC)[None]).astype(np.float32)
    rowm = np.zeros((P, 3), np.float32)
    rowm[R_W:R_W + IDXH, 0] = (IDXH ** -0.5) * (IDXD ** -0.5)
    rowm[R_A:R_A + NH, 1] = 1.0
    rowm[R_B:R_B + NH, 2] = 1.0
    eps = np.tile(np.array([[LN_EPS, NORM_EPS] + [1 / (k + 1) for k in range(KD)]], np.float32), (P, 1))
    return {"c_mats": mats.reshape(P, -1), "c_early": early.reshape(P, -1), "c_rope": rope.reshape(P, -1), "c_caus": caus,
            "c_own": own, "c_rowm": rowm, "c_eps": eps}


def build(nc, din, dout):
    with ExitStack() as ctx:
        def sb(name, shape, dt=F32):
            return ctx.enter_context(nc.sbuf_tensor(name, shape, dt))

        sems = {}

        def S(name):
            if name not in sems:
                sems[name] = ctx.enter_context(nc.semaphore(name))
            return sems[name]

        wring = sb("wring", [P, RING, KD * P])
        cring = sb("cring", [P, CRING, KD * P])
        xT = sb("xT", [P, KD, T])
        big = sb("big", [P, KF * T])
        gates = sb("gates", [P, 2, KD, T])
        gA, gB = gates[:, 0], gates[:, 1]
        hT = big[:, :].rearrange("p (k t) -> p k t", k=KF)
        at = [0]

        def part(n):
            a = big[:, at[0]:at[0] + n]
            at[0] += n
            return a

        qT = part(NH * T).rearrange("p (h t) -> p h t", h=NH)
        kT = part(NKV * T).rearrange("p (h t) -> p h t", h=NKV)
        vT = part(NKV * T).rearrange("p (h t) -> p h t", h=NKV)
        vtok = part(2 * NKV * DH).rearrange("p (s d) -> p s d", s=2)
        low = at[0]
        qiT = part(8 * T).rearrange("p (j t) -> p j t", j=8)
        zq = part(DEC * P).rearrange("p (b c) -> p b c", b=DEC)
        assert at[0] <= KF * T
        at[0] = low
        y3 = part(3 * T).rearrange("p (j t) -> p j t", j=3)
        e4 = part(4 * T).rearrange("p (j t) -> p j t", j=4)
        sq = part(2 * SEQ + 24)
        rs = part(2 * SEQ + 16)
        dab = part(4 * P)
        oS = part(NH * NH).rearrange("p (u n) -> p u n", u=NH)
        sgs = part(2 * NH * DEC).rearrange("p (k h b) -> p k h b", k=2, h=NH)
        pn, rin = (part(DEC * NH).rearrange("p (b n) -> p b n", b=DEC) for _ in range(2))
        assert at[0] <= KF * T, at[0]
        pool = sb("pool", [P, 2 * (PAST + 8)])
        rl = pool[:, 0:PAST + 1]
        scS = pool[0:DEC, PAST + 8:2 * PAST + 9]
        at2 = [0]

        def part2(n):
            a = pool[:, at2[0]:at2[0] + n]
            at2[0] += n
            return a

        qkn = part2(2 * SEQ)
        kbe, kd, vb = (part2(2 * P).rearrange("p (a b) -> p a b", a=2) for _ in range(3))
        lf, lm0, lm1, qkt, wt = (part2(2 * P).rearrange("p (a b) -> p a b", a=2) for _ in range(5))
        lm = (lm0, lm1)
        xx = part2(4 * P).rearrange("p (x a b) -> p x a b", x=2, a=2)
        eg, qe, nwt = part2(2 * P), part2(2 * P), part2(2 * P)
        assert at2[0] <= 2 * (PAST + 8), at2[0]
        knT = part2(P)[0:DEC]
        turn = sb("turn", [P, 2608])
        at3 = [0]

        def part3(n):
            a = turn[:, at3[0]:at3[0] + n]
            at3[0] += n
            return a

        rope = part3(4 * T).rearrange("p (a t) -> p a t", a=4)
        caus, pscore = part3(3 * P), part3(3 * P)
        msc, val = part3(T), part3(T)
        valk = part3(2 * P).rearrange("p (a b) -> p a b", a=2)
        assert at3[0] == 2608
        at3[0] = 0
        dg, vh = (part3(2 * P).rearrange("p (a b) -> p a b", a=2) for _ in range(2))
        qh, sm, pT = part3(2 * P), part3(3 * P), part3(3 * P)
        vn, St = part3(P), part3(P)
        ob, zs, osq = part3(T), part3(T), part3(T)
        assert at3[0] <= 2608
        rms, zraw = sb("rms", [P, T]), sb("zraw", [P, T])
        raw = sb("raw", [P, 3, SEQ + CONVW - 1])
        sst = sb("sst", [P, DEC, P])
        early = sst[:, 0:len(EARLY), :]
        vm = e4.rearrange("p j t -> p (j t)")[0:DEC, 0:DEC * P].rearrange("p (b e) -> p b e", b=DEC)
        sal = sb("sal", [P, 4 * DEC, 4, NH])
        mats = sb("mats", [P, len(CONSTS), P])
        M = {k: mats[:, n, :] for n, k in enumerate(CONSTS)}
        M.update({k: early[:, n, :] for n, k in enumerate(EARLY)})
        own, rowm, epsc = sb("own", [P, DEC]), sb("rowm", [P, 3]), sb("epsc", [P, 2 + KD])
        lnp = sb("lnp", [P, 6, KD])
        cw = sb("cw", [P, NH, 12])
        cs = sb("cs", [P, NH, 3, CONVW, DEC])
        cpb = sb("cpb", [P, NH, 3, CONVW - 1])
        gnorm, alog, dtb = sb("gnorm", [P, 1]), sb("alog", [P, 1]), sb("dtb", [P, 1])
        pt = sb("pt", [1, DEC * PAGES], I32)
        raw2 = sb("raw2", [P, 2, T])
        tmp = sb("tmp", [P, T])
        kiT = sb("kiT", [P, T])
        gsc = sb("gsc", [P, NH, 4, 2])
        w8 = sb("w8", [P, DEC])
        pbias = sb("pbias", [P, 3 * P])
        top8 = sb("top8", [P, 8])
        mbt = sb("mbt", [P, DEC, PAGES])
        nbt = sb("nbt", [P, DEC])
        sn, gmx = (sb(n, [P, DEC, NH]) for n in ("sn", "gmx"))
        hc, hw = sb("hc", [P, 4, 2]), sb("hw", [P, 12])
        hg = sb("hg", [P, 2, DEC])
        kq = sb("kq", [P, 2, DEC])
        s8 = sb("s8", [P, 6, DEC])
        at_s = sb("at_s", [P, 6])
        mean, rstd = tmp, rms
        m1, m2, dev, dev2 = (gB[:, k, :] for k in range(4))
        bank = [ctx.enter_context(nc.psum_tensor(f"bank{i}", [P, 512], F32)) for i in range(8)]
        acc = bank[0:2]
        gT, gK, gG, gO, aS, aV = bank[2:8]
        upb = [(bank[0], bank[1]), (bank[2], bank[3])]
        sg = raw2

        ki_dram = nc.dram_tensor("ki_ordered", (DEC, P, PAST), F32, kind="Internal").ap()

        block = ctx.enter_context(nc.Block())

        class Own:

            def __init__(self, eng, sem):
                self.eng, self.sem, self.base, self.k, self.it, self.per = eng, sem, 0, 0, 0, 0

            def __call__(self, ins, lag=0):
                ins.then_inc(self.sem, 1)
                self.k += 1
                self.eng.wait_ge(self.sem, self.it * self.per + (self.base + self.k - lag))

            def enter(self, it, per):
                self.base, self.k, self.it, self.per = self.base + self.k, 0, it, per

            def leave(self, n):
                assert self.k == self.per, (self.k, self.per)
                self.base, self.k, self.it, self.per = self.base + n * self.per, 0, 0, 0

        def unit_done(eng, n, it=0, per=0):
            eng.wait_ge(S("units_done"), it * per + (n + 1))

        def landed(eng, n0, it=0, per=4):
            eng.wait_ge(S(f"weights_in{n0 % RING}"), (it * (per // RING) + (n0 // RING + 1)) * 16)

        def multiplied(eng, h, name):
            eng.wait_ge(S("multiplied"), count(BY_PE, name, h))

        def answered(eng, h, name):
            eng.wait_ge(S("answered"), count(BY_DVE, name, h))

        def act_done(eng, h, name):
            eng.wait_ge(S("act_done"), count(BY_ACT, name, h))

        def act_done_next(eng, g, name):
            eng.wait_ge(S("act_done_next"), count(DONE_NEXT, name, g))

        def pages_landed(eng, c0, it=0, per=2, dmas=4):
            n = c0 // CRING + 1
            ki = DEC // CRING
            eng.wait_ge(S(f"pages_in{c0 % CRING}"),
                        (it * (per // CRING) * dmas + (n if c0 < C_K else ki + (n - ki) * dmas)) * 16)

        def centre(eng, k):
            return eng.tensor_tensor(xT[:, k:k + 4, :], xT[:, k:k + 4, :], mean[:, :].unsqueeze(1).to_broadcast([P, 4, T]),
                                     ALU.subtract)

        @block.sync
        def _(sp):
            small = [(mats[:, :, :], "c_mats"), (early, "c_early"), (rope, "c_rope"), (caus, "c_caus"),
                     (own[:, :], "c_own"), (rowm[:, :], "c_rowm"), (epsc[:, :], "c_eps"),
                     (lnp[:, :, :], "lnp"), (cw[:, :, :], "cw"),
                     (gnorm[:, :], "gnorm"), (alog[:, :], "alog"), (dtb[:, :], "dtb")]

            def weights(n0, u, it, per, src, w=KD * P):
                if n0 + u >= RING:
                    sp.wait_ge(S("units_done"), it * per + (n0 + u + 1 - RING))
                sp.dma_start(wring[:, (n0 + u) % RING, 0:w], src).then_inc(S(f"weights_in{(n0 + u) % RING}"), 16)

            def ffn_loads(n_up, n_dn, up, dn):
                with sp.Fori(0, 2 * KF // 4) as i:
                    for u in range(4):
                        weights(n_up, u, i, 4, up[i * 4 + u])
                with sp.Fori(0, KD // 2) as i:
                    for u in range(8):
                        weights(n_dn, u, i, 8, dn[i * 8 + u], QD * P)

            def x_in(c):
                k = slice(c * KD // 4, (c + 1) * KD // 4)
                sp.dma_start(xT[:, k, :], din["xT"].rearrange("p (k t) -> p k t", k=KD)[:, k, :]).then_inc(S(f"x_in{c}"), 16)

            x_in(0)
            weights(U_UP1, 0, 0, 4, din["up1"][0])
            for c in range(1, 4):
                x_in(c)
            for u in range(1, 4):
                weights(U_UP1, u, 0, 4, din["up1"][u])
            for dst, name in small:
                s = din[name]
                if len(dst.shape) == 3:
                    s = s.rearrange("p (a b) -> p a b", a=dst.shape[1])
                sp.dma_start(dst, s).then_inc(S("small_in"), 16)
            for h in range(NH):
                sp.dma_start(cs[:, h, :, 0:CONVW - 1, :],
                             din["convs"][:, h].rearrange("p j (t b) -> p j t b", b=DEC)).then_inc(S("small_in"), 16)
            sp.dma_start(pt[:, :], din["pt"]).then_inc(S("table_in"), 16)
            with sp.Fori(0, 2 * KF // 4 - 1) as i:
                for u in range(4):
                    weights(U_UP1 + 4, u, i, 4, din["up1"][i * 4 + (u + 4)])
            with sp.Fori(0, KD // 2) as i:
                for u in range(8):
                    weights(U_DN1, u, i, 8, din["dn1"][i * 8 + u], QD * P)

            w_in = din["w_in"]

            def pages(c0, it, per, first, dmas, cache, width):
                if c0 >= CRING:
                    sp.wait_ge(S("page_units_done"), it * per + (c0 + 1 - CRING))
                for g in range(dmas):
                    page = sp.value_load(pt[0:1, bass.ds(first + g, 1)], min_val=0, max_val=cache.shape[0] - 1)
                    sp.dma_start(cring[:, c0 % CRING, g * width:(g + 1) * width], cache[page]).then_inc(
                        S(f"pages_in{c0 % CRING}"), 16)

            weights(U_MISC, 0, 0, 0, w_in[0])
            with sp.Fori(0, 2) as i:
                for u in range(4):
                    weights(U_IDXQ, u, i, 4, w_in[i * 4 + (U_IDXQ - U_MISC + u)])
            sp.wait_ge(S("table_in"), 16)
            sp.wait_ge(S("keys_ordered"), DEC * PAGES * 16)
            for b in range(DEC):
                if b >= CRING:
                    sp.wait_ge(S("page_units_done"), b + 1 - CRING)
                sp.dma_start(cring[:, b % CRING, :], ki_dram[b]).then_inc(S(f"pages_in{b % CRING}"), 16)
                if b == CRING - 1:
                    for u in range(4):
                        weights(U_K, u, 0, 0, w_in[U_K - U_MISC + u])
            with sp.Fori(0, (NKV + NH) // 4) as i:
                for u in range(4):
                    weights(U_V, u, i, 4, w_in[i * 4 + (U_V - U_MISC + u)])
            sp.wait_ge(S("kv_ready"), 3)
            sp.dma_start(dout["kT"].rearrange("p (a b) -> p a b", a=NKV), kT).then_inc(S("stored"), 16)
            sp.dma_start(dout["vT"].rearrange("p (a b) -> p a b", a=NKV), vT).then_inc(S("stored"), 16)
            sp.dma_start(dout["kiT"], kiT[0:IDXD, :]).then_inc(S("stored"), 16)
            for u in range(AHEAD):
                weights(U_GATE, u, 0, 0, w_in[U_GATE - U_MISC + u])
            with sp.Fori(0, DEC) as i:
                for u in range(4):
                    weights(U_GATE + AHEAD, u, i, 4, w_in[i * 4 + (U_GATE + AHEAD - U_MISC + u)])
                    pages(C_K + u, i, 4, i * PAGES + 4 * u, 4, din["ck"], NKV * DH)
            for u in range(AHEAD, 4):
                weights(U_HEAD, u, 0, 0, w_in[U_HEAD - U_MISC + u])
            for u in range(AHEAD):
                weights(U_HEAD + 4, u, 0, 0, w_in[U_HEAD + 4 - U_MISC + u])
            with sp.Fori(0, NH - 2) as i:
                for u in range(4):
                    weights(U_HEAD + 4 + AHEAD, u, i, 4, w_in[i * 4 + (U_HEAD + 4 + AHEAD - U_MISC + u)])
                    if u % 2 == 0:
                        pages(C_V + u // 2, i, 2, i * 8 + 4 * (u // 2), 4, din["cv"], NKV * DH)
            for u in range(AHEAD, 4):
                weights(U_HEAD + 4 * (NH - 1), u, 0, 0, w_in[U_HEAD + 4 * (NH - 1) - U_MISC + u])
                pages(C_V + 2 * (NH - 2) + u - AHEAD, 0, 0, 4 * (2 * (NH - 2) + u - AHEAD), 4, din["cv"], NKV * DH)
            for c in range(2 * (NH - 1), 2 * NH):
                pages(C_V + c, 0, 0, 4 * c, 4, din["cv"], NKV * DH)
            with sp.Fori(0, KD // 4) as i:
                for u in range(4):
                    weights(U_WO, u, i, 4, din["w_o"][i * 4 + u])
            ffn_loads(U_UP2, U_DN2, din["up2"], din["dn2"])
            sp.wait_ge(S("head_over"), NH)
            sp.dma_start(dout["convp"], cpb[:, :, :, :].rearrange("p h j t -> p (h j t)")).then_inc(S("stored"), 16)
            sp.dma_start(dout["convs"], cs[:, :, :, :, :].rearrange("p h j t b -> p (h j t b)")).then_inc(S("stored"), 16)
            for k in range(KD):
                sp.wait_ge(S("y_out_ready"), k + 1)
                sp.dma_start(dout["yT"][:, k * T:(k + 1) * T], xT[:, k, :]).then_inc(S("stored"), 16)
            sp.wait_ge(S("stored"), (5 + KD) * 16)

        @block.gpsimd
        def _(pool_e):
            def state_in(h):
                pool_e.dma_start(sst[:, :, :], din["ssm"][h]).then_inc(S("state_in"), 16)

            def state_steps(h, more):
                multiplied(pool_e, h, "mix")
                pool_e.tensor_tensor(sst[:, :, :], sst[:, :, :], hg[:, 0, :].unsqueeze(2).to_broadcast([P, DEC, P]),
                                     ALU.mult).then_inc(S("state_scaled"), 1)
                answered(pool_e, h, "added")
                pool_e.dma_start(dout["ssm_s"][h], sst[:, :, :]).then_inc(S("state_out"), 16)
                pool_e.wait_ge(S("state_out"), h * 16 + 16)
                if more:
                    state_in(h + 1)
                answered(pool_e, h, "c3b")
                pool_e.dma_start(dout["ssm_p"][h], St[:, :]).then_inc(S("prompt_state_out"), 16)
                pool_e.wait_ge(S("prompt_state_out"), h * 16 + 16)
                pool_e.sem_inc(S("prompt_state_free"), 1)

            def centre_half(n):
                pool_e.wait_ge(S("moments"), 3 * n + 3)
                for k in (8, 12):
                    centre(pool_e, k).then_inc(S("centred"), 1)

            pool_e.sem_inc(S("prompt_state_free"), 1)
            pool_e.wait_ge(S("table_in"), 16)
            with pool_e.Fori(0, DEC) as b:
                for g in range(PAGES):
                    page = pool_e.value_load(pt[0:1, bass.ds(b * PAGES + g, 1)], min_val=0, max_val=din["cki"].shape[0] - 1)
                    pool_e.dma_start(ki_dram[b, :, g * PAGE:(g + 1) * PAGE], din["cki"][page]).then_inc(S("keys_ordered"), 16)
            centre_half(0)
            pool_e.wait_ge(S("part_max"), 1)
            pool_e.partition_all_reduce(gmx[:, :, :].rearrange("p b n -> p (b n)"),
                                        gmx[:, :, :].rearrange("p b n -> p (b n)"), P,
                                        bass.bass_isa.ReduceOp.max).then_inc(S("all_max"), 1)
            state_in(0)
            with pool_e.Fori(0, NH - 1) as h:
                state_steps(h, True)
            state_steps(NH - 1, False)
            centre_half(1)
            centre_half(2)

        @block.tensor
        def _(pe):
            mm = pe.matmul

            def unit(n0, u, it, per, rhs, out, nk=KD, first=True, last=True, lo=0, hi=None, after=None):
                slot = (n0 + u) % RING
                hi = nk if hi is None else hi
                if lo == 0:
                    landed(pe, n0 + u, it, per)
                for k in range(lo, hi):
                    if after == "load" and k % 4 == 0:
                        pe.wait_ge(S(f"x_in{k // 4}"), 16)
                    elif after in (0, 1):
                        pe.wait_ge(S("x_ready"), after * KD + k + 1)
                    ins = mm(out, wring[:, slot, k * P:(k + 1) * P], rhs(k),
                             start=first and k == 0, stop=last and k == nk - 1)
                if hi == nk:
                    ins.then_inc(S("units_done"), 1)

            def tile(n0, t0, u, it, per, rhs, lo=0, hi=KD, after=None):
                a = acc[(t0 + u) % 2]
                if lo == 0:
                    pe.wait_ge(S("acc_free"), it * per + (t0 + u + 1))
                unit(n0, u, it, per, rhs, a[:, 0:T], lo=lo, hi=hi, after=after)

            def ffn_up(n_up, base, after=None):
                def two_pairs(i, p0, after=None):
                    for f in range(2):
                        g, up = upb[f]
                        pe.wait_ge(S("pair_free"), i * 2 + (base + p0 + f + 1))
                        unit(n_up + 2 * p0, 2 * f, i, 4, lambda k: xT[:, k, :], g[:, 0:T], after=after if f == 0 else None)
                        unit(n_up + 2 * p0, 2 * f + 1, i, 4, lambda k: xT[:, k, :], up[:, 0:T])

                two_pairs(0, 0, after)
                with pe.Fori(0, KF // 2 - 1) as i:
                    two_pairs(i, 2)

            def ffn_down(n_dn, t0, base):
                pe.wait_ge(S("pair_free"), base + KF + 2)
                with pe.Fori(0, KD // 2) as i:
                    for c in range(2):
                        pe.wait_ge(S("acc_free"), i * 2 + (t0 + c + 1))
                        for q in range(4):
                            unit(n_dn, 4 * c + q, i, 8, lambda k, q=q: hT[:, QD * q + k, :],
                                 acc[(t0 + c) % 2][:, 0:T], nk=QD, first=q == 0, last=q == 3)

            def norm(n):
                pe.wait_ge(S("moments"), 3 * n + 1)
                mm(gG[:, 0:T], M["ones"], m1, start=True, stop=True).then_inc(S("stat"), 1)
                mm(gO[:, 0:T], M["ones"], m2, start=True, stop=False)
                pe.wait_ge(S("moments"), 3 * n + 2)
                mm(gO[:, 0:T], M["ones"], dev2, start=False, stop=True).then_inc(S("stat"), 1)

            ffn_up(U_UP1, 0, after="load")
            ffn_down(U_DN1, T_DN1, 0)
            pe.wait_ge(S("small_in"), 16 * 28)
            norm(0)

            x = lambda k: xT[:, k, :]
            tile(U_MISC, T_MISC, 0, 0, 0, x, after=0)
            pe.wait_ge(S("misc_raw"), 1)
            mm(gT[:, 0:T], M["dup"], msc[:, :], start=True, stop=True)
            mm(gK[:, 0:T], M["rotdup"], msc[:, :], start=True, stop=True).then_inc(S("ki_rot"), 1)

            def rotate(r, it, m):
                pe.wait_ge(S("raw_ready"), it + (r + 1))
                pe.wait_ge(S("rope_free"), it + (r + 1))
                mm([gT, gK][r % 2][:, 0:T], m, raw2[:, r % 2, :], start=True, stop=True).then_inc(S("rotated"), 1)

            with pe.Fori(0, 2) as i:
                for u in range(4):
                    tile(U_IDXQ, T_IDXQ, u, i, 4, x)
                    if u == 1:
                        pe.wait_ge(S("ki_ready"), 1)
                    if u:
                        rotate(u - 1, i * 4, M["roti"])
                rotate(3, i * 4, M["roti"])
            pe.wait_ge(S("val_ready"), 1)
            for t in range(2):
                ins = pe.transpose(gG[:, t * P:(t + 1) * P], val[:, t * P:(t + 1) * P], M["ident"])
            ins.then_inc(S("val_turned"), 1)
            pe.wait_ge(S("picked"), 1)
            mm(gO[:, 0:2 * NH * DEC], M["ones"], rms[:, 0:2 * NH * DEC], start=True, stop=True)
            mm(gO[:, 256:256 + DEC], M["spread"], val[:, SEQ:T], start=True, stop=True).then_inc(S("rows_done"), 1)
            pe.wait_ge(S("valk_ready"), 1)
            pe.wait_ge(S("rope_free"), 2 + 8)
            for t in range(2):
                mm(gK[:, 32 * t:32 * t + 16], M["cumul"], valk[:, t, R_A:R_A + NH], start=True, stop=True)
                ins = mm(gK[:, 32 * t + 16:32 * t + 32], M["whole"], valk[:, t, R_A:R_A + NH], start=True, stop=True)
            ins.then_inc(S("decays"), 1)
            tile(U_K, T_K, 0, 0, 0, x, hi=10)
            idx = [gT, gK, gG, gO]
            pe.wait_ge(S("zq_ready"), 1)
            pe.wait_ge(S("decays_read"), 1)
            for b in range(DEC):
                pages_landed(pe, C_KI + b)
                for c in range(4):
                    mm(idx[c][:, :], zq[:, b, :], cring[:, b % CRING, c * 512:(c + 1) * 512],
                       start=b == 0, stop=b == DEC - 1)
                ins = mm(aS[:, 0:1], zq[:, b, :], kiT[:, SEQ + b:SEQ + b + 1], start=b == 0, stop=b == DEC - 1)
                ins.then_inc(S("page_units_done"), 1)
                if b in (1, 3, 5):
                    tile(U_K, T_K, 0, 0, 0, x, lo=9 + b, hi=11 + b)
            for c in range(4):
                pe.wait_ge(S("rectified"), c + 1)
                mm(idx[c][0:DEC, :], w8[:, :], rl[:, c * 512:(c + 1) * 512], start=True, stop=True).then_inc(S("weighed"), 1)
            pe.wait_ge(S("rectified"), 5)
            mm(aS[0:DEC, 0:1], w8[:, :], rl[:, PAST:PAST + 1], start=True, stop=True).then_inc(S("weighed"), 1)
            pe.wait_ge(S("scored"), 5)
            def turned(u):
                pe.wait_ge(S("v_raw"), u + 1)
                for t in range(2):
                    ins = pe.transpose([gG, gO][t][:, u * P:(u + 1) * P], vT[:, u, t * P:(t + 1) * P], M["ident"])
                return ins

            for e, j, c in BESIDE:
                if e == "part":
                    tile(U_K, T_K, j, 0, 0, x, lo=2 * c, hi=2 * c + 2)
                elif e == "score":
                    h, t = j // 2, j % 2
                    w, r0 = (t + 1) * P, IDXD * (h % 2)
                    pe.wait_ge(S("pidx_free"), j + 1)
                    mm([aS, aV][t][:, 0:w], qiT[r0:r0 + IDXD, h // 2, t * P:(t + 1) * P], kiT[r0:r0 + IDXD, 0:w],
                       start=True, stop=True).then_inc(S("pidx_done"), 1)
                elif j <= NKV:
                    rotate(8 + j - 1, 0, M["roth"])
                else:
                    turned(j - NKV - 1)
            turned(NKV - 1).then_inc(S("v_turned"), 1)
            pe.wait_ge(S("pidx_free"), 2 + SCORES)
            with pe.Fori(0, 4) as i:
                for u in range(4):
                    tile(U_Q, T_Q, u, i, 4, x)
                    if u:
                        rotate(12 + u - 1, i * 4, M["roth"])
                rotate(15, i * 4, M["roth"])
            with pe.Fori(0, DEC) as i:
                for u in range(4):
                    tile(U_GATE, T_GATE, u, i, 4, x)
                    if u == 0:
                        pe.wait_ge(S("rope_free"), 2 + 28)
                    pages_landed(pe, C_K + u, i, 4)
                    pe.wait_ge(S("kscore_free"), i * 4 + (u + 1))
                    for g in range(4):
                        for kv in range(NKV):
                            o = g * NH + kv * GRP
                            ins = mm([aS, aV][u % 2][:, o:o + GRP],
                                     cring[:, u % CRING, (g * NKV + kv) * P:(g * NKV + kv + 1) * P],
                                     qT[:, kv * GRP:(kv + 1) * GRP, bass.ds(i + SEQ, 1)], start=True, stop=True)
                    ins.then_inc(S("page_units_done"), 1)
            pe.wait_ge(S("selected"), 1)
            for g in range(PAGES):
                ins = pe.transpose(gT[:, g * DEC:(g + 1) * DEC], scS[:, g * PAGE:(g + 1) * PAGE], M["ident"][0:DEC, 0:DEC])
            mm(gK[:, 0:DEC], M["ones"][0:DEC, :], s8[0:DEC, 0, :], start=True, stop=True)
            ins = mm(gG[:, 0:DEC * NH], M["ones"], sn[:, :, :].rearrange("p b n -> p (b n)"), start=True, stop=True)
            ins.then_inc(S("masks_turned"), 1)
            for u in range(4):
                tile(U_HEAD, T_HEAD, u, 0, 0, x)

            def norms(g):
                pe.wait_ge(S("squared"), g + 1)
                mm(gT[:, :], M["ones"], sq[:, 0:2 * SEQ], start=True, stop=True)
                mm(aS[:, 0:24], M["ones"], sq[:, 2 * SEQ:2 * SEQ + 24], start=True, stop=True).then_inc(S("summed"), 1)

            def step(h, e, v=0, last=False):
                if e == "mix":
                    pe.wait_ge(S("normalized"), h + 1)
                    pe.wait_ge(S("state_in"), h * 16 + 16)
                    mm(gG[:, 0:2 * P], M["ones"], dg.rearrange("p a b -> p (a b)"), start=True, stop=True)
                    for b in range(DEC):
                        mm(gG[:, 256 + 2 * b:258 + 2 * b], sst[:, b, :], kq[:, :, b], start=True, stop=True)
                    pe.transpose(gG[0:DEC, 384:512], kq[:, 0, :], M["ident"])
                    for p in range(2):
                        c = slice(p * P, (p + 1) * P)
                        pe.transpose(gT[:, c], qkn[:, SEQ + p * P:SEQ + (p + 1) * P], M["ident"])
                        pe.transpose(gT[:, SEQ + p * P:SEQ + (p + 1) * P], y3[:, 2, c], M["ident"])
                    for p in range(2):
                        kn = qkn[:, SEQ + p * P:SEQ + (p + 1) * P]
                        mm(gK[:, p * P:(p + 1) * P], kn, kn, start=True, stop=True)
                        ins = mm(gK[:, SEQ + p * P:SEQ + (p + 1) * P], kn, qkn[:, p * P:(p + 1) * P], start=True, stop=True)
                elif e == "qk":
                    pe.wait_ge(S("head_copied"), h + 1)
                    mm(aS[:, 0:P], qh[:, 0:P], kT[:, h // GRP, 0:P], start=True, stop=True)
                    ins = mm(aS[:, P:3 * P], qh[:, P:2 * P], kT[:, h // GRP, 0:2 * P], start=True, stop=True)
                elif e == "pt":
                    answered(pe, h, "share")
                    for s in range(3):
                        ins = pe.transpose(aS[:, s * P:(s + 1) * P], sm[:, s * P:(s + 1) * P], M["ident"])
                elif e == "pv":
                    act_done(pe, h, "pt")
                    mm(aS[:, 0:P], vh[:, 0, :], pT[:, 0:P], start=True, stop=True)
                    mm(aS[:, P:2 * P], vh[:, 0, :], pT[:, P:2 * P], start=True, stop=False)
                    ins = mm(aS[:, P:2 * P], vh[:, 1, :], pT[:, 2 * P:3 * P], start=False, stop=True)
                elif e == "V":
                    u, g = v // 4, v % 4
                    if v == 0 and not last:
                        pe.wait_ge(S("sample_soft"), 1)
                        answered(pe, h, "mix")
                    if g == 0:
                        pages_landed(pe, C_V + u, h, 2)
                    for kv in range(NKV):
                        ins = mm(aV[:, kv * GRP:(kv + 1) * GRP], cring[:, u, (g * NKV + kv) * P:(g * NKV + kv + 1) * P],
                                 sal[:, 2 * h + u, g, kv * GRP:(kv + 1) * GRP],
                                 start=v == 0 and kv == 0, stop=v == 7, skip_group_check=True)
                    if g == 3:
                        ins.then_inc(S("page_units_done"), 1)
                    return
                elif e == "xt":
                    answered(pe, h, "mix")
                    act_done(pe, h, "ktok")
                    for p in range(2):
                        pe.transpose(gT[:, p * P:(p + 1) * P], xx[:, 0, p, :], M["ident"])
                    ins = pe.transpose(gT[0:DEC, 256:384], s8[:, 1, :], M["ident"])
                elif e == "outer":
                    pe.wait_ge(S("vm_ready"), h + 1)
                    mm(gT[:, :], knT[:, :], vm[:, 0:4, :].rearrange("p a b -> p (a b)"), start=True, stop=True)
                    ins = mm(gO[:, :], knT[:, :], vm[:, 4:8, :].rearrange("p a b -> p (a b)"), start=True, stop=True)
                elif e in SOLVE_W:
                    n = int(e[1])
                    answered(pe, h, "mix2" if n == 0 else f"x{n - 1}")
                    act_done(pe, h, "xt" if n == 0 else f"w{n - 1}")
                    for p in range(2):
                        ins = mm(gK[:, p * P:(p + 1) * P], lm[n % 2][:, p, :], xx[:, 1, p, :], start=True, stop=True)
                elif e in SOLVE_X:
                    act_done(pe, h, f"w{e[1]}")
                    for p in range(2):
                        if e != SOLVE_X[-1]:
                            mm(gG[:, p * P:(p + 1) * P], wt[:, p, :], xx[:, 0, p, :], start=True, stop=True)
                        ins = mm(gG[:, (2 + p) * P:(3 + p) * P], xx[:, 0, p, :], wt[:, p, :], start=True, stop=True)
                elif e == "uw":
                    answered(pe, h, "x4")
                    for p in range(2):
                        ins = mm(gK[:, p * P:(p + 1) * P], kbe[:, p, :], xx[:, 1, p, :], start=True, stop=True)
                elif e in CHUNKS_A or e in CHUNKS_B:
                    c = int(e[1])
                    p, r0 = c // 2, CHUNK * (c % 2)
                    rows = slice(r0, r0 + CHUNK)
                    if e[2] == "a":
                        answered(pe, h, "uw" if c == 0 else f"c{c - 1}b")
                        if c == 0:
                            act_done(pe, h, "uw")
                        o = gT[rows, c * P:(c + 1) * P]
                        mm(o, xx[:, 1, p, rows], vb[:, p, :], start=True, stop=False)
                        ins = mm(o, nwt[:, c * CHUNK:(c + 1) * CHUNK], St[:, :], start=False, stop=True)
                    else:
                        act_done(pe, h, f"c{c}a")
                        mm(gG[:, 0:P], kd[rows, p, :], vn[rows, :], start=True, stop=True)
                        o = gO[:, c * CHUNK:(c + 1) * CHUNK]
                        mm(o, St[:, :], qe[:, c * CHUNK:(c + 1) * CHUNK], start=True, stop=False)
                        ins = mm(o, vn[rows, :], qkt[rows, p, rows], start=False, stop=True)
                elif e == "ms":
                    act_done(pe, h, "c3b")
                    ins = mm(gK[:, 0:T], M["ones"], osq[:, :], start=True, stop=True)
                ins.then_inc(S("multiplied"), 1)

            norms(0)
            pe.wait_ge(S("expsum"), 1)
            mm(gO[:, 0:DEC * NH], M["ones"], rin[:, :, :].rearrange("p b n -> p (b n)"),
               start=True, stop=True).then_inc(S("denoms"), 1)

            def turn(h, events, last=False):
                n = v = w = 0
                if last:
                    answered(pe, NH - 2, "vout")
                for e in events:
                    if e == "P":
                        tile(U_HEAD + 4, T_HEAD + 4, n // 8, h, 4, x, lo=2 * (n % 8), hi=2 * (n % 8) + 2)
                        n += 1
                    elif e == "ss":
                        answered(pe, h, "pv")
                        norms(h + 1)
                    elif e == "V":
                        step(h, e, v, last)
                        v += 1
                    elif e == "W":
                        if w == 0:
                            pe.wait_ge(S("merged"), 1)
                        lo = W_PART * (w % 5)
                        tile(U_WO, T_WO, w // 5, 0, 0, lambda k: gA[:, k, :], lo=lo, hi=lo + W_PART)
                        w += 1
                    elif e in BY_PE:
                        step(h, e)
                act_done(pe, h, "ms")

            with pe.Fori(0, NH - 1) as h:
                turn(h, TURN)
            turn(NH - 1, LAST_TURN, last=True)
            pe.wait_ge(S("merged"), 2)
            for u in range(4):
                tile(U_WO, T_WO, u, 0, 0, lambda k: gA[:, k, :], lo=NH - 1 if u < 2 else 0)
            with pe.Fori(0, KD // 4 - 1) as i:
                for u in range(4):
                    tile(U_WO + 4, T_WO + 4, u, i, 4, lambda k: gA[:, k, :])
            norm(1)
            ffn_up(U_UP2, KF, after=1)
            ffn_down(U_DN2, T_DN2, KF)
            norm(2)

        @block.scalar
        def _(act):
            do = act.activation
            own_a = Own(act, S("act_own"))

            def silu_gates(n_up, base):
                with act.Fori(0, KF // 2) as i:
                    for f in range(2):
                        unit_done(act, n_up + 2 * f, i, 4)
                        act.wait_ge(S("pair_free"), i * 2 + (base + f + 1))
                        do(sg[:, f, :], upb[f][0][:, 0:T], ACT.Silu).then_inc(S("silu_done"), 1)

            def norm(n):
                act.preload_act_table_set("sqrt_and_others")
                act.wait_ge(S("stat"), 2 * n + 2)
                do(rstd[:, :], gO[:, 0:T], ACT.Sqrt, bias=epsc[:, 0:1], scale=1.0 / D).then_inc(S("deviation"), 1)
                for k in range(KD):
                    act.wait_ge(S("scaled"), n * KD + k + 1)
                    do(xT[:, k, :], xT[:, k, :], ACT.Identity, bias=lnp[:, 2 * n + 1, k:k + 1],
                       scale=lnp[:, 2 * n, k:k + 1]).then_inc(S("x_ready"), 1)
                    if n == 2:
                        act.wait_ge(S("x_ready"), n * KD + k + 1)
                        act.sem_inc(S("y_out_ready"), 1)

            silu_gates(U_UP1, 0)
            act.wait_ge(S("small_in"), 16 * 28)
            norm(0)
            unit_done(act, U_MISC)
            do(msc[:, :], acc[T_MISC % 2][:, 0:T], ACT.Copy).then_inc(S("misc_raw"), 1)
            act.wait_ge(S("misc_raw"), 1)
            act.sem_inc(S("acc_free"), 1)
            own_a(do(raw2[:, 0, :], msc[:, :], ACT.Exp, scale=-1.0))
            act.sem_inc(S("misc_exp"), 1)
            own_a(do(val[:, :], msc[:, :], ACT.Abs, bias=dtb[:, 0:1]))
            own_a(do(val[:, :], val[:, :], ACT.Exp, scale=-1.0))
            own_a(do(val[:, :], val[:, :], ACT.Ln, bias=1.0))
            own_a(do(alog[:, :], alog[:, :], ACT.Exp))
            act.sem_inc(S("misc_exp"), 1)

            def evacuate(n0, t0, u, it, per, outs):
                unit_done(act, n0 + u, it, per)
                a = acc[(t0 + u) % 2]
                for dst, cols, func in outs:
                    own_a(do(dst, a[:, cols], func))
                act.sem_inc(S("acc_free"), 1)

            def raw_tile(n0, t0, r0, u, it):
                act.wait_ge(S("rope_free"), it * 4 + (r0 + u + 1))
                evacuate(n0, t0, u, it, 4, [(raw2[:, (r0 + u) % 2, :], slice(0, T), ACT.Copy)])
                act.sem_inc(S("raw_ready"), 1)

            act.wait_ge(S("ki_ready"), 1)
            with act.Fori(0, 2) as i:
                own_a.enter(i, 4)
                for u in range(4):
                    raw_tile(U_IDXQ, T_IDXQ, 0, u, i)
            own_a.leave(2)
            act.wait_ge(S("val_turned"), 1)
            do(valk[:, :, :], gG[:, 0:2 * P].rearrange("p (a b) -> p a b", a=2), ACT.Copy).then_inc(S("valk_ready"), 1)
            act.wait_ge(S("rows_done"), 1)
            own_a(do(sgs[:, 0, :, :], gO[:, 0:P].rearrange("p (h b) -> p h b", b=DEC), ACT.Exp))
            own_a(do(sgs[:, 1, :, :], gO[:, P:2 * P].rearrange("p (h b) -> p h b", b=DEC), ACT.Copy))
            act.sem_inc(S("rows_read"), 1)
            act.wait_ge(S("exponents"), 1)
            for kind in (2, 3):
                own_a(do(gsc[:, :, kind, :], gsc[:, :, kind, :], ACT.Exp))
            act.sem_inc(S("factors"), 1)
            raw_tile(U_K, T_K, 8, 0, 0)
            act.wait_ge(S("page_units_done"), C_K)
            for c, b in enumerate((gT, gK, gG, gO)):
                do(rl[:, c * 512:(c + 1) * 512], b[:, :], ACT.Relu).then_inc(S("rectified"), 1)
            do(rl[:, PAST:PAST + 1], aS[:, 0:1], ACT.Relu).then_inc(S("rectified"), 1)
            for c, b in enumerate((gT, gK, gG, gO)):
                act.wait_ge(S("weighed"), c + 1)
                do(scS[:, c * 512:(c + 1) * 512], b[0:DEC, :], ACT.Copy).then_inc(S("scored"), 1)
            act.wait_ge(S("weighed"), 5)
            do(scS[:, PAST:PAST + 1], aS[0:DEC, 0:1], ACT.Copy).then_inc(S("scored"), 1)
            for e, j, c in BESIDE:
                if e == "score":
                    w = (j % 2 + 1) * P
                    act.wait_ge(S("pidx_done"), j + 1)
                    act.wait_ge(S("pterm_free"), j + 1)
                    own_a(do(rl[:, (j % 2) * 256:(j % 2) * 256 + w], [aS, aV][j % 2][:, 0:w], ACT.Relu))
                    act.sem_inc(S("pidx_free"), 1)
                    act.sem_inc(S("pterm"), 1)
                elif e == "tile" and j < NKV:
                    raw_tile(U_K, T_K, 8, j, 0)
                elif e == "tile":
                    evacuate(U_K, T_K, j, 0, 0, [(vT[:, j - NKV, :], slice(0, T), ACT.Copy)])
                    act.sem_inc(S("v_raw"), 1)
            act.wait_ge(S("v_turned"), 1)
            own_a(do(vtok[:, 0, :], gG[:, :], ACT.Copy))
            own_a(do(vtok[:, 1, :], gO[:, :], ACT.Copy))
            act.sem_inc(S("kv_ready"), 1)
            with act.Fori(0, 4) as i:
                own_a.enter(i, 4)
                for u in range(4):
                    raw_tile(U_Q, T_Q, 12, u, i)
            own_a.leave(4)
            flat = gates[:, :, :, :].rearrange("p g k t -> p (g k) t")
            with act.Fori(0, DEC) as i:
                own_a.enter(i, 8)
                for u in range(4):
                    evacuate(U_GATE, T_GATE, u, i, 4, [(flat[:, i * 4 + u, :], slice(0, T), ACT.Sigmoid)])
                    act.wait_ge(S("page_units_done"), i * 4 + (C_K + u + 1))
                    own_a(do(sal[:, i * 4 + u, :, :], [aS, aV][u % 2][:, 0:64].rearrange("p (g n) -> p g n", g=4),
                             ACT.Copy, scale=SCALE))
                    act.sem_inc(S("kscore_free"), 1)
            own_a.leave(DEC)
            act.sem_inc(S("past_scored"), 1)

            act.preload_act_table_set("natural_log_exp_and_others")

            def head_copy(g):
                own_a(do(qh, qT[:, g, 0:SEQ], ACT.Copy), lag=1)
                own_a(do(vh, vtok.rearrange("p s (k d) -> p s k d", k=NKV)[:, :, g // GRP, :], ACT.Copy))
                act.sem_inc(S("head_copied"), 1)

            def sigmoid(dst, src):
                own_a(do(dst, src, ACT.Exp, scale=-1.0))
                own_a(do(dst, dst, ACT.Ln, bias=1.0))
                own_a(do(dst, dst, ACT.Exp, scale=-1.0))

            def prepare(g, e, n0, t0, it):
                if e[0] == "e":
                    u = int(e[1])
                    unit_done(act, n0 + u, it, 4)
                    a = acc[(t0 + u) % 2]
                    if u < 3:
                        own_a(do(raw[:, u, CONVW - 1:], a[:, 0:SEQ], ACT.Copy), lag=1)
                        own_a(do(cs[:, g, u, CONVW - 1, :], a[:, SEQ:T], ACT.Copy))
                        act.sem_inc(S("head_raw"), 1)
                    else:
                        own_a(do(zraw[:, :], a[:, 0:T], ACT.Copy))
                    act.sem_inc(S("acc_free"), 1)
                elif e == "sig3":
                    sigmoid(e4[:, 3, :], zraw[:, :])
                    act.sem_inc(S("z_ready"), 1)
                elif e[0:3] == "sig":
                    j = int(e[3])
                    act.wait_ge(S("asked_next"), count(ASKS_NEXT, f"conv{j}", g))
                    sigmoid(e4[:, j, :], y3[:, j, :])
                    act.sem_inc(S("act_done_next"), 1)
                elif e == "ss":
                    act.wait_ge(S("summed"), g + 1)
                    own_a(do(rs[:, 0:512], gT[:, :], ACT.Ln, bias=epsc[:, 1:2]), lag=1)
                    own_a(do(rs[:, 512:528], aS[:, 0:16], ACT.Ln, bias=epsc[:, 1:2]))
                    own_a(do(rs[:, :], rs[:, :], ACT.Exp, scale=-0.5))
                    act.sem_inc(S("act_done_next"), 1)

            def step(h, e):
                def done():
                    act.sem_inc(S("act_done"), 1)

                if e == "mix":
                    multiplied(act, h, "mix")
                    own_a(do(eg, gG[:, 0:256], ACT.Exp))
                    done()
                    for p in range(2):
                        c = slice(p * P, (p + 1) * P)
                        own_a(do(kbe[:, p, :], gT[:, c], ACT.Copy, scale=hc[:, 2, p:p + 1]), lag=1)
                        own_a(do(kd[:, p, :], gT[:, c], ACT.Copy, scale=hc[:, 3, p:p + 1]), lag=1)
                        own_a(do(vb[:, p, :], gT[:, 256 + p * P:256 + (p + 1) * P], ACT.Copy, scale=hc[:, 1, p:p + 1]), lag=1 - p)
                    done()
                    act.wait_ge(S("asked"), count(ASKS, "decay", h))
                    own_a(do(dab[:, 0:256], dab[:, 0:256], ACT.Exp, scale=-1.0), lag=1)
                    own_a(do(dab[:, 256:512], dab[:, 256:512], ACT.Exp))
                    done()
                elif e == "soft":
                    act.wait_ge(S("asked"), count(ASKS, "soft", h))
                    own_a(do(sm[:, 0:P], sm[:, 0:P], ACT.Exp, bias=at_s[:, 2:3], accum_out=at_s[:, 4:5]), lag=1)
                    own_a(do(sm[:, P:3 * P], sm[:, P:3 * P], ACT.Exp, bias=at_s[:, 3:4], accum_out=at_s[:, 5:6]))
                    done()
                elif e == "pt":
                    multiplied(act, h, "pt")
                    own_a(do(pT, aS[:, 0:3 * P], ACT.Copy))
                    done()
                elif e == "xt":
                    multiplied(act, h, "xt")
                    own_a(do(xx[:, 1], gT[:, 0:256].rearrange("p (a b) -> p a b", a=2), ACT.Copy), lag=1)
                    own_a(do(knT[:, :], gG[0:DEC, 384:512], ACT.Copy))
                    done()
                elif e in SOLVE_W:
                    multiplied(act, h, e)
                    own_a(do(wt, gK[:, 0:256].rearrange("p (a b) -> p a b", a=2), ACT.Copy))
                    done()
                elif e == "uw":
                    multiplied(act, h, "uw")
                    own_a(do(nwt, gK[:, 0:256], ACT.Copy, scale=-1.0))
                    done()
                elif e in CHUNKS_A:
                    c = int(e[1])
                    r0 = CHUNK * (c % 2)
                    multiplied(act, h, e)
                    own_a(do(vn[r0:r0 + CHUNK, :], gT[r0:r0 + CHUNK, c * P:(c + 1) * P], ACT.Copy))
                    done()
                elif e == "c3b":
                    multiplied(act, h, e)
                    own_a(do(ob[:, 0:SEQ], gO[:, 0:SEQ], ACT.Copy), lag=1)
                    own_a(do(osq[:, 0:SEQ], gO[:, 0:SEQ], ACT.Square), lag=1)
                    own_a(do(osq[:, SEQ:T], ob[:, SEQ:T], ACT.Square))
                    done()
                elif e == "ms":
                    multiplied(act, h, "ms")
                    own_a(do(rms[:, :], gK[:, 0:T], ACT.Ln, bias=epsc[:, 1:2], scale=1.0 / P))
                    own_a(do(rms[:, :], rms[:, :], ACT.Exp, scale=-0.5))
                    done()

            for e in FIRST:
                if e == "exps":
                    act.wait_ge(S("shifted"), 1)
                    own_a(do(sal[:, :, :, :], sal[:, :, :, :], ACT.Exp))
                    own_a(do(pn[:, :, :], pn[:, :, :], ACT.Exp))
                    act.sem_inc(S("soft_exp"), 1)
                else:
                    prepare(0, e, U_HEAD, T_HEAD, 0)
            head_copy(0)

            def turn(h, events):
                for e in events:
                    if e in NEXT:
                        prepare(h + 1, e, U_HEAD + 4, T_HEAD + 4, h)
                        if e == "e3":
                            head_copy(h + 1)
                    else:
                        step(h, e)

            with act.Fori(0, NH - 1) as h:
                own_a.enter(h, ACT_PER_HEAD)
                turn(h, TURN)
            own_a.leave(NH - 1)
            turn(NH - 1, LAST_TURN)
            norm(1)
            silu_gates(U_UP2, KF)
            norm(2)

        @block.vector
        def _(v):
            own_v = Own(v, S("dve_own"))
            ts, stt, tt, cp = v.tensor_scalar, v.scalar_tensor_tensor, v.tensor_tensor, v.tensor_copy

            def bc(ap, shape):
                return ap.to_broadcast(shape)

            v.sem_inc(S("pair_free"), 2)
            v.sem_inc(S("acc_free"), 2)
            v.sem_inc(S("rope_free"), 2)
            v.sem_inc(S("pidx_free"), 2)
            v.sem_inc(S("pterm_free"), 2)
            v.sem_inc(S("kscore_free"), 2)

            def products(n_up, base):
                with v.Fori(0, KF // 2) as i:
                    for f in range(2):
                        unit_done(v, n_up + 2 * f + 1, i, 4)
                        v.wait_ge(S("silu_done"), i * 2 + (base + f + 1))
                        stt(out=hT[:, i * 2 + f, :], in0=upb[f][1][:, 0:T], scalar=0.5, in1=sg[:, f, :],
                            op0=ALU.mult, op1=ALU.mult).then_inc(S("pair_free"), 1)

            def residual(n0, units, t0):
                own_v(v.memset(m1, 0.0), lag=1)
                own_v(v.memset(m2, 0.0))
                with v.Fori(0, KD // 2) as i:
                    own_v.enter(i, 12)
                    for c in range(2):
                        unit_done(v, n0 + units * (c + 1) - 1, i, 2 * units)
                        y = xT[:, i * 2 + c, :]
                        own_v(stt(out=y, in0=y, scalar=ALPHA, in1=acc[(t0 + c) % 2][:, 0:T], op0=ALU.mult, op1=ALU.add))
                        v.sem_inc(S("acc_free"), 1)
                        own_v(tt(dev, y, m1, ALU.subtract))
                        own_v(stt(out=m1, in0=dev, scalar=epsc[:, bass.ds(i * 2 + (c + 2), 1)], in1=m1, op0=ALU.mult, op1=ALU.add))
                        own_v(tt(dev2, y, m1, ALU.subtract))
                        own_v(tt(dev2, dev2, dev, ALU.mult))
                        own_v(tt(m2, m2, dev2, ALU.add))
                own_v.leave(KD // 2)
                v.sem_inc(S("moments"), 1)

            def norm(n):
                v.wait_ge(S("stat"), 2 * n + 1)
                own_v(stt(out=dev, in0=gG[:, 0:T], scalar=1.0 / P, in1=m1, op0=ALU.mult, op1=ALU.subtract))
                own_v(stt(out=dev2, in0=dev, scalar=float(KD), in1=dev, op0=ALU.mult, op1=ALU.mult))
                v.sem_inc(S("moments"), 1)
                own_v(ts(mean[:, :], gG[:, 0:T], 1.0 / P, None, ALU.mult))
                v.sem_inc(S("moments"), 1)
                own_v(centre(v, 0))
                v.wait_ge(S("deviation"), n + 1)
                own_v(v.reciprocal(rstd[:, :], rstd[:, :]))
                for k in range(KD):
                    if k == 4:
                        own_v(centre(v, k))
                    elif k in (8, 12):
                        v.wait_ge(S("centred"), 2 * n + (k - 4) // 4)
                    tt(xT[:, k, :], xT[:, k, :], rstd[:, :], ALU.mult).then_inc(S("scaled"), 1)

            products(U_UP1, 0)
            v.wait_ge(S("small_in"), 16 * 28)
            residual(U_DN1, 4, T_DN1)
            norm(0)
            own_v(v.memset(raw[:, :, 0:CONVW - 1], 0.0))
            v.wait_ge(S("ki_rot"), 1)
            v.wait_ge(S("misc_raw"), 1)
            own_v(tt(kiT[:, :], gT[:, 0:T], rope[:, 2, :], ALU.mult))
            own_v(tt(tmp[:, :], gK[:, 0:T], rope[:, 3, :], ALU.mult))
            own_v(tt(kiT[:, :], kiT[:, :], tmp[:, :], ALU.add))
            v.sem_inc(S("kv_ready"), 1)
            v.wait_ge(S("misc_exp"), 2)
            own_v(ts(raw2[:, 0, :], raw2[:, 0, :], 1.0, None, ALU.add))
            own_v(v.reciprocal(raw2[:, 0, :], raw2[:, 0, :]))
            own_v(ts(raw2[:, 0, :], raw2[:, 0, :], rowm[:, 2:3], None, ALU.mult))
            own_v(ts(alog[:, :], alog[:, :], -1.0, rowm[:, 1:2], ALU.mult, ALU.mult))
            own_v(ts(tmp[:, :], msc[:, :], dtb[:, 0:1], 0.0, ALU.add, ALU.max))
            own_v(tt(val[:, :], val[:, :], tmp[:, :], ALU.add))
            own_v(stt(out=val[:, :], in0=val[:, :], scalar=alog[:, 0:1], in1=raw2[:, 0, :], op0=ALU.mult, op1=ALU.add))
            own_v(stt(out=val[:, :], in0=msc[:, :], scalar=rowm[:, 0:1], in1=val[:, :], op0=ALU.mult, op1=ALU.add))
            v.sem_inc(S("val_ready"), 1)
            own_v(tt(rms[:, 0:256].rearrange("p (k b) -> p k b", b=DEC),
                     M["ident"][:, R_A:R_A + 2 * NH].unsqueeze(2).to_broadcast([P, 2 * NH, DEC]),
                     val[:, SEQ:T].unsqueeze(1).to_broadcast([P, 2 * NH, DEC]), ALU.mult))
            v.sem_inc(S("picked"), 1)
            v.sem_inc(S("ki_ready"), 1)

            def roped(r0, u, it, dst, table):
                v.wait_ge(S("rotated"), it * 4 + (r0 + u + 1))
                r = r0 + u
                own_v(tt(dst, raw2[:, r % 2, :], rope[:, table, :], ALU.mult))
                own_v(tt(tmp[:, :], [gT, gK][r % 2][:, 0:T], rope[:, table + 1, :], ALU.mult))
                own_v(tt(dst, dst, tmp[:, :], ALU.add))
                v.sem_inc(S("rope_free"), 1)

            with v.Fori(0, 2) as i:
                own_v.enter(i, 12)
                for u in range(4):
                    roped(0, u, i, qiT[:, i * 4 + u, :], 2)
            own_v.leave(2)
            own_v(v.memset(zq[:, :, :], 0.0))
            for h2 in range(2):
                rows = slice(h2 * IDXD, (h2 + 1) * IDXD)
                for b in range(DEC):
                    own_v(cp(zq[rows, b, b * IDXH + h2:(b + 1) * IDXH:2], qiT[rows, :, SEQ + b]))
            v.sem_inc(S("zq_ready"), 1)
            v.wait_ge(S("decays"), 1)
            v.wait_ge(S("rows_done"), 1)
            v.wait_ge(S("valk_ready"), 1)
            v.wait_ge(S("rows_read"), 1)
            own_v(tt(w8[:, :], gO[:, 256:256 + DEC], own[:, :], ALU.mult))
            for t in range(2):
                own_v(cp(gsc[:, :, 0, t], gK[:, 32 * t:32 * t + 16]))
                own_v(cp(gsc[:, :, 1, t], valk[:, t, R_B:R_B + NH]))
                own_v(cp(gsc[:, :, 2, t], gK[:, 32 * t:32 * t + 16]))
                own_v(tt(gsc[:, :, 3, t], gK[:, 32 * t + 16:32 * t + 32], gsc[:, :, 0, t], ALU.subtract))
            v.sem_inc(S("exponents"), 1)
            v.wait_ge(S("factors"), 1)
            own_v(tt(gsc[:, :, 2, :], gsc[:, :, 2, :], gsc[:, :, 1, :], ALU.mult))
            v.sem_inc(S("decays_read"), 1)
            own_v(v.memset(pscore[:, :], 0.0))
            for e, j, _c in BESIDE:
                if e == "score":
                    h, t = j // 2, j % 2
                    w, c = (t + 1) * P, slice(t * P, 3 * P if t else P)
                    v.wait_ge(S("pterm"), j + 1)
                    own_v(stt(out=pscore[:, c], in0=rl[:, t * 256:t * 256 + w],
                              scalar=valk[:, t, R_W + h:R_W + h + 1], in1=pscore[:, c], op0=ALU.mult, op1=ALU.add))
                    v.sem_inc(S("pterm_free"), 1)
                elif e == "tile" and j <= NKV:
                    roped(8, j - 1, 0, kT[:, j - 1, :], 0)
            v.sem_inc(S("kv_ready"), 1)
            with v.Fori(0, 4) as i:
                own_v.enter(i, 12)
                for u in range(4):
                    roped(12, u, i, qT[:, i * 4 + u, :], 0)
            own_v.leave(4)
            own_v(tt(pscore[:, :], pscore[:, :], caus[:, :], ALU.mult))
            own_v(ts(pbias[:, :], caus[:, :], -1.0, -NEG, ALU.add, ALU.mult))
            own_v(tt(pscore[:, :], pscore[:, :], pbias[:, :], ALU.add))
            for t in range(2):
                c = slice(t * P, 3 * P if t else P)
                for _r in range(TOPK_P // 8):
                    own_v(v.max(out=top8[:, :], in_=pscore[:, c]))
                    own_v(v.match_replace(out=pscore[:, c], in_to_replace=top8[:, :], in_values=pscore[:, c], imm_value=GONE))
            own_v(stt(out=pbias[:, :], in0=pscore[:, :], scalar=GONE, in1=caus[:, :], op0=ALU.is_equal, op1=ALU.mult))
            own_v(ts(pbias[:, :], pbias[:, :], -1.0, OFF, ALU.add, ALU.mult))
            v.wait_ge(S("scored"), 5)
            for _r in range(TOPK_S // 8):
                own_v(v.max(out=top8[0:DEC, :], in_=scS[:, :]))
                own_v(v.match_replace(out=scS[:, :], in_to_replace=top8[0:DEC, :], in_values=scS[:, :], imm_value=GONE))
            own_v(ts(scS[:, :], scS[:, :], GONE, None, ALU.is_equal))
            own_v(ts(s8[0:DEC, 0, :], M["ident"][0:DEC, 0:DEC], scS[:, PAST:PAST + 1], None, ALU.mult))
            for kv in range(NKV):
                own_v(tt(sn[:, :, kv * GRP:(kv + 1) * GRP].rearrange("p b g -> p g b"),
                         qT[:, kv * GRP:(kv + 1) * GRP, SEQ:T],
                         kT[:, kv, SEQ:T].unsqueeze(1).to_broadcast([P, GRP, DEC]), ALU.mult))
            v.sem_inc(S("selected"), 1)
            v.wait_ge(S("masks_turned"), 1)
            own_v(ts(mbt[:, :, :].rearrange("p b g -> p g b"), gT[:, 0:P].rearrange("p (g b) -> p g b", b=DEC),
                     -1.0, OFF, ALU.add, ALU.mult))
            own_v(ts(nbt[:, :], gK[:, 0:DEC], -1.0, OFF, ALU.add, ALU.mult))
            own_v(ts(sn[:, :, :], gG[:, 0:P].rearrange("p (b n) -> p b n", n=NH), SCALE, None, ALU.mult))
            own_v(tt(sn[:, :, :], sn[:, :, :], nbt[:, :].unsqueeze(2).to_broadcast([P, DEC, NH]), ALU.add))
            v.wait_ge(S("past_scored"), 1)
            salf = sal[:, :, :, :].rearrange("p u g n -> p (u g) n")
            own_v(tt(salf, salf, mbt[:, :, :].rearrange("p b g -> p (b g)").unsqueeze(2).to_broadcast([P, P, NH]), ALU.add))
            bgn = sal[:, :, :, :].rearrange("p (b q) g n -> p b n (q g)", b=DEC)
            own_v(v.tensor_reduce(gmx[:, :, :], bgn, AX.X, ALU.max))
            v.sem_inc(S("part_max"), 1)
            def two(ap):
                return ap.unsqueeze(1).to_broadcast([P, 2, P])

            def take(dst, src):
                return ts(dst, src, 1.0, None, ALU.mult)

            def factors(g):
                own_v(take(hc[:, :, :], gsc[:, g, :, :]), lag=1)
                own_v(take(hg[:, :, :], sgs[:, :, g, :]), lag=1)
                own_v(cp(dg[:, 0, :], M["ident"]), lag=1)
                own_v(cp(dg[:, 1, :], M["ident"]))
                for p in range(2):
                    own_v(ts(dg[:, p, :], dg[:, p, :], hc[:, 0, p:p + 1], None, ALU.mult), lag=1 - p)

            def prepare(g, e):
                if e[0:4] == "conv":
                    j = int(e[4])
                    if e[5] == "a":
                        v.wait_ge(S("head_raw"), g * 3 + (j + 1))
                        own_v(take(hw[:, :], cw[:, g, :]), lag=1)
                        own_v(take(cpb[:, g, j, :], raw[:, j, SEQ:]))
                    for k in (0, 1) if e[5] == "a" else (2, 3):
                        w = hw[:, 4 * j + k:4 * j + k + 1]
                        if k == 0:
                            own_v(ts(y3[:, j, 0:SEQ], raw[:, j, 0:SEQ], w, None, ALU.mult), lag=1)
                            own_v(ts(y3[:, j, SEQ:T], cs[:, g, j, 0, :], w, None, ALU.mult), lag=1)
                        else:
                            own_v(stt(out=y3[:, j, 0:SEQ], in0=raw[:, j, k:k + SEQ], scalar=w, in1=y3[:, j, 0:SEQ],
                                      op0=ALU.mult, op1=ALU.add), lag=1)
                            own_v(stt(out=y3[:, j, SEQ:T], in0=cs[:, g, j, k, :], scalar=w, in1=y3[:, j, SEQ:T],
                                      op0=ALU.mult, op1=ALU.add), lag=0 if k % 2 else 1)
                    if e[5] == "b":
                        v.sem_inc(S("asked_next"), 1)
                elif e[0:4] == "silu":
                    j = int(e[4])
                    act_done_next(v, g, f"sig{j}")
                    own_v(tt(y3[:, j, :], y3[:, j, :], e4[:, j, :], ALU.mult))
                    own_v(tt(sq[:, j * SEQ:(j + 1) * SEQ], y3[:, j, 0:SEQ], y3[:, j, 0:SEQ], ALU.mult), lag=1)
                    own_v(tt(sq[:, 512 + 8 * j:520 + 8 * j], y3[:, j, SEQ:T], y3[:, j, SEQ:T], ALU.mult))
                    if j == 1:
                        own_v(tt(sq[:, 528:536], y3[:, 0, SEQ:T], y3[:, 1, SEQ:T], ALU.mult))
                        v.sem_inc(S("squared"), 1)
                elif e == "norm":
                    act_done_next(v, g, "sig2")
                    own_v(tt(y3[:, 2, :], y3[:, 2, :], e4[:, 2, :], ALU.mult), lag=1)
                    factors(g)
                    act_done_next(v, g, "ss")
                    own_v(stt(out=qkn[:, 0:SEQ], in0=y3[:, 0, 0:SEQ], scalar=SCALE, in1=rs[:, 0:SEQ], op0=ALU.mult, op1=ALU.mult), lag=1)
                    own_v(tt(qkn[:, SEQ:512], y3[:, 1, 0:SEQ], rs[:, SEQ:512], ALU.mult), lag=1)
                    own_v(tt(kq[:, 0, :], y3[:, 1, SEQ:T], rs[:, 520:528], ALU.mult), lag=1)
                    own_v(stt(out=kq[:, 1, :], in0=y3[:, 0, SEQ:T], scalar=SCALE, in1=rs[:, 512:520], op0=ALU.mult, op1=ALU.mult), lag=1)
                    own_v(stt(out=s8[:, 2, :], in0=aS[:, 16:24], scalar=SCALE, in1=rs[:, 512:520], op0=ALU.mult, op1=ALU.mult))
                    own_v(tt(s8[:, 2, :], s8[:, 2, :], rs[:, 520:528], ALU.mult))
                    v.sem_inc(S("normalized"), 1)

            def values_out(h):
                v.wait_ge(S("page_units_done"), h * 2 + (C_V + 2))
                own_v(take(oS[:, h, :], aV[:, 0:NH]))

            def merge(h):
                own_v(tt(gA[:, h, SEQ:T], gA[:, h, SEQ:T], gB[:, h, SEQ:T], ALU.add))
                v.sem_inc(S("merged"), 1)

            def step(h, e, last=False):
                def answer():
                    v.sem_inc(S("answered"), 1)

                if e == "mix":
                    multiplied(v, h, "mix")
                    act_done(v, h, "eg")
                    for p in range(2):
                        c = slice(p * P, (p + 1) * P)
                        own_v(ts(dab[:, c], gG[:, c], hc[:, 0, p:p + 1], 0.0, ALU.subtract, ALU.max), lag=1)
                        own_v(ts(dab[:, 256 + p * P:256 + (p + 1) * P], gG[:, c], hc[:, 0, p:p + 1], 0.0,
                                 ALU.subtract, ALU.min), lag=1 - p)
                    v.sem_inc(S("asked"), 1)
                    st = gG[:, 256:272].rearrange("p (b c) -> p c b", c=2)
                    own_v(tt(s8[:, 3, :], st[:, 0, :], hg[:, 0, :], ALU.mult), lag=1)
                    own_v(tt(s8[:, 4, :], st[:, 1, :], hg[:, 0, :], ALU.mult), lag=1)
                    own_v(tt(s8[:, 3, :], y3[:, 2, SEQ:T], s8[:, 3, :], ALU.subtract))
                    own_v(tt(s8[:, 1, :], s8[:, 3, :], hg[:, 1, :], ALU.mult))
                    act_done(v, h, "decay")
                    for p in range(2):
                        own_v(stt(out=lf[:, p, :], in0=gK[:, p * P:(p + 1) * P], scalar=hc[:, 1, p:p + 1],
                                  in1=dab[:, p * P:(p + 1) * P], op0=ALU.mult, op1=ALU.mult), lag=1 - p)
                    own_v(tt(wt, lf, two(M["lv1"]), ALU.mult))
                    own_v(tt(xx[:, 0], two(M["ident"]), wt, ALU.subtract))
                    answer()
                    v.wait_ge(S("z_ready"), h + 1)
                    own_v(tt(zs, zraw[:, :], e4[:, 3, :], ALU.mult))
                elif e == "lift":
                    multiplied(v, h, "qk")
                    own_v(stt(out=sm, in0=aS[:, 0:3 * P], scalar=SCALE, in1=pbias[:, :], op0=ALU.mult, op1=ALU.add))
                    own_v(v.tensor_reduce(at_s[:, 0:1], sm[:, 0:P], AX.X, ALU.max), lag=1)
                    own_v(v.tensor_reduce(at_s[:, 1:2], sm[:, P:3 * P], AX.X, ALU.max))
                    own_v(ts(at_s[:, 2:4], at_s[:, 0:2], -1.0, None, ALU.mult))
                    v.sem_inc(S("asked"), 1)
                elif e == "mix2":
                    own_v(tt(qkt, gK[:, 256:512].rearrange("p (a b) -> p a b", a=2),
                             dab[:, 256:512].rearrange("p (a b) -> p a b", a=2), ALU.mult), lag=1)
                    own_v(tt(lm[0], lf, two(M["lv2"]), ALU.mult))
                    answer()
                    own_v(tt(lm[1], lf, two(M["lv4"]), ALU.mult), lag=1)
                    own_v(tt(qe, qkn[:, 0:SEQ], eg, ALU.mult))
                    own_v(tt(qkt, qkt, two(M["incl"]), ALU.mult), lag=1)
                    own_v(tt(s8[:, 5, :], s8[:, 2, :], s8[:, 1, :], ALU.mult))
                    own_v(tt(ob[:, SEQ:T], s8[:, 4, :], s8[:, 5, :], ALU.add), lag=1)
                elif e == "share":
                    act_done(v, h, "soft")
                    own_v(v.reciprocal(at_s[:, 4:6], at_s[:, 4:6]))
                    own_v(ts(sm[:, 0:P], sm[:, 0:P], at_s[:, 4:5], None, ALU.mult), lag=1)
                    own_v(ts(sm[:, P:3 * P], sm[:, P:3 * P], at_s[:, 5:6], None, ALU.mult))
                    answer()
                elif e == "pv":
                    multiplied(v, h, e)
                    own_v(tt(gA[:, h, 0:SEQ], gA[:, h, 0:SEQ], aS[:, 0:SEQ], ALU.mult))
                    answer()
                elif e == "vout":
                    if not last:
                        values_out(h)
                    answer()
                elif e == "vm":
                    act_done(v, h, "xt")
                    own_v(tt(vm, M["ident"][0:DEC, 0:DEC].unsqueeze(2).to_broadcast([DEC, DEC, P]),
                             gT[0:DEC, 256:384].unsqueeze(1).to_broadcast([DEC, DEC, P]), ALU.mult))
                    v.sem_inc(S("vm_ready"), 1)
                elif e == "added":
                    multiplied(v, h, "outer")
                    v.wait_ge(S("state_scaled"), h + 1)
                    for q, b in enumerate((gT, gO)):
                        own_v(tt(sst[:, 4 * q:4 * q + 4, :], sst[:, 4 * q:4 * q + 4, :],
                                 b[:, :].rearrange("p (a b) -> p a b", a=4), ALU.add), lag=1 - q)
                    answer()
                elif e in SOLVE_X:
                    n = int(e[1])
                    multiplied(v, h, e)
                    flat = xx.rearrange("p x a b -> p (x a b)")
                    c = slice(0 if e != SOLVE_X[-1] else 2 * P, 4 * P)
                    own_v(tt(flat[:, c], flat[:, c], gG[:, c], ALU.subtract))
                    answer()
                    if n + 2 < len(LEVELS):
                        own_v(tt(lm[n % 2], lf, two(M[f"lv{LEVELS[n + 2]}"]), ALU.mult))
                elif e == "uw":
                    v.wait_ge(S("prompt_state_free"), h + 1)
                    own_v(v.memset(St, 0.0))
                    answer()
                elif e in CHUNKS_B:
                    c = int(e[1])
                    multiplied(v, h, e)
                    own_v(stt(out=St, in0=St, scalar=eg[:, (c + 1) * CHUNK - 1:(c + 1) * CHUNK],
                              in1=gG[:, 0:P], op0=ALU.mult, op1=ALU.add))
                    answer()
                elif e == "gated":
                    act_done(v, h, "ms")
                    own_v(stt(out=ob, in0=ob, scalar=gnorm[:, 0:1], in1=rms[:, :], op0=ALU.mult, op1=ALU.mult))
                    own_v(tt(ob, ob, zs, ALU.mult))
                    own_v(tt(gB[:, h, :], gB[:, h, :], ob, ALU.mult))
                    own_v(tt(gA[:, h, 0:SEQ], gA[:, h, 0:SEQ], gB[:, h, 0:SEQ], ALU.add))
                    answer()
                    v.sem_inc(S("head_over"), 1)

            def sample_softmax(part):
                if part == "shift":
                    v.wait_ge(S("all_max"), 1)
                    own_v(tt(gmx[:, :, :], gmx[:, :, :], sn[:, :, :], ALU.max))
                    for b in range(DEC):
                        own_v(tt(salf[:, b * PAGES:(b + 1) * PAGES, :], salf[:, b * PAGES:(b + 1) * PAGES, :],
                                 gmx[:, b, :].unsqueeze(1).to_broadcast([P, PAGES, NH]), ALU.subtract))
                    own_v(tt(pn[:, :, :], sn[:, :, :], gmx[:, :, :], ALU.subtract))
                    v.sem_inc(S("shifted"), 1)
                elif part == "sum":
                    v.wait_ge(S("soft_exp"), 1)
                    own_v(v.tensor_reduce(rin[:, :, :], bgn, AX.X, ALU.add))
                    v.sem_inc(S("expsum"), 1)
                else:
                    v.wait_ge(S("denoms"), 1)
                    own_v(tt(rin[:, :, :], gO[:, 0:P].rearrange("p (b n) -> p b n", n=NH), pn[:, :, :], ALU.add))
                    own_v(v.reciprocal(rin[:, :, :], rin[:, :, :]))
                    v.sem_inc(S("sample_soft"), 1)

            def sample_attention():
                pair = oS[:, :, :].rearrange("p (b u) n -> p b u n", u=2)
                own_v(tt(sn[:, :, :], pair[:, :, 0, :], pair[:, :, 1, :], ALU.add))
                for kv in range(NKV):
                    g = slice(kv * GRP, (kv + 1) * GRP)
                    own_v(tt(gmx[:, :, g], pn[:, :, g], vT[:, kv, SEQ:T].unsqueeze(2).to_broadcast([P, DEC, GRP]), ALU.mult))
                own_v(tt(sn[:, :, :], sn[:, :, :], gmx[:, :, :], ALU.add))
                own_v(tt(sn[:, :, :], sn[:, :, :], rin[:, :, :], ALU.mult))
                own_v(tt(gA[:, :, SEQ:T], gA[:, :, SEQ:T], sn[:, :, :].rearrange("p b n -> p n b"), ALU.mult))

            for e in FIRST:
                if e in ("shift", "sum", "divide"):
                    sample_softmax(e)
                else:
                    prepare(0, e)

            def turn(h, events, last=False):
                for e in events:
                    if e in NEXT:
                        prepare(h + 1, e)
                    elif e == "attend":
                        values_out(h)
                        sample_attention()
                        merge(slice(0, NH - 1))
                    else:
                        step(h, e, last)

            with v.Fori(0, NH - 1) as h:
                own_v.enter(h, DVE_PER_HEAD)
                turn(h, TURN)
            own_v.leave(NH - 1)
            turn(NH - 1, LAST_TURN, last=True)
            merge(slice(NH - 1, NH))
            residual(U_WO, 1, T_WO)
            norm(1)
            products(U_UP2, KF)
            residual(U_DN2, 4, T_DN2)
            norm(2)


DVE_PER_HEAD, ACT_PER_HEAD = 99, 53
_OUTS = [("yT", (P, KD * T)), ("kT", (P, NKV * T)), ("vT", (P, NKV * T)), ("kiT", (IDXD, T)),
         ("ssm_p", (NH, P, P)), ("ssm_s", (NH, P, DEC, P)), ("convp", (P, NH * 9)), ("convs", (P, NH * 96))]


def lay_out(a):
    f = lambda n: np.asarray(a[n])
    x = np.concatenate([f("x_prompt")[0], f("x_sample")[:, 0]], 0)

    def units(w, nk):
        k, n = w.shape
        return w.reshape(k // P // nk, nk, P, n // P, P).transpose(3, 0, 2, 1, 4)

    def up(g, u):
        return np.stack([units(g, KD)[:, 0], units(u, KD)[:, 0]], 1).reshape(2 * KF, P, KD * P)

    def down(w):
        return np.ascontiguousarray(units(w, QD)).reshape(4 * KD, P, QD * P)

    w = f("w_in")[0]
    names = [("q", 2048), ("k", 512), ("v", 512), ("qi", 1024), ("ki", 64), ("wi", 16), ("qkv", 6144),
             ("a", 16), ("b", 16), ("z", 2048), ("ga", 2048), ("gb", 2048)]
    s, at = {}, 0
    for n, c in names:
        s[n] = w[:, at:at + c]
        at += c
    heads = []
    for h in range(NH):
        c = slice(h * P, (h + 1) * P)
        heads += [s["qkv"][:, 0:2048][:, c], s["qkv"][:, 2048:4096][:, c], s["qkv"][:, 4096:][:, c], s["z"][:, c]]
    pad = np.zeros((D, P - 112), np.float32)
    w_in = np.concatenate([s["ki"], s["wi"], s["a"], s["b"], pad, s["qi"], s["k"], s["v"], s["q"], s["ga"], s["gb"]] + heads, 1)
    cols = lambda m: np.ascontiguousarray(m.reshape(KD, P).T)
    place = lambda m: np.concatenate([np.zeros(R_A, np.float32), m, np.zeros(P - R_A - NH, np.float32)]).reshape(P, 1)
    conv = f("conv_w")[0].reshape(CONVW, 3, NH, P).transpose(3, 2, 1, 0)
    sconv = f("state_conv")[0].reshape(DEC, CONVW - 1, 3, NH, P).transpose(4, 3, 2, 1, 0)
    ki = f("cache_idx_k")[0].transpose(0, 2, 1)
    d = {
        "xT": x.T.reshape(KD, P, T).transpose(1, 0, 2).reshape(P, KD * T),
        "up1": up(f("ffn1_w_gate")[0], f("ffn1_w_up")[0]), "dn1": down(f("ffn1_w_down")[0]),
        "up2": up(f("ffn2_w_gate")[0], f("ffn2_w_up")[0]), "dn2": down(f("ffn2_w_down")[0]),
        "w_in": units(w_in, KD)[:, 0].reshape(-1, P, KD * P), "w_o": units(f("w_o")[0], KD)[:, 0].reshape(KD, P, KD * P),
        "cki": np.concatenate([ki, ki], 1), "ck": f("cache_k")[0].transpose(0, 3, 2, 1).reshape(-1, P, NKV * DH),
        "cv": f("cache_v")[0].reshape(-1, P, NKV * DH),
        "ssm": f("state_ssm")[0].transpose(1, 2, 0, 3),
        "lnp": np.stack([cols(f(n)[0]) for n in ("ln1_g", "ln1_b", "ln2_g", "ln2_b", "ln3_g", "ln3_b")], 1).reshape(P, -1),
        "cw": conv.reshape(P, -1), "convs": sconv.reshape(P, NH, 3, -1),
        "gnorm": f("gdn_norm_g")[0].reshape(P, 1), "alog": place(f("a_log")[0]), "dtb": place(f("dt_bias")[0]),
        "pt": f("page_table").reshape(1, -1),
    }
    d.update(host_constants())
    return {k: np.ascontiguousarray(m) for k, m in d.items()}


def kernel(**inputs):
    import concourse.bacc as bacc
    from concourse.bass_utils import run_bass_kernel_spmd

    nc = bacc.Bacc("TRN2", target_bir_lowering=False, num_devices=1)
    arrays = lay_out(inputs)
    din = {k: nc.dram_tensor(f"in_{k}", a.shape, mybir.dt.from_np(a.dtype), kind="ExternalInput").ap() for k, a in arrays.items()}
    dout = {k: nc.dram_tensor(f"out_{k}", s, F32, kind="ExternalOutput").ap() for k, s in _OUTS}
    build(nc, din, dout)
    r = run_bass_kernel_spmd(nc, [{f"in_{k}": a for k, a in arrays.items()}], core_ids=[0]).results[0]
    o = {k: np.asarray(r[f"out_{k}"]) for k, _ in _OUTS}
    y = o["yT"].reshape(P, KD, T).transpose(2, 1, 0).reshape(T, D)
    kv = {k: o[k].reshape(P, NKV, T).transpose(2, 1, 0) for k in ("kT", "vT")}
    ki = o["kiT"].T
    ssm_s = o["ssm_s"].transpose(2, 0, 1, 3)
    convp = o["convp"].reshape(P, NH, 3, CONVW - 1).transpose(3, 2, 1, 0).reshape(CONVW - 1, -1)
    convs = o["convs"].reshape(P, NH, 3, CONVW, DEC)[:, :, :, 1:].transpose(4, 3, 2, 1, 0).reshape(DEC, CONVW - 1, -1)
    c = np.ascontiguousarray
    return (c(y[None, :SEQ]), c(y[SEQ:, None]),
            c(kv["kT"][None, None, :SEQ]), c(kv["vT"][None, None, :SEQ]), c(ki[None, None, :SEQ]),
            c(o["ssm_p"][None, None]), c(convp[None, None]),
            c(kv["kT"][None, SEQ:, None]), c(kv["vT"][None, SEQ:, None]), c(ki[None, SEQ:, None]),
            c(ssm_s[None]), c(convs[None]))
```
